# Optimizing a Trainium2 kernel written in Bass

```python
import jax
import jax.numpy as jnp
from jax import lax
import numpy as np
import math
import jax, jax.numpy as jnp

D_MODEL = 2048
BATCH = 1
SEQ = 256
DEPTH = 2

MLSTM_HEADS = 4
MLSTM_V_DIM = D_MODEL // (2 * MLSTM_HEADS)
MLSTM_QK_DIM = MLSTM_V_DIM // 2
MLSTM_CHUNK = 64
CONV_WIDTH = 4
HEAD_DIM = 64
ATTN_HEADS = D_MODEL // (2 * HEAD_DIM)
KV_HEADS = 4
WINDOW = 128
ATTN_BLOCK = WINDOW
D_FF = 4 * D_MODEL
NORM_EPS = 1e-6
N_MOD = 6

MLSTM_QK_W = MLSTM_HEADS * MLSTM_QK_DIM
MLSTM_V_W = MLSTM_HEADS * MLSTM_V_DIM
ATTN_Q_W = ATTN_HEADS * HEAD_DIM
ATTN_KV_W = KV_HEADS * HEAD_DIM
D_MIX = MLSTM_V_W + ATTN_Q_W
IN_SIZES = (MLSTM_QK_W, MLSTM_QK_W, MLSTM_V_W, MLSTM_V_W, MLSTM_HEADS, MLSTM_HEADS, ATTN_Q_W, ATTN_KV_W, ATTN_KV_W)
D_IN = sum(IN_SIZES)


def rms_norm(x, g):
    xf = x.astype(jnp.float32)
    y = xf * lax.rsqrt(jnp.mean(xf * xf, axis=-1, keepdims=True) + NORM_EPS)
    return (y * g.astype(jnp.float32)).astype(x.dtype)

def causal_depthwise_conv(x, w, b):
    y = lax.conv_general_dilated(
        x, w[:, None, :].astype(x.dtype), window_strides=(1,),
        padding=((CONV_WIDTH - 1, 0),), dimension_numbers=('NWC', 'WIO', 'NWC'),
        feature_group_count=x.shape[-1])
    return y + b.astype(x.dtype)

def mlstm_chunkwise(q, k, v, i_pre, f_pre):
    B, S, H, Dk = q.shape
    Dv = v.shape[-1]
    L = MLSTM_CHUNK
    NC = S // L
    q = q.reshape(B, NC, L, H, Dk) * (Dk ** -0.5)
    k = k.reshape(B, NC, L, H, Dk)
    v = v.reshape(B, NC, L, H, Dv)
    ig = i_pre.reshape(B, NC, L, H)
    b = jnp.cumsum(jax.nn.log_sigmoid(f_pre).reshape(B, NC, L, H), axis=2)
    b_end = b[:, :, -1]

    a = b_end[:, :, None] - b + ig
    m_loc = jnp.max(a, axis=2)
    kw = k * jnp.exp(a - m_loc[:, :, None])[..., None]
    C_loc = jnp.einsum('bclhk,bclhv->bchkv', kw, v)
    n_loc = jnp.sum(kw, axis=2)

    def step(carry, inp):
        C, n, m = carry
        be, ml, Cl, nl = inp
        m_new = jnp.maximum(be + m, ml)
        s_prev = jnp.exp(be + m - m_new)
        s_loc = jnp.exp(ml - m_new)
        C_new = s_prev[..., None, None] * C + s_loc[..., None, None] * Cl
        n_new = s_prev[..., None] * n + s_loc[..., None] * nl
        return (C_new, n_new, m_new), (C, n, m)

    init = (jnp.zeros((B, H, Dk, Dv), q.dtype), jnp.zeros((B, H, Dk), q.dtype), jnp.zeros((B, H), q.dtype))
    xs = tuple(jnp.moveaxis(t, 1, 0) for t in (b_end, m_loc, C_loc, n_loc))
    _, (C_prev, n_prev, m_prev) = lax.scan(step, init, xs)
    C_prev = jnp.moveaxis(C_prev, 0, 1)
    n_prev = jnp.moveaxis(n_prev, 0, 1)
    m_prev = jnp.moveaxis(m_prev, 0, 1)

    causal = jnp.tril(jnp.ones((L, L), dtype=bool))
    Dlog = b[:, :, :, None, :] - b[:, :, None, :, :] + ig[:, :, None, :, :]
    Dlog = jnp.where(causal[None, None, :, :, None], Dlog, -jnp.inf)
    inter = b + m_prev[:, :, None, :]
    m_t = jnp.maximum(inter, jnp.max(Dlog, axis=3))
    Pqk = jnp.exp(Dlog - m_t[:, :, :, None, :]) * jnp.einsum('bcthd,bcshd->bctsh', q, k)
    s_inter = jnp.exp(inter - m_t)
    num = (jnp.einsum('bctsh,bcshv->bcthv', Pqk, v)
           + s_inter[..., None] * jnp.einsum('bcthd,bchdv->bcthv', q, C_prev))
    den = jnp.sum(Pqk, axis=3) + s_inter * jnp.einsum('bcthd,bchd->bcth', q, n_prev)
    h = num / jnp.maximum(jnp.abs(den), jnp.exp(-m_t))[..., None]
    return h.reshape(B, S, H, Dv)

def sliding_window_sink_attention(q, k, v, sinks):
    B, S, Hq, Dh = q.shape
    Hkv = k.shape[2]
    G = Hq // Hkv
    T = ATTN_BLOCK
    NB = S // T
    f32 = jnp.float32
    qb = q.astype(f32).reshape(B, NB, T, Hkv, G, Dh) * (Dh ** -0.5)

    def banded(t):
        tb = t.astype(f32).reshape(B, NB, T, Hkv, Dh)
        prev = jnp.pad(tb, ((0, 0), (1, 0), (0, 0), (0, 0), (0, 0)))[:, :-1]
        return jnp.concatenate([prev, tb], axis=2)

    kb, vb = banded(k), banded(v)
    scores = jnp.einsum('bnqhgd,bnkhd->bnhgqk', qb, kb)
    r = jnp.arange(T)[:, None]
    u = jnp.arange(2 * T)[None, :]
    dist = r + T - u
    key_pos = jnp.arange(NB)[:, None] * T + jnp.arange(2 * T)[None, :] - T
    valid = ((dist >= 0) & (dist < WINDOW))[None] & (key_pos >= 0)[:, None, :]
    slopes = jnp.exp2(-8.0 * (jnp.arange(Hq, dtype=f32) + 1.0) / Hq).reshape(Hkv, G)
    alibi = -slopes[:, :, None, None] * dist.astype(f32)
    scores = jnp.where(valid[None, :, None, None], scores + alibi[None, None], -jnp.inf)
    sink = sinks.astype(f32).reshape(Hkv, G)[None, None, :, :, None, None]
    m = jnp.maximum(jnp.max(scores, axis=-1, keepdims=True), sink)
    p = jnp.exp(scores - m)
    probs = p / (jnp.sum(p, axis=-1, keepdims=True) + jnp.exp(sink - m))
    out = jnp.einsum('bnhgqk,bnkhd->bnqhgd', probs, vb)
    return out.reshape(B, S, Hq, Dh)

def token_mixer(h, w_in, conv_w, conv_b, b_i, b_f, g_mlstm_head, g_attn_out, attn_sinks, w_out):
    B, S, _ = h.shape
    f32 = jnp.float32
    proj = h @ w_in
    offs = [int(o) for o in np.cumsum(IN_SIZES)[:-1]]
    q_m, k_m, v_m, o_m, i_pre, f_pre, q_a, k_a, v_a = jnp.split(proj, offs, axis=-1)

    qk = jax.nn.silu(causal_depthwise_conv(jnp.concatenate([q_m, k_m], axis=-1), conv_w, conv_b))
    q_m, k_m = jnp.split(qk, 2, axis=-1)
    hm = mlstm_chunkwise(
        q_m.reshape(B, S, MLSTM_HEADS, MLSTM_QK_DIM).astype(f32),
        k_m.reshape(B, S, MLSTM_HEADS, MLSTM_QK_DIM).astype(f32),
        v_m.reshape(B, S, MLSTM_HEADS, MLSTM_V_DIM).astype(f32),
        (i_pre + b_i).astype(f32), (f_pre + b_f).astype(f32))
    hm = rms_norm(hm, g_mlstm_head) * jax.nn.sigmoid(o_m.reshape(B, S, MLSTM_HEADS, MLSTM_V_DIM).astype(f32))
    hm = hm.reshape(B, S, MLSTM_V_W).astype(h.dtype)

    ha = sliding_window_sink_attention(
        q_a.reshape(B, S, ATTN_HEADS, HEAD_DIM),
        k_a.reshape(B, S, KV_HEADS, HEAD_DIM),
        v_a.reshape(B, S, KV_HEADS, HEAD_DIM), attn_sinks)
    ha = rms_norm(ha.reshape(B, S, ATTN_Q_W), g_attn_out).astype(h.dtype)

    return jnp.concatenate([hm, ha], axis=-1) @ w_out

def squared_relu_mlp(h, w_up, w_down):
    return jnp.square(jax.nn.relu(h @ w_up)) @ w_down

def first_inputs(seed: int = 0) -> dict:
    key = jax.random.key(seed)
    ks = jax.random.split(key, 24)
    nrm = jax.random.normal
    L = DEPTH
    def gain(k, shape):
        return 1.0 + 0.05 * nrm(k, shape, jnp.float32)
    return {
        'x': nrm(ks[0], (BATCH, SEQ, D_MODEL), jnp.float32),
        'c': nrm(ks[1], (BATCH, D_MODEL), jnp.float32),
        'w_ada': 0.5 * D_MODEL ** -0.5 * nrm(ks[2], (L, D_MODEL, N_MOD * D_MODEL), jnp.float32),
        'b_ada': 0.02 * nrm(ks[3], (L, N_MOD * D_MODEL), jnp.float32),
        'g_pre_mix': gain(ks[4], (L, D_MODEL)),
        'g_post_mix': gain(ks[5], (L, D_MODEL)),
        'g_pre_mlp': gain(ks[6], (L, D_MODEL)),
        'g_post_mlp': gain(ks[7], (L, D_MODEL)),
        'w_in': D_MODEL ** -0.5 * nrm(ks[8], (L, D_MODEL, D_IN), jnp.float32),
        'conv_w': CONV_WIDTH ** -0.5 * nrm(ks[9], (L, CONV_WIDTH, 2 * MLSTM_QK_W), jnp.float32),
        'conv_b': 0.02 * nrm(ks[10], (L, 2 * MLSTM_QK_W), jnp.float32),
        'b_i': 0.1 * nrm(ks[11], (L, MLSTM_HEADS), jnp.float32),
        'b_f': jnp.linspace(3.0, 6.0, MLSTM_HEADS, dtype=jnp.float32)[None, :] + 0.1 * nrm(ks[12], (L, MLSTM_HEADS), jnp.float32),
        'g_mlstm_head': gain(ks[13], (L, MLSTM_HEADS, MLSTM_V_DIM)),
        'g_attn_out': gain(ks[14], (L, ATTN_Q_W)),
        'attn_sinks': 0.5 * nrm(ks[15], (L, ATTN_HEADS), jnp.float32),
        'w_out': D_MIX ** -0.5 * nrm(ks[16], (L, D_MIX, D_MODEL), jnp.float32),
        'w_up': D_MODEL ** -0.5 * nrm(ks[17], (L, D_MODEL, D_FF), jnp.float32),
        'w_down': D_FF ** -0.5 * nrm(ks[18], (L, D_FF, D_MODEL), jnp.float32),
    }

def first_block(x, c, w_ada, b_ada, g_pre_mix, g_post_mix, g_pre_mlp, g_post_mlp, w_in, conv_w, conv_b,
              b_i, b_f, g_mlstm_head, g_attn_out, attn_sinks, w_out, w_up, w_down):
    c_act = jax.nn.silu(c)
    for l in range(DEPTH):
        mod = c_act @ w_ada[l] + b_ada[l]
        shift_a, scale_a, gate_a, shift_m, scale_m, gate_m = [m[:, None, :] for m in jnp.split(mod, N_MOD, axis=-1)]
        h = rms_norm(x, g_pre_mix[l]) * (1.0 + scale_a) + shift_a
        y = token_mixer(h, w_in[l], conv_w[l], conv_b[l], b_i[l], b_f[l], g_mlstm_head[l],
                        g_attn_out[l], attn_sinks[l], w_out[l])
        x = x + gate_a * rms_norm(y, g_post_mix[l])
        h = rms_norm(x, g_pre_mlp[l]) * (1.0 + scale_m) + shift_m
        y = squared_relu_mlp(h, w_up[l], w_down[l])
        x = x + gate_m * rms_norm(y, g_post_mlp[l])
    return x


N_A_LAYERS = DEPTH // 2
N_B_LAYERS = DEPTH - N_A_LAYERS
S5_WIDTH = D_MODEL
S5_GROUP = 16
S5_GROUPS = S5_WIDTH // S5_GROUP
S5_STATE = 64
DT_MIN = 1e-3
DT_MAX = 1e-1
FOX_HEAD_DIM = 128
FOX_HEADS = D_MODEL // FOX_HEAD_DIM
FOX_WIDTH = FOX_HEADS * FOX_HEAD_DIM
Q_BLOCK = 128
RMS_EPS = 1e-6
NEG_INF = -1e30


F32 = jnp.float32

def rmsnorm(x, g):
    xf = x.astype(F32)
    y = xf * lax.rsqrt(jnp.mean(xf * xf, axis=-1, keepdims=True) + RMS_EPS)
    return (y * g.astype(F32)).astype(x.dtype)

def s5_ssm(u, a_re, a_im, log_dt, b_re, b_im, c_re, c_im, d_skip):
    bsz, seq, _ = u.shape
    uf = u.astype(F32).reshape(bsz, seq, S5_GROUPS, S5_GROUP)
    dt = jnp.exp(log_dt.astype(F32))[:, None]
    ar = a_re.astype(F32)
    ai = a_im.astype(F32)
    mag = jnp.exp(ar * dt)
    abar_re = mag * jnp.cos(ai * dt)
    abar_im = mag * jnp.sin(ai * dt)
    den = ar * ar + ai * ai
    nr = abar_re - 1.0
    coef_re = (nr * ar + abar_im * ai) / den
    coef_im = (abar_im * ar - nr * ai) / den
    bu_re = jnp.einsum('bsgc,gpc->bsgp', uf, b_re.astype(F32))
    bu_im = jnp.einsum('bsgc,gpc->bsgp', uf, b_im.astype(F32))
    x_re = coef_re * bu_re - coef_im * bu_im
    x_im = coef_re * bu_im + coef_im * bu_re
    shape_a = (1, seq, S5_GROUPS, S5_STATE)
    a_seq_re = jnp.broadcast_to(abar_re, shape_a)
    a_seq_im = jnp.broadcast_to(abar_im, shape_a)

    def combine(left, right):
        a1r, a1i, b1r, b1i = left
        a2r, a2i, b2r, b2i = right
        return (a2r * a1r - a2i * a1i,
                a2r * a1i + a2i * a1r,
                a2r * b1r - a2i * b1i + b2r,
                a2r * b1i + a2i * b1r + b2i)

    _, _, h_re, h_im = lax.associative_scan(combine, (a_seq_re, a_seq_im, x_re, x_im), axis=1)
    y = (jnp.einsum('bsgp,gcp->bsgc', h_re, c_re.astype(F32))
         - jnp.einsum('bsgp,gcp->bsgc', h_im, c_im.astype(F32)))
    y = y + d_skip.astype(F32).reshape(S5_GROUPS, S5_GROUP) * uf
    return y.reshape(bsz, seq, S5_WIDTH)

def s5_layer(h, g_pre, g_post, w_in, a_re, a_im, log_dt, b_re, b_im, c_re, c_im, d_skip, w_glu, b_glu, w_out):
    xn = rmsnorm(h, g_pre)
    uz = xn @ w_in
    u, z = jnp.split(uz, 2, axis=-1)
    y = s5_ssm(u, a_re, a_im, log_dt, b_re, b_im, c_re, c_im, d_skip)
    y = jax.nn.gelu(y)
    y = y * jax.nn.sigmoid(y @ w_glu.astype(F32) + b_glu.astype(F32))
    y = y.astype(h.dtype) * jax.nn.silu(z)
    return h + rmsnorm(y @ w_out, g_post)

def shared_kv(h, g_kv, w_kv, b_f):
    bsz, seq, _ = h.shape
    kvf = rmsnorm(h, g_kv) @ w_kv
    k = kvf[..., :FOX_WIDTH]
    v = kvf[..., FOX_WIDTH:2 * FOX_WIDTH]
    f_logit = kvf[..., 2 * FOX_WIDTH:]
    k = k.reshape(bsz, seq, FOX_HEADS, FOX_HEAD_DIM).transpose(0, 2, 1, 3)
    v = v.reshape(bsz, seq, FOX_HEADS, FOX_HEAD_DIM).transpose(0, 2, 1, 3)
    log_f = jax.nn.log_sigmoid(f_logit.astype(F32) + b_f.astype(F32))
    cum = jnp.cumsum(log_f, axis=1).transpose(0, 2, 1)
    return k, v, cum

def fox_attention(q, k, v, cum):
    bsz, nh, seq, dh = q.shape
    nblk = seq // Q_BLOCK
    qb = q.reshape(bsz, nh, nblk, Q_BLOCK, dh).transpose(2, 0, 1, 3, 4)
    cb = cum.reshape(bsz, nh, nblk, Q_BLOCK).transpose(2, 0, 1, 3)
    kpos = jnp.arange(seq)
    scale = dh ** -0.5

    def block(args):
        q_i, c_i, i = args
        s = jnp.einsum('bhqd,bhkd->bhqk', q_i, k, preferred_element_type=F32) * scale
        s = s + c_i[..., :, None] - cum[:, :, None, :]
        qpos = i * Q_BLOCK + jnp.arange(Q_BLOCK)
        s = jnp.where(kpos[None, :] <= qpos[:, None], s, NEG_INF)
        p = jax.nn.softmax(s, axis=-1)
        return jnp.einsum('bhqk,bhkd->bhqd', p.astype(v.dtype), v)

    o = lax.map(block, (qb, cb, jnp.arange(nblk)))
    return o.transpose(1, 2, 0, 3, 4).reshape(bsz, nh, seq, dh)

def fox_layer(h, g_pre, g_post, w_in, w_out, k, v, cum):
    bsz, seq, _ = h.shape
    qz = rmsnorm(h, g_pre) @ w_in
    q, z = jnp.split(qz, 2, axis=-1)
    q = q.reshape(bsz, seq, FOX_HEADS, FOX_HEAD_DIM).transpose(0, 2, 1, 3)
    o = fox_attention(q, k, v, cum)
    o = o.transpose(0, 2, 1, 3).reshape(bsz, seq, FOX_WIDTH)
    o = o.astype(h.dtype) * jax.nn.silu(z)
    return h + rmsnorm(o @ w_out, g_post)

def second_inputs(seed: int = 0) -> dict:
    key = jax.random.key(seed)
    ks = jax.random.split(key, 24)
    nrm = lambda k, shp, s: jax.random.normal(k, shp, F32) * s
    n = jnp.arange(S5_STATE, dtype=F32)
    a_re = -0.5 + nrm(ks[4], (N_A_LAYERS, S5_GROUPS, S5_STATE), 0.01)
    a_im = math.pi * n + nrm(ks[5], (N_A_LAYERS, S5_GROUPS, S5_STATE), 0.01)
    log_dt = jax.random.uniform(ks[6], (N_A_LAYERS, S5_GROUPS), F32, math.log(DT_MIN), math.log(DT_MAX))
    return {
        "x": nrm(ks[0], (BATCH, SEQ, D_MODEL), 1.0),
        "norm_pre": 1.0 + nrm(ks[1], (DEPTH, D_MODEL), 0.02),
        "norm_post": 1.0 + nrm(ks[2], (DEPTH, D_MODEL), 0.02),
        "s5_w_in": nrm(ks[3], (N_A_LAYERS, D_MODEL, 2 * S5_WIDTH), D_MODEL ** -0.5),
        "s5_a_re": a_re,
        "s5_a_im": a_im,
        "s5_log_dt": log_dt,
        "s5_b_re": nrm(ks[7], (N_A_LAYERS, S5_GROUPS, S5_STATE, S5_GROUP), (2 * S5_GROUP) ** -0.5),
        "s5_b_im": nrm(ks[8], (N_A_LAYERS, S5_GROUPS, S5_STATE, S5_GROUP), (2 * S5_GROUP) ** -0.5),
        "s5_c_re": nrm(ks[9], (N_A_LAYERS, S5_GROUPS, S5_GROUP, S5_STATE), S5_STATE ** -0.5),
        "s5_c_im": nrm(ks[10], (N_A_LAYERS, S5_GROUPS, S5_GROUP, S5_STATE), S5_STATE ** -0.5),
        "s5_d": nrm(ks[11], (N_A_LAYERS, S5_WIDTH), 1.0),
        "s5_w_glu": nrm(ks[12], (N_A_LAYERS, S5_WIDTH, S5_WIDTH), S5_WIDTH ** -0.5),
        "s5_b_glu": nrm(ks[13], (N_A_LAYERS, S5_WIDTH), 0.01),
        "s5_w_out": nrm(ks[14], (N_A_LAYERS, S5_WIDTH, D_MODEL), S5_WIDTH ** -0.5),
        "kv_norm": 1.0 + nrm(ks[15], (D_MODEL,), 0.02),
        "kv_w": nrm(ks[16], (D_MODEL, 2 * FOX_WIDTH + FOX_HEADS), D_MODEL ** -0.5),
        "kv_b_f": jax.random.uniform(ks[17], (FOX_HEADS,), F32, 2.0, 7.0),
        "fox_w_in": nrm(ks[18], (N_B_LAYERS, D_MODEL, 2 * FOX_WIDTH), D_MODEL ** -0.5),
        "fox_w_out": nrm(ks[19], (N_B_LAYERS, FOX_WIDTH, D_MODEL), FOX_WIDTH ** -0.5),
    }

def second_block(x, norm_pre, norm_post, s5_w_in, s5_a_re, s5_a_im, s5_log_dt, s5_b_re, s5_b_im,
              s5_c_re, s5_c_im, s5_d, s5_w_glu, s5_b_glu, s5_w_out, kv_norm, kv_w, kv_b_f,
              fox_w_in, fox_w_out):
    h = x
    k = v = cum = None
    for layer in range(DEPTH):
        if layer < N_A_LAYERS:
            i = layer
            h = s5_layer(h, norm_pre[layer], norm_post[layer], s5_w_in[i], s5_a_re[i], s5_a_im[i],
                         s5_log_dt[i], s5_b_re[i], s5_b_im[i], s5_c_re[i], s5_c_im[i], s5_d[i],
                         s5_w_glu[i], s5_b_glu[i], s5_w_out[i])
        else:
            if layer == N_A_LAYERS:
                k, v, cum = shared_kv(h, kv_norm, kv_w, kv_b_f)
            j = layer - N_A_LAYERS
            h = fox_layer(h, norm_pre[layer], norm_post[layer], fox_w_in[j], fox_w_out[j], k, v, cum)
    return h


def setup_inputs(seed=0):
    out = dict(first_inputs(seed))
    for name, value in second_inputs(seed + 1).items():
        if name != "x":
            out[name + "_2"] = value
    return out


def reference(
    x, c, w_ada, b_ada, g_pre_mix, g_post_mix, g_pre_mlp, g_post_mlp, w_in, conv_w, conv_b, b_i,
    b_f, g_mlstm_head, g_attn_out, attn_sinks, w_out, w_up, w_down, norm_pre_2, norm_post_2,
    s5_w_in_2, s5_a_re_2, s5_a_im_2, s5_log_dt_2, s5_b_re_2, s5_b_im_2, s5_c_re_2, s5_c_im_2,
    s5_d_2, s5_w_glu_2, s5_b_glu_2, s5_w_out_2, kv_norm_2, kv_w_2, kv_b_f_2, fox_w_in_2,
    fox_w_out_2,
):
    x = first_block(
        x, c, w_ada, b_ada, g_pre_mix, g_post_mix, g_pre_mlp, g_post_mlp, w_in, conv_w, conv_b,
        b_i, b_f, g_mlstm_head, g_attn_out, attn_sinks, w_out, w_up, w_down,
    )
    return second_block(
        x, norm_pre_2, norm_post_2, s5_w_in_2, s5_a_re_2, s5_a_im_2, s5_log_dt_2, s5_b_re_2,
        s5_b_im_2, s5_c_re_2, s5_c_im_2, s5_d_2, s5_w_glu_2, s5_b_glu_2, s5_w_out_2, kv_norm_2,
        kv_w_2, kv_b_f_2, fox_w_in_2, fox_w_out_2,
    )


_drawn_inputs = setup_inputs


def setup_inputs(seed=0):
    import zlib

    import numpy as np

    out = dict(_drawn_inputs(seed))
    spreads = {}
    factors = {'conv_b': 8.0,
     'b_i': 8.0,
     'g_mlstm_head': 3.274,
     'norm_post_2': 3.005,
     's5_a_re_2': 8.0,
     's5_b_glu_2': 8.0,
     'kv_norm_2': 4.75}
    for name, (base, spread) in spreads.items():
        noise = np.random.default_rng([zlib.crc32(name.encode()), seed]).standard_normal(out[name].shape)
        drawn = base * np.exp(spread * noise) if base else spread * noise
        out[name] = jnp.asarray(drawn.astype(out[name].dtype))
    for name, factor in factors.items():
        out[name] = (out[name] * factor).astype(out[name].dtype)
    return out
```

```python
import numpy as np
from contextlib import ExitStack

import concourse.bass as bass
from concourse import mybir

F32 = mybir.dt.float32
F32R = mybir.dt.float32r
ALU = mybir.AluOpType
ACT = mybir.ActivationFunctionType
AX = mybir.AxisListType

P = 128
T = 256
KT = 16
D = 2048
BIG = -1e30
RING = 5
EPS = 1e-6

PRE_MIX, POST_MIX, PRE_MLP, POST_MLP, B_ADA, CONV_W, CONV_B, G_HEAD, G_ATT, SINK, GATE_B = (
    0, 16, 32, 48, 64, 160, 192, 200, 208, 216, 232)
PER_LAYER = 234
S5_PRE, S5_POST, S5_D, S5_BGLU, KV_G, FOX_PRE, FOX_POST, C_COL, KV_BF = (
    2 * PER_LAYER + n for n in (0, 16, 32, 48, 64, 80, 96, 112, 128))
N_PRM = 2 * PER_LAYER + 129

IDENT, NDIST, MASKT, MASKF, N_CST = 0, 128, 512, 640, 1024


class Lane:

    def __init__(self, sem):
        self.sem, self.n, self.items, self.seen = sem, 0, [], {}

    def need(self, waits):
        out = []
        for w in waits:
            if w is None:
                continue
            if isinstance(w, list):
                out += self.need(w)
            elif self.seen.get(id(w[0]), 0) < w[1]:
                self.seen[id(w[0])] = w[1]
                out.append(w)
        return out

    def put(self, fn, *waits, sig=True):
        w = self.need(waits)
        if sig:
            self.n += 1
        self.items.append((w, fn, self.sem if sig else None, 1))
        return (self.sem, self.n)

    def dma(self, fn, sem, value, *waits):
        self.items.append((self.need(waits), fn, sem, 16))
        return (sem, value)

    def last(self):
        return (self.sem, self.n) if self.n else None

    def emit(self, eng):
        for waits, fn, sem, by in self.items:
            for s, v in waits:
                eng.wait_ge(s, v)
            ins = fn(eng)
            if sem is not None:
                ins.then_inc(sem, by)


class Slots:

    def __init__(self, items):
        self.items, self.free, self.at = items, [[] for _ in items], 0

    def take(self):
        i = self.at % len(self.items)
        self.at += 1
        return i, self.items[i], self.free[i]

    def give(self, i, *tokens):
        self.free[i] = list(tokens)


def build(nc, d, out):
    ctx = ExitStack()
    with ctx:
        base = (nc.sbuf_base + 63) // 64 * 64
        top = nc.sbuf_usable_end
        kb = 1024

        def at(name, shape, off, dt=F32):
            return nc.alloc_sbuf_tensor_at(name, (P, *shape), dt, offset=off)

        def psum(name):
            return ctx.enter_context(nc.psum_tensor(name, [P, 512], F32))

        def sem(name):
            return ctx.enter_context(nc.semaphore(name))

        o = base
        X = at("X", (KT, T), o); o += 16 * kb
        RAW = [at(f"raw{i}", (KT, 128), o + 8 * kb * i) for i in range(RING)]; o += 8 * kb * RING
        WH = [at(f"wh{i}", (KT, 128), o + 8 * kb * i, F32R) for i in range(2)]; o += 16 * kb
        WL = [at(f"wl{i}", (KT, 128), o + 8 * kb * i, F32R) for i in range(2)]; o += 16 * kb
        CST = at("cst", (N_CST,), o); o += 4 * N_CST
        PRM = at("prm", (N_PRM,), o); o += (4 * N_PRM + 63) // 64 * 64
        MOD = at("mod", (12, 16), o); o += 768
        ONES = at("ones", (256,), o); o += 1024
        SM = at("sm", (96,), o); o += 384
        RS = at("rs", (T,), o); o += 1024
        LN = at("ln", (T,), o); o += 1024
        A0 = o
        HH = at("HH", (KT, T), A0, F32R)
        HL = at("HL", (KT, T), A0 + 16 * kb, F32R)
        M = A0 + 32 * kb
        assert M + 92 * kb <= top, (M + 92 * kb, top)

        def m(name, shape, off, dt=F32):
            return at(name, shape, int(M + off * kb), dt)

        BK = [psum(f"bk{i}") for i in range(8)]
        ident = CST[:, IDENT:IDENT + 128]

        pe, act, dve, sp = (Lane(sem(f"s_{n}")) for n in ("pe", "act", "dve", "sp"))
        s_raw = [sem(f"s_raw{i}") for i in range(RING)]
        s_cst, s_prm, s_row, s_tab, s_out = (sem(f"s_{n}") for n in ("cst", "prm", "row", "tab", "out"))
        s_b = [sem(f"s_b{i}") for i in range(3)]
        gbank = Slots([0, 1, 2])
        bbank = Slots([3, 4, 5, 6, 7])

        def mm(out_, l, r, start, stop, *waits, sig=False):
            return pe.put(lambda e: e.matmul(out_, l, r, start=start, stop=stop, skip_group_check=True),
                          *waits, sig=sig)

        def tr(out_, in_, *waits, sig=False):
            n = in_.shape[0]
            return pe.put(lambda e: e.transpose(out_, in_, ident[0:n, 0:n]), *waits, sig=sig)

        def fn(out_, in_, f, *waits, **kw):
            return act.put(lambda e: e.activation(out_, in_, f, **kw), *waits)

        def tt(out_, a, b, op, *waits):
            return dve.put(lambda e: e.tensor_tensor(out_, a, b, op), *waits)

        def ts(out_, a, s1, s2, op0, op1, *waits):
            if op1 is None:
                return dve.put(lambda e: e.tensor_scalar(out_, a, s1, None, op0), *waits)
            return dve.put(lambda e: e.tensor_scalar(out_, a, s1, s2, op0, op1), *waits)

        def stt(out_, a, s, b, op0, op1, *waits):
            return dve.put(lambda e: e.scalar_tensor_tensor(out_, a, s, b, op0, op1), *waits)

        def cp(out_, in_, *waits):
            return dve.put(lambda e: e.tensor_copy(out_, in_), *waits)

        def rec(out_, in_, *waits):
            return dve.put(lambda e: e.reciprocal(out_, in_), *waits)

        def bc(ap, n):
            return ap.rearrange("p (a t) -> p a t", a=1).to_broadcast([ap.shape[0], n, ap.shape[1]])

        def fence():
            return [t for t in (pe.last(), act.last(), dve.last()) if t]

        stream = []

        def ada(l, piece):
            return [("ada", d["w_ada"][l, piece, k], (l, piece, k)) for k in range(16)]

        def slabs(w, idx):
            return [("w", w[i], None) for i in idx]

        def blend(a, b):
            out_, n = [], 0
            for i, s in enumerate(a):
                out_.append(s)
                while n < len(b) and (n + 1) * len(a) <= (i + 1) * len(b):
                    out_.append(b[n])
                    n += 1
            return out_ + b[n:]

        SHIFT_A, SCALE_A, GATE_A, SHIFT_M, SCALE_M, GATE_M = range(6)
        stream += ada(0, SCALE_A) + ada(0, SHIFT_A)
        mlp_order = [n for j in range(4) for n in [("u", 16 * j + i) for i in range(16)]
                     + [("d", 16 * j + i) for i in range(16)]]
        for l in range(2):
            stream += blend(slabs(d["w_in"][l], range(37)), ada(l, GATE_A) + ada(l, SCALE_M))
            stream += blend(slabs(d["w_out"][l], range(16)), ada(l, SHIFT_M))
            up_down = [("w", d["w_up" if k == "u" else "w_down"][l, i], None) for k, i in mlp_order]
            stream += blend(up_down, ada(l, GATE_M) + (ada(1, SCALE_A) + ada(1, SHIFT_A) if l == 0 else []))
        stream += slabs(d["s5_w_in"], range(32))
        stream += slabs(d["s5_w_glu"], range(16))
        stream += slabs(d["s5_w_out"], range(16))
        stream += slabs(d["kv_w"], range(33))
        stream += slabs(d["fox_w_in"], range(32))
        stream += slabs(d["fox_w_out"], range(16))

        raw_free = [[] for _ in range(RING)]
        loaded, staged_at = [0], [0]
        wslots = Slots([0, 1])
        ready = []
        background = []

        def load_next():
            n = loaded[0]
            if n >= len(stream):
                return
            loaded[0] += 1
            s = n % RING
            dst = RAW[s][:, :, :].rearrange("p a b -> p (a b)")
            sp.dma(lambda e, dst=dst, src=stream[n][1]: e.dma_start(dst, src), s_raw[s],
                   16 * (n // RING + 1), raw_free[s])

        ACC = m("acc", (D,), 76)
        ROW = m("row", (D,), 84)
        acc_tok, acc_read, acc_gen = [None], [True], [None]
        row_n = [0]
        row_free = [None]
        mod_ready = {}

        def finish_ada(l, piece, tok):
            last = None
            for c in range(4):
                i, b, free = bbank.take()
                t = mm(BK[b][0:1, :], ONES[:, 0:1], ACC[:, 512 * c:512 * c + 512], True, True,
                       tok, free, ones_tok, sig=True)
                last = fn(ROW[0:1, 512 * c:512 * c + 512], BK[b][0:1, :], ACT.Copy, t, row_free[0])
                bbank.give(i, last)
                acc_tok[0] = t
                acc_read[0] = c == 3
                yield
            row_n[0] += 1
            col = MOD[:, 6 * l + piece, :]
            src = ROW[0:1, :].rearrange("o (p k) -> o p k", k=16)
            t = sp.dma(lambda e: e.dma_start(col, src), s_row, 16 * row_n[0], last)
            row_free[0] = t
            yield
            b0 = PER_LAYER * l + B_ADA + 16 * piece
            t = tt(col, col, PRM[:, b0:b0 + 16], ALU.add, t, prm_tok)
            if piece in (SCALE_A, SCALE_M):
                g = PER_LAYER * l + (PRE_MIX if piece == SCALE_A else PRE_MLP)
                t = stt(col, col, 1.0, PRM[:, g:g + 16], ALU.add, ALU.mult, t)
            if piece in (GATE_A, GATE_M):
                g = PER_LAYER * l + (POST_MIX if piece == GATE_A else POST_MLP)
                t = tt(col, col, PRM[:, g:g + 16], ALU.mult, t)
            mod_ready[(l, piece)] = t

        def stage_next():
            n = staged_at[0]
            if n >= len(stream):
                return
            staged_at[0] += 1
            kind, _, key = stream[n]
            s = n % RING
            here = (s_raw[s], 16 * (n // RING + 1))
            if kind == "ada":
                l, piece, k = key
                raw = RAW[s][:, :, :].rearrange("p a b -> p (a b)")
                if k == 0:
                    while not acc_read[0]:
                        next(acc_gen[0])
                    t = ts(ACC[:, :], raw, CA[:, 0:1], None, ALU.mult, None, here, ca_tok, acc_tok[0])
                else:
                    t = stt(ACC[:, :], raw, CA[:, k:k + 1], ACC[:, :], ALU.mult, ALU.add, here, dve.last())
                raw_free[s] = [t]
                if k == 15:
                    acc_read[0] = False
                    acc_gen[0] = finish_ada(l, piece, t)
                    background.insert(0, acc_gen[0])
            else:
                i, w, free = wslots.take()
                th = fn(WH[w][:, :, :], RAW[s][:, :, :], ACT.Copy, here, free)
                tl = tt(WL[w][:, :, :], RAW[s][:, :, :], WH[w][:, :, :].bitcast(F32), ALU.subtract, here, th, free)
                raw_free[s] = [th, tl]
                ready.append((i, w, [th, tl]))
            load_next()

        def pump(n=1):
            for _ in range(n):
                if not background:
                    return
                g = background[0]
                try:
                    next(g)
                except StopIteration:
                    background.remove(g)

        def drain():
            while background:
                pump()

        def want_mod(key):
            while key not in mod_ready:
                if background:
                    pump()
                else:
                    stage_next()
            return mod_ready[key]

        def gemm(count, xh, xl, xready, evac, each=1):
            order = sorted(range(KT), key=lambda k: xready(k)[1]) if False else range(KT)
            pending = None
            for n in range(count):
                while not ready:
                    stage_next()
                i, w, wt = ready.pop(0)
                g, b, free = gbank.take()
                ps = BK[b][:, 0:T]
                for q, k in enumerate(order):
                    wh, wl = WH[w][:, k, :], WL[w][:, k, :]
                    mm(ps, wh, xh(k), q == 0, False, wt[0], free, xready(k))
                    mm(ps, wh, xl(k), False, False)
                    t = mm(ps, wl, xh(k), False, q == KT - 1, wt[1], sig=q == KT - 1)
                wslots.give(i, t)
                while not ready and staged_at[0] < len(stream):
                    stage_next()
                if pending:
                    gbank.give(pending[0], evac(*pending[1:]))
                pending = (g, n, ps, t)
                pump(each)
            gbank.give(pending[0], evac(*pending[1:]))
            return t

        Xf = X[:, :, :]
        cst_tok = sp.dma(lambda e: e.dma_start(CST[:, :], d["cst"]), s_cst, 16)
        prm_tok = sp.dma(lambda e: e.dma_start(PRM[:, :], d["prm"]), s_prm, 16)
        for _ in range(RING):
            load_next()
        x_tok = act.dma(lambda e: e.dma_start(Xf, d["x"]), s_tab, 16)
        ones_tok = dve.put(lambda e: e.memset(ONES[:, :], 1.0))
        pe.need([cst_tok, ones_tok])
        pe.items.append(([cst_tok, ones_tok], lambda e: e.wait_ge(s_cst, 16), None, 0))

        CA, CE = SM[:, 16:32], SM[:, 32:48]
        ccol = PRM[:, C_COL:C_COL + 16]
        t = fn(CE, ccol, ACT.Exp, prm_tok, scale=-1.0)
        t = ts(CE, CE, 1.0, None, ALU.add, None, t)
        t = rec(CE, CE, t)
        ca_tok = tt(CA, CE, ccol, ALU.mult, t, prm_tok)

        SQ = m("sq", (KT, T), 60)
        RED = LN

        def stats(src, *waits):
            tk = []
            for c in range(4):
                tk.append(fn(SQ[:, 4 * c:4 * c + 4, :], src[:, 4 * c:4 * c + 4, :], ACT.Square, *waits))
            t = dve.put(lambda e: e.tensor_reduce(RED[:, :], SQ[:, :, :].rearrange("p k t -> p t k"),
                                                  AX.X, ALU.add), tk[3], *waits)
            i, b, free = bbank.take()
            t = mm(BK[b][:, 0:T], ONES[:, 0:128], RED[:, :], True, True, t, free, sig=True)
            t = rsqrt(RS[:, :], BK[b][:, 0:T], D, LN[:, :], t)
            bbank.give(i, act.last())
            return t

        def rsqrt(out_, in_, n, tmp, *waits):
            t = fn(tmp, in_, ACT.Ln, *waits, scale=1.0 / n, bias=EPSC[:, :])
            return fn(out_, tmp, ACT.Exp, t, scale=-0.5)

        EPSC = SM[:, 0:1]
        eps_tok = dve.put(lambda e: e.memset(EPSC, EPS))
        act.items.append((act.need([eps_tok]), lambda e: e.wait_ge(dve.sem, eps_tok[1]), None, 0))

        def to_h(gs, sh, ts_, *waits):
            toks = []
            for c in range(4):
                q = slice(4 * c, 4 * c + 4)
                t = tt(SQ[:, q, :], X[:, q, :], bc(RS[:, :], 4), ALU.mult, *waits)
                last = []
                for k in range(4 * c, 4 * c + 4):
                    kw = {"scale": gs[:, k:k + 1]}
                    if sh is not None:
                        kw["bias"] = sh[:, k:k + 1]
                    last = fn(SQ[:, k, :], SQ[:, k, :], ACT.Identity, t, ts_, **kw)
                th = fn(HH[:, q, :], SQ[:, q, :], ACT.Copy, last)
                tl = tt(HL[:, q, :], SQ[:, q, :], HH[:, q, :].bitcast(F32), ALU.subtract, th)
                toks += [[th, tl]] * 4
            return toks

        def add_y(Y, gg, gtok, *waits):
            t0 = stats(Y, *waits)
            t = None
            for c in range(4):
                q = slice(4 * c, 4 * c + 4)
                t = tt(SQ[:, q, :], Y[:, q, :], bc(RS[:, :], 4), ALU.mult, t0, *waits)
                for k in range(4 * c, 4 * c + 4):
                    t2 = stt(X[:, k, :], SQ[:, k, :], gg[:, k:k + 1], X[:, k, :], ALU.mult, ALU.add, t, gtok)
            return t2

        def split(hi, lo, src, *waits):
            th = fn(hi, src, ACT.Copy, *waits)
            tl = tt(lo, src, hi.bitcast(F32), ALU.subtract, th, *waits)
            return [th, tl]

        QA = m("qa", (8, T), 0)
        QAL = m("qal", (8, T), 0, F32R)
        KA = m("ka", (2, T), 8)
        VA = m("va", (2, T), 10)
        QM = m("qm", (4, T), 12)
        KM = m("km", (4, T), 16)
        VM = m("vm", (2, 1024), 20)
        OS = m("os", (8, T), 28)
        OSL = m("osl", (8, T), 28, F32R)
        AHI = m("ahi", (8, T), 36, F32R)
        MHI = m("mhi", (8, T), 44, F32R)
        S0 = 52
        Y1 = m("y1", (KT, T), 12)
        CV = [m(f"cv{i}", (3 + T,), S0 + 1.125 * i) for i in range(2)]
        CO = [m(f"co{i}", (T,), S0 + 2.25 + i) for i in range(2)]
        TV = [m(f"tv{i}", (T,), S0 + 4.25 + i) for i in range(2)]
        EV = [m(f"ev{i}", (T,), S0 + 6.25 + i) for i in range(2)]
        GI = m("gi", (T,), S0 + 8.25)
        GF = m("gf", (T,), S0 + 9.25)
        GT = m("gt", (T,), S0 + 10.25)
        GR = m("gr", (2, T), S0 + 11.25)
        AC = m("ac", (2, 4), S0 + 13.25)
        EM = m("em", (T,), S0 + 13.5)
        E0 = m("e0", (384,), S0 + 14.5)
        P0 = m("p0", (384,), S0 + 16)
        HN = m("hn", (2, T), S0 + 17.5)
        HS = m("hs", (2, T), S0 + 19.5)
        DN = m("dn", (T,), S0 + 21.5)
        TA = [m(f"ta{i}", (384,), S0 + 8.25 + 1.5 * i) for i in range(2)]
        PA = [m(f"pa{i}", (384,), S0 + 11.25 + 1.5 * i) for i in range(2)]
        XA = m("xa", (16,), S0 + 22.5)

        def transposed(dst, src, *waits):
            i, b, free = bbank.take()
            tr(BK[b][:, 0:128], src[:, 0:128], *waits, free)
            t = tr(BK[b][:, 128:256], src[:, 128:256], sig=True)
            t = cp(dst, BK[b][:, 0:256].rearrange("p (a f) -> p a f", a=2), t)
            bbank.give(i, t)
            return t

        def sigmoid_of(dst, e, *waits):
            t = ts(e, e, 1.0, None, ALU.add, None, *waits)
            return rec(dst, e, t)

        def conv_evac(l, n, ps, t, slot, dst, fr):
            cv, co, ev = CV[slot], CO[slot], EV[slot]
            w0 = PER_LAYER * l + CONV_W + 4 * n
            b0 = PER_LAYER * l + CONV_B + n
            t = fn(cv[:, 3:3 + T], ps, ACT.Copy, t, fr)
            free = t
            t = ts(co[:, :], cv[:, 0:T], PRM[:, w0:w0 + 1], PRM[:, b0:b0 + 1], ALU.mult, ALU.add, t)
            for j in range(1, 4):
                t = stt(co[:, :], cv[:, j:j + T], PRM[:, w0 + j:w0 + j + 1], co[:, :], ALU.mult, ALU.add, t)
            t = fn(ev[:, :], co[:, :], ACT.Exp, t, scale=-1.0)
            t = sigmoid_of(ev[:, :], ev[:, :], t)
            t = tt(dst, co[:, :], ev[:, :], ALU.mult, t)
            return free, t

        def mixer(l, xtok, start_tok):
            prm = PER_LAYER * l
            tokv = {}
            zt = None
            for i in range(2):
                zt = dve.put(lambda e, i=i: e.memset(CV[i][:, 0:3], 0.0), start_tok)
            slot_tok = [zt, zt]

            def evac(n, ps, t):
                if n < 8:
                    r = fn(QA[:, n, :], ps, ACT.Copy, t, start_tok)
                    tokv["qa", n] = r
                elif n < 10:
                    r = fn(KA[:, n - 8, :], ps, ACT.Copy, t, start_tok)
                    tokv["ka", n - 8] = r
                elif n < 12:
                    s = n % 2
                    r = fn(TV[s][:, :], ps, ACT.Copy, t, tokv.get(("tv", s)), start_tok)
                    tokv["tv", s] = tokv["va", n - 10] = transposed(
                        VA[:, :, 128 * (n - 10):128 * (n - 9)], TV[s], r)
                elif n == 12:
                    r = cp(GI[0:4, :], ps[0:4, :], t, tokv["att"])
                    r = cp(GF[0:4, :], ps[32:36, :], t, tokv["att"])
                    tokv["gate"] = r
                    gates(r)
                elif n < 21:
                    j = n - 13
                    s = j % 2
                    dst = QM[:, j, :] if j < 4 else KM[:, j - 4, :]
                    r, slot_tok[s] = conv_evac(l, j, ps, t, s, dst, slot_tok[s])
                    tokv["qk", j] = slot_tok[s]
                elif n < 29:
                    j = n - 21
                    s = n % 2
                    r = fn(TV[s][:, :], ps, ACT.Copy, t, tokv.get(("tv", s)))
                    tokv["tv", s] = tokv["vm", j] = transposed(VM[:, :, 128 * j:128 * j + 128], TV[s], r)
                else:
                    j = n - 29
                    r = fn(OS[:, j, :], ps, ACT.Exp, t, start_tok, scale=-1.0)
                    tokv["os", j] = sigmoid_of(OS[:, j, :], OS[:, j, :], r)
                return r

            def gates(t):
                gi, gf, gt = GI[0:4, :], GF[0:4, :], GT[0:4, :]
                t = ts(gi, gi, PRM[0:4, prm + GATE_B:prm + GATE_B + 1], None, ALU.add, None, t)
                t = ts(gf, gf, PRM[0:4, prm + GATE_B + 1:prm + GATE_B + 2], None, ALU.add, None, t)
                t = fn(gt, gf, ACT.Abs, t)
                t = fn(gt, gt, ACT.Exp, t, scale=-1.0)
                t = fn(gt, gt, ACT.Ln, t, bias=1.0)
                t = stt(gf, gf, 0.0, gt, ALU.min, ALU.subtract, t)
                t = dve.put(lambda e: e.tensor_tensor_scan(gt, ONES[0:4, :], gf, 0.0, ALU.mult, ALU.add), t)
                t = tt(gi, gi, gt, ALU.subtract, t)
                t = dve.put(lambda e: e.tensor_tensor_scan(gf, ONES[0:4, :], gi, 0.0, ALU.mult, ALU.max), t)
                a_tok = t
                t = ts(GR[0:4, 0, :], gf, -1.0, None, ALU.mult, None, t)
                t = tt(gt, gt, gf, ALU.add, t)
                t = fn(GR[0:4, 1, :], gt, ACT.Exp, t, scale=-1.0)
                tokv["rows"] = t
                i, b, free = bbank.take()
                tr(BK[b][:, 0:4], GI[0:4, 0:128], a_tok, free)
                t = tr(BK[b][:, 4:8], GI[0:4, 128:256], sig=True)
                t = cp(AC[:, :, :], BK[b][:, 0:8].rearrange("p (a h) -> p a h", a=2), t)
                bbank.give(i, t)
                tokv["acol"] = t

            def attention(pair, i):
                tile = 4 * pair + i
                wait = [tokv["qa", tile], tokv["ka", pair], tokv["va", 0], tokv["va", 1], tokv.get("att")]
                mx, nm, rs, es = XA[:, 0:4], XA[:, 4:8], XA[:, 8:12], XA[:, 12:16]
                held = []
                tks = []
                for par in range(2):
                    head = (2 * pair + par) * 4 + i
                    a = slice(64 * par, 64 * par + 64)
                    bi, b, free = bbank.take()
                    mm(BK[b][:, 0:256], QA[a, tile, 128:256], KA[a, pair, :], True, True, *wait, free)
                    t = mm(BK[b][:, 256:384], QA[a, tile, 0:128], KA[a, pair, 0:128], True, True, sig=True)
                    slope = 2.0 ** (-8.0 * (head + 1) / 16) * 8.0
                    t = stt(TA[par][:, :], CST[:, NDIST:NDIST + 384], slope, BK[b][:, 0:384],
                            ALU.mult, ALU.add, t, tokv.get("att"))
                    bbank.give(bi, t)
                    t = dve.put(lambda e, p=par: e.tensor_reduce(XA[:, 2 * p:2 * p + 1], TA[p][:, 0:256],
                                                                 AX.X, ALU.max), t)
                    t = dve.put(lambda e, p=par: e.tensor_reduce(XA[:, 2 * p + 1:2 * p + 2], TA[p][:, 256:384],
                                                                 AX.X, ALU.max))
                    sk = PRM[:, prm + SINK + head:prm + SINK + head + 1]
                    t = ts(nm[:, 2 * par:2 * par + 2], mx[:, 2 * par:2 * par + 2], 0.125, sk, ALU.mult, ALU.max, t)
                    t = ts(nm[:, 2 * par:2 * par + 2], nm[:, 2 * par:2 * par + 2], -1.0, None, ALU.mult, None, t)
                    tks.append(t)
                yield
                for par in range(2):
                    head = (2 * pair + par) * 4 + i
                    sk = PRM[:, prm + SINK + head:prm + SINK + head + 1]
                    for blk, s in ((0, slice(0, 256)), (1, slice(256, 384))):
                        c = 2 * par + blk
                        t = fn(PA[par][:, s], TA[par][:, s], ACT.Exp, tks[par], tokv.get("att"), scale=0.125,
                               bias=nm[:, c:c + 1], accum_out=rs[:, c:c + 1])
                    t2 = fn(es[:, 2 * par:2 * par + 2], nm[:, 2 * par:2 * par + 2], ACT.Exp, bias=sk)
                t = tt(rs, rs, es, ALU.add, t2)
                t = rec(rs, rs, t)
                tks = []
                for par in range(2):
                    ts(PA[par][:, 0:256], PA[par][:, 0:256], rs[:, 2 * par:2 * par + 1], None, ALU.mult, None, t)
                    tks.append(ts(PA[par][:, 256:384], PA[par][:, 256:384], rs[:, 2 * par + 1:2 * par + 2],
                                  None, ALU.mult, None))
                yield
                bo, bout, free = bbank.take()
                for par in range(2):
                    bi, b, fr = bbank.take()
                    tr(BK[b][:, 0:128], PA[par][:, 256:384], tks[par], fr)
                    tr(BK[b][:, 128:256], PA[par][:, 0:128])
                    t = tr(BK[b][:, 256:384], PA[par][:, 128:256], sig=True)
                    t = cp(TA[par][:, :], BK[b][:, 0:384], t)
                    bbank.give(bi, t)
                    v = slice((2 * pair + par) * 64, (2 * pair + par) * 64 + 64)
                    a = slice(64 * par, 64 * par + 64)
                    mm(BK[bout][a, 0:256], VA[:, 0, v], TA[par][:, 0:256], True, False, t, free)
                    t = mm(BK[bout][a, 128:256], VA[:, 1, v], TA[par][:, 256:384], False, True, sig=True)
                t = cp(QA[:, tile, :], BK[bout][:, 0:256], t)
                bbank.give(bo, t)
                tokv["att"] = t
                yield

            def att_norm():
                t = tokv["att"]
                sq = SQ
                for c in range(2):
                    t1 = fn(SQ[:, 4 * c:4 * c + 4, :], QA[:, 4 * c:4 * c + 4, :], ACT.Square, t, tokv["m_done"])
                t = dve.put(lambda e: e.tensor_reduce(RED[:, :], SQ[:, 0:8, :].rearrange("p k t -> p t k"),
                                                      AX.X, ALU.add), t1)
                i, b, free = bbank.take()
                t = mm(BK[b][:, 0:T], ONES[:, 0:128], RED[:, :], True, True, t, free, sig=True)
                t = rsqrt(RS[:, :], BK[b][:, 0:T], 1024, LN[:, :], t)
                bbank.give(i, act.last())
                t = tt(SQ[:, 0:8, :], QA[:, :, :], bc(RS[:, :], 8), ALU.mult, t)
                for k in range(8):
                    c = prm + G_ATT + k
                    t1 = ts(SQ[:, k, :], SQ[:, k, :], PRM[:, c:c + 1], None, ALU.mult, None, t)
                tokv["a_hl"] = split(AHI[:, :, :], QAL[:, :, :], SQ[:, 0:8, :], t1, start_tok)

            def mlstm(h):
                i1, b1, f1 = bbank.take()
                rowb = mm(BK[b1][:, :], ident[0:4, h:h + 1].to_broadcast([4, 128]),
                          GR[0:4, :, :].rearrange("p a t -> p (a t)"), True, True, tokv["rows"], f1, sig=True)
                i2, b2, f2 = bbank.take()
                sc = BK[b2]
                mm(sc[:, 0:256], KM[:, h, 0:128], QM[:, h, :], True, True, tokv["qk", h], tokv["qk", 4 + h], f2)
                st = mm(sc[:, 256:384], KM[:, h, 128:256], QM[:, h, 128:256], True, True, sig=True)
                prev = tokv.get("m_done")
                em = fn(EM[:, :], BK[b1][:, 256:512], ACT.Copy, rowb, prev)
                mk = CST[:, MASKT:MASKT + 128]
                t = stt(E0[:, 0:128], BK[b1][:, 0:128], AC[:, 0, h:h + 1], mk, ALU.add, ALU.add,
                        em, tokv["acol"], prev)
                t = stt(E0[:, 256:384], BK[b1][:, 128:256], AC[:, 1, h:h + 1], mk, ALU.add, ALU.add)
                t = fn(E0[:, 128:256], BK[b1][:, 128:256], ACT.Exp, t, bias=AC[:, 0, h:h + 1])
                bbank.give(i1, em, t)
                fn(E0[:, 0:128], E0[:, 0:128], ACT.Exp)
                t = fn(E0[:, 256:384], E0[:, 256:384], ACT.Exp)
                yield
                t = stt(P0[:, :], sc[:, 0:384], 128.0 ** -0.5, E0[:, :], ALU.mult, ALU.mult, t, st)
                bbank.give(i2, t)
                i3, b3, f3 = bbank.take()
                i4, b4, f4 = bbank.take()
                for j in range(2):
                    v = slice(256 * h + 128 * j, 256 * h + 128 * j + 128)
                    o0 = 256 * j
                    mm(BK[b3][:, o0:o0 + 256], VM[:, 0, v], P0[:, 0:256], True, False,
                       t, f3, tokv["vm", 2 * h], tokv["vm", 2 * h + 1])
                    nt = mm(BK[b3][:, o0 + 128:o0 + 256], VM[:, 1, v], P0[:, 256:384], False, True, sig=True)
                mm(BK[b4][:, 0:256], ONES[:, 0:128], P0[:, 0:256], True, False, f4)
                t = mm(BK[b4][:, 128:256], ONES[:, 0:128], P0[:, 256:384], False, True, sig=True)
                t = fn(DN[:, :], BK[b4][:, 0:256], ACT.Abs, t, prev)
                bbank.give(i4, t)
                t = tt(DN[:, :], DN[:, :], EM[:, :], ALU.max, t, em)
                t = rec(DN[:, :], DN[:, :], t)
                t = tt(HN[:, :, :], BK[b3][:, :].rearrange("p (a t) -> p a t", a=2), bc(DN[:, :], 2),
                       ALU.mult, t, nt)
                bbank.give(i3, t)
                hn = t
                yield
                t = fn(HS[:, :, :], HN[:, :, :], ACT.Square, t)
                i4, b4, f4 = bbank.take()
                mm(BK[b4][:, 0:256], ONES[:, 0:128], HS[:, 0, :], True, False, t, f4)
                t = mm(BK[b4][:, 0:256], ONES[:, 0:128], HS[:, 1, :], False, True, sig=True)
                t = rsqrt(DN[:, :], BK[b4][:, 0:256], 256, DN[:, :], t, hn)
                bbank.give(i4, t)
                t = tt(HS[:, :, :], HN[:, :, :], bc(DN[:, :], 2), ALU.mult, t)
                for j in range(2):
                    c = prm + G_HEAD + 2 * h + j
                    t1 = stt(HN[:, j, :], HS[:, j, :], PRM[:, c:c + 1], OS[:, 2 * h + j, :],
                             ALU.mult, ALU.mult, t, tokv["os", 2 * h + j])
                q = slice(2 * h, 2 * h + 2)
                r = split(MHI[:, q, :], OSL[:, q, :], HN[:, :, :], t1, start_tok)
                tokv["m_hl", h] = r
                tokv["m_done"] = r[1]
                yield

            return evac, tokv, attention, mlstm, att_norm

        def run(g):
            for _ in g:
                pass

        def start_heads(l, tokv, attention):
            pass

        HBH = m("hbh", (KT, T), 28, F32R)
        HBL = m("hbl", (KT, T), 44, F32R)
        UR = [m(f"ur{i}", (T,), 60 + i) for i in range(2)]

        def first_layer(l, x_ready):
            t0 = stats(Xf, x_ready)
            want_mod((l, SCALE_A))
            want_mod((l, SHIFT_A))
            gs, sh, gg = (MOD[:, 6 * l + p_, :] for p_ in (SCALE_A, SHIFT_A, GATE_A))
            xt = to_h(gs, sh, [mod_ready[l, SCALE_A], mod_ready[l, SHIFT_A]], t0)
            start = fence()
            evac, tokv, attention, mlstm, att_norm = mixer(l, xt, start)
            tokv["att"] = None

            def all_attention():
                for pair in range(2):
                    for i in range(4):
                        yield from attention(pair, i)

            def first_evac(n, ps, t):
                if n == 12:
                    drain()
                r = evac(n, ps, t)
                if n == 11:
                    background.append(all_attention())
                return r

            gemm(37, lambda k: HH[:, k, :], lambda k: HL[:, k, :], lambda k: xt[k], first_evac)
            drain()
            for h in range(4):
                run(mlstm(h))
            att_norm()

            def xh(k):
                return MHI[:, k, :] if k < 8 else AHI[:, k - 8, :]

            def xl(k):
                return OSL[:, k, :] if k < 8 else QAL[:, k - 8, :]

            def xr(k):
                return tokv["m_hl", k // 2] if k < 8 else tokv["a_hl"]

            f = fence()
            yt = []

            def yevac(n, ps, t):
                r = fn(Y1[:, n, :], ps, ACT.Copy, t, f)
                yt.append(r)
                return r

            gemm(16, xh, xl, xr, yevac)
            gt = want_mod((l, GATE_A))
            t = add_y(Y1, gg, gt, yt[-1], fence())
            t0 = stats(Xf, t)
            want_mod((l, SCALE_M))
            want_mod((l, SHIFT_M))
            gs, sh, gg = (MOD[:, 6 * l + p_, :] for p_ in (SCALE_M, SHIFT_M, GATE_M))
            xt = to_h(gs, sh, [mod_ready[l, SCALE_M], mod_ready[l, SHIFT_M]], t0)
            f = fence()
            ht = {}
            ur = Slots(UR)
            yprev = [None] * KT
            pe_done = [f]

            def up_evac(n, ps, t):
                i, u, free = ur.take()
                r = fn(u[:, :], ps, ACT.Relu, t, free, pe_done[0])
                t1 = tt(u[:, :], u[:, :], u[:, :], ALU.mult, r)
                ht[n] = split(HBH[:, n, :], HBL[:, n, :], u[:, :], t1, pe_done[0])
                ur.give(i, *ht[n])
                return r

            def down_evac(n, ps, t):
                if yprev[n] is None:
                    yprev[n] = fn(Y1[:, n, :], ps, ACT.Copy, t, f)
                else:
                    yprev[n] = tt(Y1[:, n, :], ps, Y1[:, n, :], ALU.add, t, yprev[n])
                return yprev[n]

            for j in range(4):
                gemm(16, lambda k: HH[:, k, :], lambda k: HL[:, k, :], lambda k: xt[k], up_evac)
                h_now = dict(ht)
                t = gemm(16, lambda k: HBH[:, k, :], lambda k: HBL[:, k, :], lambda k: h_now[k], down_evac)
                pe_done[0] = t
            gt = want_mod((l, GATE_M))
            return add_y(Y1, gg, gt, [v for v in yprev], fence())

        xt_ = x_tok
        for l in range(2):
            xt_ = first_layer(l, xt_)
        drain()

        H = at("Hst", (128, 2, 64), A0)
        U = m("u", (KT, T), 32)
        Z = m("z", (KT, T), 48)
        CB = m("cb", (64, 2, 32), 64)
        BS = [m(f"bs{i}", (2, 128), 80 + i) for i in range(3)]
        TAB = m("tab", (2, 2, 64), 83)
        PR = m("pr", (2, 2, 64), 84)
        SS = m("ss", (2, 64), 85)
        AP_ = m("ap", (12, 64), 86)
        CR = at("cr", (2, 64, 16), A0)
        CT = at("ct", (2, 64, 16), A0 + 8 * kb)
        C2 = at("c2", (64, 16), A0 + 16 * kb)
        ZE = [m(f"ze{i}", (T,), 90 + i) for i in range(2)]

        f0 = fence()
        ap_tok = act.dma(lambda e: e.dma_start(AP_[:, 0:3, :], d["s5_ap"]), s_tab, 32, f0)
        t0 = stats(Xf, xt_, f0)
        xt = to_h(PRM[:, S5_PRE:S5_PRE + 16], None, None, t0)
        f = fence()
        uz = {}
        ze = Slots(ZE)

        def uz_evac(n, ps, t):
            if n < 16:
                uz[n] = fn(U[:, n, :], ps, ACT.Copy, t, f)
                return uz[n]
            i, e_, free = ze.take()
            r = fn(e_[:, :], ps, ACT.Exp, t, free, f, scale=-1.0)
            t1 = sigmoid_of(e_[:, :], e_[:, :], r)
            uz[n] = tt(Z[:, n - 16, :], ps, e_[:, :], ALU.mult, t1)
            ze.give(i, uz[n])
            return uz[n]

        a_re, a_im, ldt, dt_, mag, th, sn, cs, arr, t8, t9, t10 = (AP_[:, i, :] for i in range(12))
        uz_pe = gemm(32, lambda k: HH[:, k, :], lambda k: HL[:, k, :], lambda k: xt[k], uz_evac)

        t = fn(dt_, ldt, ACT.Exp, ap_tok)
        t = tt(mag, a_re, dt_, ALU.mult, t)
        t = fn(mag, mag, ACT.Exp, t)
        mag_t = t
        t = tt(th, a_im, dt_, ALU.mult, dve.last())
        TWO_PI = 2.0 * np.pi
        C1 = float(np.float32(6.28125))
        C2_ = float(np.float32(TWO_PI - 6.28125))
        C3_ = float(TWO_PI - C1 - C2_)
        MAGIC = float(1.5 * 2 ** 23)

        def reduced(dst, src, add, *waits):
            t = ts(t8, src, add, 1.0 / TWO_PI, ALU.add, ALU.mult, *waits)
            t = ts(t8, t8, MAGIC, None, ALU.add, None, t)
            t = ts(t8, t8, -MAGIC, None, ALU.add, None, t)
            t = stt(dst, t8, -C1, src, ALU.mult, ALU.add, t)
            t = stt(dst, t8, -C2_, dst, ALU.mult, ALU.add, t)
            t = stt(dst, t8, -C3_, dst, ALU.mult, ALU.add, t)
            t = ts(dst, dst, add, float(np.float32(np.pi) - np.float32(2e-7)), ALU.add, ALU.min, t)
            return ts(dst, dst, -float(np.float32(np.pi) - np.float32(2e-7)), None, ALU.max, None, t)

        t = reduced(sn, th, 0.0, t)
        t = reduced(cs, th, float(np.pi / 2), t)
        t = fn(sn, sn, ACT.Sin, t)
        t = fn(cs, cs, ACT.Sin, t)
        t = tt(cs, cs, mag, ALU.mult, t, mag_t)
        t = tt(sn, sn, mag, ALU.mult, t)
        for ri in range(2):
            cp(TAB[:, 0, ri, :], cs, t)
        cp(TAB[:, 1, 0, :], sn)
        ts(TAB[:, 1, 1, :], sn, -1.0, None, ALU.mult, None)
        t = ts(arr, cs, -1.0, None, ALU.add, None, t)
        t = tt(t8, a_re, a_re, ALU.mult, t)
        t = tt(t9, a_im, a_im, ALU.mult, t)
        t = tt(t8, t8, t9, ALU.add, t)
        t = rec(t8, t8, t)
        t = tt(t9, arr, a_re, ALU.mult, t)
        t = tt(t10, sn, a_im, ALU.mult, t)
        t = tt(t9, t9, t10, ALU.add, t)
        t = tt(t9, t9, t8, ALU.mult, t)
        t = tt(t10, sn, a_re, ALU.mult, t)
        t = tt(arr, arr, a_im, ALU.mult, t)
        t = tt(t10, t10, arr, ALU.subtract, t)
        t = tt(t10, t10, t8, ALU.mult, t)
        c_tok = act.dma(lambda e: e.dma_start(CR[:, :, :, :], d["s5_c"]), s_tab, 48, uz_pe)

        def over_c(ap):
            return ap.rearrange("p (g c) -> p g c", c=1).to_broadcast([P, 64, 16])

        t = dve.put(lambda e: e.memset(CB[:, :, :, :], 0.0), t)
        cre, cim = CR[:, 0, :, :], CR[:, 1, :, :]
        t = tt(CT[:, 0, :, :], cre, over_c(t9), ALU.mult, t, c_tok)
        t = tt(C2[:, :, :], cim, over_c(t10), ALU.mult, t)
        t = tt(CT[:, 0, :, :], CT[:, 0, :, :], C2[:, :, :], ALU.subtract, t)
        t = tt(CT[:, 1, :, :], cre, over_c(t10), ALU.mult, t)
        t = tt(C2[:, :, :], cim, over_c(t9), ALU.mult, t)
        t = stt(CT[:, 1, :, :].rearrange("p g c -> p (g c)"), CT[:, 1, :, :].rearrange("p g c -> p (g c)"), -1.0,
                C2[:, :, :].rearrange("p g c -> p (g c)"), ALU.mult, ALU.subtract, t)
        for gh in range(2):
            for ri in range(2):
                ct_tok = cp(CB[64 * gh:64 * gh + 64, :, ri, 16 * gh:16 * gh + 16],
                            CT[64 * gh:64 * gh + 64, ri, :, :], t)

        bs = Slots([0, 1, 2])
        bn = [0, 0, 0]
        h_free = [ct_tok]
        scan_done = None
        y_tok = None
        for ch in range(2):
            tc = slice(128 * ch, 128 * ch + 128)
            xs = []
            for q in range(16):
                i, b_, free = bs.take()
                bn[b_] += 16
                bt = sp.dma(lambda e, q=q, b_=b_: e.dma_start(BS[b_][:, :, :], d["s5_b"][q]),
                            s_b[b_], bn[b_], free, f0)
                last = None
                for w in range(4):
                    rows = slice(32 * w, 32 * w + 32)
                    gt = 4 * q + w
                    gi_, bk, fr = bbank.take()
                    mm(BK[bk][:, 0:128], BS[b_][rows, 0, :], U[rows, q, tc], True, True, bt, fr, uz[q], h_free)
                    last = mm(BK[bk][:, 128:256], BS[b_][rows, 1, :], U[rows, q, tc], True, True, sig=True)
                    e_ = fn(H[:, :, :, gt].rearrange("p t r -> p r t"),
                            BK[bk][:, 0:256].rearrange("p (r t) -> p r t", r=2), ACT.Copy, last, h_free)
                    bbank.give(gi_, e_)
                bs.give(i, last)
            t = act.last()
            for s in range(128):
                if ch == 0 and s == 0:
                    continue
                if s == 0:
                    src = HP
                else:
                    src = H[:, s - 1, :, :]
                t = tt(PR[:, :, :, :], TAB[:, :, :, :],
                       src.rearrange("p (a r) g -> p a r g", a=1).to_broadcast([P, 2, 2, 64]), ALU.mult, t,
                       dve.last())
                t = tt(SS[:, :, :], PR[:, 0, :, :], PR[:, 1, ::-1, :], ALU.add, t)
                t = tt(H[:, s, :, :], H[:, s, :, :], SS[:, :, :], ALU.add, t)
            if ch == 0:
                HP = m("hp", (2, 64), 89)[:, :, :]
                t = cp(HP, H[:, 127, :, :], t)
            for q in range(16):
                gi_, bk, fr = bbank.take()
                for w in range(4):
                    rows = slice(32 * w, 32 * w + 32)
                    gt = 4 * q + w
                    for ri in range(2):
                        last = mm(BK[bk][rows, 0:128], CB[:, gt, ri, :], H[:, :, ri, gt], ri == 0, ri == 1,
                                  t, fr, ct_tok, sig=ri == 1)
                y_tok = stt(U[:, q, tc], U[:, q, tc], PRM[:, S5_D + q:S5_D + q + 1], BK[bk][:, 0:128],
                            ALU.mult, ALU.add, last)
                bbank.give(gi_, y_tok)
            h_free = [pe.last()]

        yt = []
        ff = fence()
        for c in range(4):
            q = slice(4 * c, 4 * c + 4)
            t = fn(U[:, q, :], U[:, q, :], ACT.Gelu_apprx_tanh, ff)
            yt += [split(HH[:, q, :], HL[:, q, :], U[:, q, :], t, ff)] * 4
        GOH = m("goh", (KT, T), 64, F32R)
        GOL = m("gol", (KT, T), 0, F32R)
        Y2 = m("y2", (KT, T), 16)
        NB = m("nb", (16,), 80)
        nb = ts(NB[:, :], PRM[:, S5_BGLU:S5_BGLU + 16], -1.0, None, ALU.mult, None, ff)
        ff = fence()
        go = {}
        ZF = [m(f"zf{i}", (T,), 90 + i) for i in range(2)]
        ze = Slots(ZF)

        def glu_evac(n, ps, t):
            i, e_, free = ze.take()
            r = fn(e_[:, :], ps, ACT.Exp, t, free, ff, nb, scale=-1.0, bias=NB[:, n:n + 1])
            t1 = sigmoid_of(e_[:, :], e_[:, :], r)
            t1 = tt(e_[:, :], e_[:, :], U[:, n, :], ALU.mult, t1)
            t1 = tt(e_[:, :], e_[:, :], Z[:, n, :], ALU.mult, t1)
            go[n] = split(GOH[:, n, :], GOL[:, n, :], e_[:, :], t1, ff)
            ze.give(i, *go[n])
            return r

        gemm(16, lambda k: HH[:, k, :], lambda k: HL[:, k, :], lambda k: yt[k], glu_evac)
        y2t = []

        def y2_evac(n, ps, t):
            y2t.append(fn(Y2[:, n, :], ps, ACT.Copy, t, ff))
            return y2t[-1]

        gemm(16, lambda k: GOH[:, k, :], lambda k: GOL[:, k, :], lambda k: go[k], y2_evac)
        t = add_y(Y2, PRM[:, S5_POST:S5_POST + 16], None, y2t[-1], fence())

        KF = m("kf", (KT, T), 0)
        VF = m("vf", (2, D), 16)
        QF = m("qf", (KT, T), 32)
        ZZ = m("zz", (KT, T), 48)
        FOL = m("fol", (KT, T), 48, F32R)
        FOH = m("foh", (KT, T), 64, F32R)
        FV = [m(f"fv{i}", (T,), 80 + i) for i in range(2)]
        FE = [m(f"fe{i}", (T,), 82 + i) for i in range(2)]
        CG = m("cg", (T,), 84)
        CN = m("cn", (T,), 85)
        TF = [m(f"tf{i}", (384,), 86 + 1.5 * i) for i in range(2)]
        PF = [m(f"pf{i}", (384,), 89 + 1.5 * i) for i in range(2)]
        XF = SM[:, 64:80]
        Y3 = m("y3", (KT, T), 0)

        t0 = stats(Xf, t, fence())
        xt = to_h(PRM[:, KV_G:KV_G + 16], None, None, t0)
        f = fence()
        kv = {}

        def kv_evac(n, ps, t):
            if n == 0:
                r = cp(CG[0:16, :], ps[0:16, :], t, f)
                t1 = ts(CG[0:16, :], CG[0:16, :], PRM[0:16, KV_BF:KV_BF + 1], None, ALU.add, None, r)
                t1 = fn(CN[0:16, :], CG[0:16, :], ACT.Abs, t1)
                t1 = fn(CN[0:16, :], CN[0:16, :], ACT.Exp, t1, scale=-1.0)
                t1 = fn(CN[0:16, :], CN[0:16, :], ACT.Ln, t1, bias=1.0)
                t1 = stt(CG[0:16, :], CG[0:16, :], 0.0, CN[0:16, :], ALU.min, ALU.subtract, t1)
                t1 = dve.put(lambda e: e.tensor_tensor_scan(CN[0:16, :], ONES[0:16, :], CG[0:16, :], 0.0,
                                                            ALU.mult, ALU.add), t1)
                kv["c"] = ts(CN[0:16, :], CN[0:16, :], -(128.0 ** 0.5), None, ALU.mult, None, t1)
                return r
            n -= 1
            if n < 16:
                kv["k", n] = fn(KF[:, n, :], ps, ACT.Copy, t, f)
                return kv["k", n]
            n -= 16
            s = n % 2
            r = fn(FV[s][:, :], ps, ACT.Copy, t, kv.get(("fv", s)), f)
            kv["fv", s] = kv["v", n] = transposed(VF[:, :, 128 * n:128 * n + 128], FV[s], r)
            return r

        kv_pe = gemm(33, lambda k: HH[:, k, :], lambda k: HL[:, k, :], lambda k: xt[k], kv_evac)
        SQ2 = SQ
        xt = to_h(PRM[:, FOX_PRE:FOX_PRE + 16], None, None, kv_pe, fence())
        f = fence()
        fe = Slots(FE)

        def fox(h):
            scale = 128.0 ** -0.5
            wait = [kv["k", h], kv["q", h], kv["c"], kv["v", h]]
            s = h % 2
            tf, pf = TF[s], PF[s]
            x4 = XF[:, 4 * s:4 * s + 4]
            i, b, free = bbank.take()
            row = ident[0:16, h:h + 1].to_broadcast([16, 128])
            mm(BK[b][:, 0:256], QF[:, h, 128:256], KF[:, h, :], True, False, *wait, free)
            mm(BK[b][:, 0:256], row, CN[0:16, :], False, True)
            mm(BK[b][:, 256:384], QF[:, h, 0:128], KF[:, h, 0:128], True, False)
            t = mm(BK[b][:, 256:384], row, CN[0:16, 0:128], False, True, sig=True)
            prev = kv.get(("fox", s))
            mk = CST[:, MASKF:MASKF + 384]
            t = tt(tf[:, :], BK[b][:, 0:384], mk, ALU.add, t, prev, f)
            bbank.give(i, t)
            t = dve.put(lambda e: e.tensor_reduce(x4[:, 0:1], tf[:, 0:256], AX.X, ALU.max), t)
            t = dve.put(lambda e: e.tensor_reduce(x4[:, 1:2], tf[:, 256:384], AX.X, ALU.max))
            t = ts(x4[:, 0:2], x4[:, 0:2], -scale, None, ALU.mult, None, t)
            yield
            for c, q in ((0, slice(0, 256)), (1, slice(256, 384))):
                t2 = fn(pf[:, q], tf[:, q], ACT.Exp, t, prev, scale=scale, bias=x4[:, c:c + 1],
                        accum_out=x4[:, 2 + c:3 + c])
            t = rec(x4[:, 2:4], x4[:, 2:4], t2)
            ts(pf[:, 0:256], pf[:, 0:256], x4[:, 2:3], None, ALU.mult, None, t)
            t = ts(pf[:, 256:384], pf[:, 256:384], x4[:, 3:4], None, ALU.mult, None)
            yield
            i, b, free = bbank.take()
            tr(BK[b][:, 0:128], pf[:, 256:384], t, free)
            tr(BK[b][:, 128:256], pf[:, 0:128])
            t = tr(BK[b][:, 256:384], pf[:, 128:256], sig=True)
            t = cp(tf[:, :], BK[b][:, 0:384], t)
            bbank.give(i, t)
            yield
            i, b, free = bbank.take()
            v = slice(128 * h, 128 * h + 128)
            mm(BK[b][:, 0:256], VF[:, 0, v], tf[:, 0:256], True, False, t, free)
            t = mm(BK[b][:, 128:256], VF[:, 1, v], tf[:, 256:384], False, True, sig=True)
            kv["o", h] = kv["fox", s] = cp(QF[:, h, :], BK[b][:, 0:256], t)
            bbank.give(i, kv["o", h])
            yield

        def qz_evac(n, ps, t):
            if n < 16:
                kv["q", n] = fn(QF[:, n, :], ps, ACT.Copy, t, f)
                background.append(fox(n))
                return kv["q", n]
            n -= 16
            i, e_, free = fe.take()
            r = fn(e_[:, :], ps, ACT.Exp, t, free, f, scale=-1.0)
            t1 = sigmoid_of(e_[:, :], e_[:, :], r)
            kv["z", n] = tt(ZZ[:, n, :], ps, e_[:, :], ALU.mult, t1)
            fe.give(i, kv["z", n])
            return kv["z", n]

        gemm(32, lambda k: HH[:, k, :], lambda k: HL[:, k, :], lambda k: xt[k], qz_evac, each=2)
        drain()
        ft = []
        for c in range(4):
            q = slice(4 * c, 4 * c + 4)
            t = tt(QF[:, q, :], QF[:, q, :], ZZ[:, q, :], ALU.mult, kv["o", 4 * c + 3], kv["z", 4 * c + 3])
            ft += [split(FOH[:, q, :], FOL[:, q, :], QF[:, q, :], t, f)] * 4
        ff = fence()
        y3t = []

        def y3_evac(n, ps, t):
            y3t.append(fn(Y3[:, n, :], ps, ACT.Copy, t, ff))
            return y3t[-1]

        gemm(16, lambda k: FOH[:, k, :], lambda k: FOL[:, k, :], lambda k: ft[k], y3_evac)
        t = add_y(Y3, PRM[:, FOX_POST:FOX_POST + 16], None, y3t[-1], fence())
        sp.dma(lambda e: e.dma_start(out, Xf), s_out, 16, t)
        sp.items.append(([(s_out, 16)], lambda e: e.wait_ge(s_out, 16), None, 0))

        with nc.Block() as block:
            @block.sync
            def _(e):
                sp.emit(e)

            @block.scalar
            def _(e):
                act.emit(e)

            @block.vector
            def _(e):
                dve.emit(e)

            @block.tensor
            def _(e):
                pe.emit(e)


def constants():
    cst = np.zeros((P, N_CST), np.float32)
    cst[:, IDENT:IDENT + 128] = np.eye(128, dtype=np.float32)
    r = np.arange(128)[:, None]
    u = np.arange(256)[None, :]
    dist = r + 128 - u
    nd = np.where((dist >= 0) & (dist < 128), -dist, BIG).astype(np.float32)
    cst[:, NDIST:NDIST + 256] = nd
    cst[:, NDIST + 256:NDIST + 384] = nd[:, 128:256]
    s = np.arange(128)[:, None]
    t = np.arange(128)[None, :]
    cst[:, MASKT:MASKT + 128] = np.where(s <= t, 0.0, BIG)
    tri = np.where(t <= s, 0.0, BIG).astype(np.float32)
    cst[:, MASKF + 128:MASKF + 256] = tri
    cst[:, MASKF + 256:MASKF + 384] = tri
    return cst


def head_columns():
    cols = []
    for pair in range(2):
        for i in range(4):
            for par in range(2):
                head = (2 * pair + par) * 4 + i
                cols += list(range(64 * head, 64 * head + 64))
    return np.array(cols)


def slab(w):
    k, n = w.shape
    a = w.reshape(k // D, KT, P, n // 128, 128).transpose(0, 3, 2, 1, 4)
    return np.ascontiguousarray(a).reshape(k // D * (n // 128), P, KT * 128)


def col(v):
    return v.reshape(-1, P).T


def layout(i):
    f = {}
    f["cst"] = constants()
    f["x"] = np.ascontiguousarray(i["x"][0].T.reshape(KT, P, T).transpose(1, 0, 2))
    f["w_ada"] = np.ascontiguousarray(
        i["w_ada"].reshape(2, 16, P, 6, 16, P).transpose(0, 3, 1, 2, 5, 4)).reshape(2, 6, 16, P, D)
    hc = head_columns()
    w_in = i["w_in"]
    gate = np.zeros((2, D, 128), np.float32)
    gate[:, :, 0:4] = w_in[:, :, 3072:3076]
    gate[:, :, 32:36] = w_in[:, :, 3076:3080]
    f["w_in"] = np.stack([slab(np.concatenate(
        [w_in[l][:, 3080 + hc], w_in[l][:, 4104:4360], w_in[l][:, 4360:4616], gate[l], w_in[l][:, 0:3072]],
        axis=1)) for l in range(2)])
    f["w_out"] = np.stack([slab(np.concatenate([i["w_out"][l][0:1024], i["w_out"][l][1024 + hc]]))
                           for l in range(2)])
    f["w_up"] = np.stack([slab(i["w_up"][l]) for l in range(2)])
    f["w_down"] = np.stack([slab(i["w_down"][l]) for l in range(2)])
    f["s5_w_in"] = slab(i["s5_w_in_2"][0])
    f["s5_w_glu"] = slab(i["s5_w_glu_2"][0])
    f["s5_w_out"] = slab(i["s5_w_out_2"][0])
    kv = i["kv_w_2"]
    pad = np.zeros((D, 128), np.float32)
    pad[:, 0:16] = kv[:, 4096:4112]
    f["kv_w"] = slab(np.concatenate([pad, kv[:, 0:4096]], axis=1))
    f["fox_w_in"] = slab(i["fox_w_in_2"][0])
    f["fox_w_out"] = slab(i["fox_w_out_2"][0])
    prm = np.zeros((P, N_PRM), np.float32)
    for l in range(2):
        b = PER_LAYER * l
        for off, name in ((PRE_MIX, "g_pre_mix"), (POST_MIX, "g_post_mix"), (PRE_MLP, "g_pre_mlp"),
                          (POST_MLP, "g_post_mlp")):
            prm[:, b + off:b + off + 16] = col(i[name][l])
        prm[:, b + B_ADA:b + B_ADA + 96] = col(i["b_ada"][l])
        prm[:, b + CONV_W:b + CONV_W + 32] = i["conv_w"][l].reshape(4, 8, P).transpose(2, 1, 0).reshape(P, 32)
        prm[:, b + CONV_B:b + CONV_B + 8] = col(i["conv_b"][l])
        prm[:, b + G_HEAD:b + G_HEAD + 8] = col(i["g_mlstm_head"][l].reshape(-1))
        prm[:, b + G_ATT:b + G_ATT + 8] = col(i["g_attn_out"][l][hc])
        prm[:, b + SINK:b + SINK + 16] = i["attn_sinks"][l][None, :]
        prm[0:4, b + GATE_B] = i["b_i"][l]
        prm[0:4, b + GATE_B + 1] = i["b_f"][l]
    for off, v in ((S5_PRE, i["norm_pre_2"][0]), (S5_POST, i["norm_post_2"][0]), (S5_D, i["s5_d_2"][0]),
                   (S5_BGLU, i["s5_b_glu_2"][0]), (KV_G, i["kv_norm_2"]), (FOX_PRE, i["norm_pre_2"][1]),
                   (FOX_POST, i["norm_post_2"][1]), (C_COL, i["c"][0])):
        prm[:, off:off + 16] = col(v)
    prm[0:16, KV_BF] = i["kv_b_f_2"]
    f["prm"] = prm

    def states(a):
        return a.reshape(64, 2, 64).transpose(1, 2, 0).reshape(P, 64)

    f["s5_ap"] = np.ascontiguousarray(np.stack(
        [states(i["s5_a_re_2"][0]), states(i["s5_a_im_2"][0]),
         states(np.broadcast_to(i["s5_log_dt_2"][0][:, None], (128, 64)))], axis=1))
    sc = []
    for name in ("s5_c_re_2", "s5_c_im_2"):
        c = i[name][0].reshape(64, 2, 16, 64).transpose(1, 3, 0, 2)
        sc.append(c.reshape(P, 64, 16))
    f["s5_c"] = np.ascontiguousarray(np.stack(sc, axis=1))
    sb = np.zeros((64, 2, 16, 2, 2, 64), np.float32)
    for ri, name in enumerate(("s5_b_re_2", "s5_b_im_2")):
        b = i[name][0].reshape(64, 2, 64, 16)
        for gh in range(2):
            sb[:, gh, :, ri, gh, :] = b[:, gh].transpose(0, 2, 1)
    f["s5_b"] = sb.reshape(16, P, 2, 128)
    return {k: np.ascontiguousarray(v, dtype=np.float32) for k, v in f.items()}


def kernel(**inputs):
    import concourse.bacc as _bacc
    from concourse.bass_utils import run_bass_kernel_spmd as _run

    arrays = layout({k: np.asarray(v) for k, v in inputs.items()})
    nc = _bacc.Bacc("TRN2", target_bir_lowering=False, num_devices=1, dynamic_dma_scratch_size=1024)
    d = {k: nc.dram_tensor(f"in_{k}", v.shape, F32, kind="ExternalInput").ap() for k, v in arrays.items()}
    out = nc.dram_tensor("out_x", (P, KT, T), F32, kind="ExternalOutput").ap()
    build(nc, d, out)
    r = _run(nc, [{f"in_{k}": v for k, v in arrays.items()}], core_ids=[0])
    got = r.results[0]["out_x"]
    return np.ascontiguousarray(np.asarray(got).transpose(1, 0, 2).reshape(D, T).T)[None]
```

```python
import numpy as np
from contextlib import ExitStack

import concourse.bass as bass
from concourse import mybir

F32 = mybir.dt.float32
F32R = mybir.dt.float32r
ALU = mybir.AluOpType
ACT = mybir.ActivationFunctionType
AX = mybir.AxisListType

P = 128
T = 256
KT = 16
D = 2048
BIG = -1e30
RING = 5
EPS = 1e-6

PRE_MIX, POST_MIX, PRE_MLP, POST_MLP, B_ADA, CONV_W, CONV_B, G_HEAD, G_ATT, SINK, GATE_B = (
    0, 16, 32, 48, 64, 160, 192, 200, 208, 216, 232)
PER_LAYER = 234
S5_PRE, S5_POST, S5_D, S5_BGLU, KV_G, FOX_PRE, FOX_POST, C_COL, KV_BF = (
    2 * PER_LAYER + n for n in (0, 16, 32, 48, 64, 80, 96, 112, 128))
N_PRM = 2 * PER_LAYER + 129

IDENT, NDIST, MASKT, MASKF, N_CST = 0, 128, 512, 640, 1024


SLABS = ([("ka", 0), ("ka", 1), ("va", 0), ("va", 1), ("gate", 0)]
         + [s for h in range(4) for s in (("q", h), ("k", h), ("v", 2 * h), ("v", 2 * h + 1),
                                          ("qa", 2 * h), ("qa", 2 * h + 1))]
         + [("os", v) for v in range(8)])


class Lane:

    def __init__(self, sem):
        self.sem, self.n, self.items, self.seen = sem, 0, [], {}

    def need(self, waits):
        out = []
        for w in waits:
            if w is None:
                continue
            if isinstance(w, list):
                out += self.need(w)
            elif self.seen.get(id(w[0]), 0) < w[1]:
                self.seen[id(w[0])] = w[1]
                out.append(w)
        return out

    def put(self, fn, *waits, sig=True):
        w = self.need(waits)
        if sig:
            self.n += 1
        self.items.append((w, fn, self.sem if sig else None, 1))
        return (self.sem, self.n)

    def dma(self, fn, sem, value, *waits):
        self.items.append((self.need(waits), fn, sem, 16))
        return (sem, value)

    def last(self):
        return (self.sem, self.n) if self.n else None

    def emit(self, eng):
        for waits, fn, sem, by in self.items:
            for s, v in waits:
                eng.wait_ge(s, v)
            ins = fn(eng)
            if sem is not None:
                ins.then_inc(sem, by)


class Slots:

    def __init__(self, items):
        self.items, self.free, self.order = items, [[] for _ in items], list(range(len(items)))

    def ready(self, n=1):
        return len(self.order) >= n

    def take(self):
        i = self.order.pop(0)
        return i, self.items[i], self.free[i]

    def give(self, i, *tokens):
        self.free[i] = list(tokens)
        self.order.append(i)


def build(nc, d, out):
    ctx = ExitStack()
    with ctx:
        base = (nc.sbuf_base + 63) // 64 * 64
        top = nc.sbuf_usable_end
        kb = 1024

        def at(name, shape, off, dt=F32):
            return nc.alloc_sbuf_tensor_at(name, (P, *shape), dt, offset=off)

        def psum(name):
            return ctx.enter_context(nc.psum_tensor(name, [P, 512], F32))

        def sem(name):
            return ctx.enter_context(nc.semaphore(name))

        o = base
        X = at("X", (KT, T), o); o += 16 * kb
        RAW = [at(f"raw{i}", (KT, 128), o + 8 * kb * i) for i in range(RING)]; o += 8 * kb * RING
        WH = [at(f"wh{i}", (KT, 128), o + 8 * kb * i, F32R) for i in range(2)]; o += 16 * kb
        WL = [at(f"wl{i}", (KT, 128), o + 8 * kb * i, F32R) for i in range(2)]; o += 16 * kb
        CST = at("cst", (N_CST,), o); o += 4 * N_CST
        PRM = at("prm", (N_PRM,), o); o += (4 * N_PRM + 63) // 64 * 64
        MOD = at("mod", (12, 16), o); o += 768
        ONES = at("ones", (256,), o); o += 1024
        SM = at("sm", (96,), o); o += 384
        RS = at("rs", (T,), o); o += 1024
        LN = at("ln", (T,), o); o += 1024
        A0 = o
        HH = at("HH", (KT, T), A0, F32R)
        HL = at("HL", (KT, T), A0 + 16 * kb, F32R)
        M = A0 + 32 * kb
        assert M + 92 * kb <= top, (M + 92 * kb, top)

        def m(name, shape, off, dt=F32):
            return at(name, shape, int(M + off * kb), dt)

        BK = [psum(f"bk{i}") for i in range(8)]
        ident = CST[:, IDENT:IDENT + 128]

        pe, act, dve, sp = (Lane(sem(f"s_{n}")) for n in ("pe", "act", "dve", "sp"))
        s_raw = [sem(f"s_raw{i}") for i in range(RING)]
        s_cst, s_prm, s_tab, s_out = (sem(f"s_{n}") for n in ("cst", "prm", "tab", "out"))
        s_row = [sem(f"s_row{i}") for i in range(2)]
        s_b = [sem(f"s_b{i}") for i in range(3)]
        s_bt = [sem(f"s_bt{i}") for i in range(2)]
        gbank = Slots([0, 1, 2])
        bbank = Slots([3, 4, 5, 6, 7])

        def mm(out_, l, r, start, stop, *waits, sig=False):
            return pe.put(lambda e: e.matmul(out_, l, r, start=start, stop=stop, skip_group_check=True),
                          *waits, sig=sig)

        def tr(out_, in_, *waits, sig=False):
            n = in_.shape[0]
            return pe.put(lambda e: e.transpose(out_, in_, ident[0:n, 0:n]), *waits, sig=sig)

        def fn(out_, in_, f, *waits, **kw):
            return act.put(lambda e: e.activation(out_, in_, f, **kw), *waits)

        def tt(out_, a, b, op, *waits):
            return dve.put(lambda e: e.tensor_tensor(out_, a, b, op), *waits)

        def ts(out_, a, s1, s2, op0, op1, *waits):
            if op1 is None:
                return dve.put(lambda e: e.tensor_scalar(out_, a, s1, None, op0), *waits)
            return dve.put(lambda e: e.tensor_scalar(out_, a, s1, s2, op0, op1), *waits)

        def stt(out_, a, s, b, op0, op1, *waits):
            return dve.put(lambda e: e.scalar_tensor_tensor(out_, a, s, b, op0, op1), *waits)

        def cp(out_, in_, *waits):
            return dve.put(lambda e: e.tensor_copy(out_, in_), *waits)

        def rec(out_, in_, *waits):
            return dve.put(lambda e: e.reciprocal(out_, in_), *waits)

        def bc(ap, n):
            return ap.rearrange("p (a t) -> p a t", a=1).to_broadcast([ap.shape[0], n, ap.shape[1]])

        def fence():
            return [t for t in (pe.last(), act.last(), dve.last()) if t]

        stream = []

        def ada(l, piece):
            return [("ada", d["w_ada"][l, piece, k], (l, piece, k)) for k in range(16)]

        def slabs(w, idx):
            return [("w", w[i], None) for i in idx]

        def blend(a, b):
            out_, n = [], 0
            for i, s in enumerate(a):
                out_.append(s)
                while n < len(b) and (n + 1) * len(a) <= (i + 1) * len(b):
                    out_.append(b[n])
                    n += 1
            return out_ + b[n:]

        SHIFT_A, SCALE_A, GATE_A, SHIFT_M, SCALE_M, GATE_M = range(6)
        stream += ada(0, SCALE_A) + ada(0, SHIFT_A)
        mlp_order = [n for j in range(4) for n in [("u", 16 * j + i) for i in range(16)]
                     + [("d", 16 * j + i) for i in range(16)]]
        for l in range(2):
            stream += blend(slabs(d["w_in"][l], range(37)), ada(l, GATE_A) * (l == 0) + ada(l, SCALE_M))
            stream += blend(slabs(d["w_out"][l], range(16)), ada(l, SHIFT_M))
            up_down = [("w", d["w_up" if k == "u" else "w_down"][l, i], None) for k, i in mlp_order]
            stream += blend(up_down, ada(l, GATE_M) + (ada(1, SCALE_A) + ada(1, SHIFT_A) + ada(1, GATE_A) if l == 0 else []))
        stream += slabs(d["s5_w_in"], range(32))
        stream += slabs(d["s5_w_glu"], range(16))
        stream += slabs(d["s5_w_out"], range(16))
        stream += slabs(d["kv_w"], range(33))
        stream += slabs(d["fox_w_in"], range(32))
        stream += slabs(d["fox_w_out"], range(16))

        raw_free = [[] for _ in range(RING)]
        loaded, staged_at = [0], [0]
        wslots = Slots([0, 1])
        ready = []
        tasks = {"tr": [], "ada": [], "att": [], "mix": []}
        WIDTH = {"tr": 4, "ada": 1, "att": 2, "mix": 1}
        later = set()

        def load_next():
            n = loaded[0]
            if n >= len(stream):
                return
            loaded[0] += 1
            s = n % RING
            dst = RAW[s][:, :, :].rearrange("p a b -> p (a b)")
            sp.dma(lambda e, dst=dst, src=stream[n][1]: e.dma_start(dst, src), s_raw[s],
                   16 * (n // RING + 1), raw_free[s])

        ACC = m("acc", (D,), 80)
        ROW = m("row", (2, 512), 88)
        acc_tok, acc_read, acc_gen = [None], [True], [None]
        row_n = [0, 0]
        row_free = [None, None]
        mod_ready = {}

        def grab(n=1):
            while not bbank.ready(n):
                yield
            return [bbank.take() for _ in range(n)]

        def finish_ada(l, piece, tok):
            toks = []
            yield True
            for c in range(4):
                (i, b, free), = yield from grab()
                r_ = c % 2
                t = mm(BK[b][0:1, :], ONES[:, 0:1], ACC[:, 512 * c:512 * c + 512], True, True,
                       tok, free, ones_tok, sig=True)
                acc_tok[0] = t
                acc_read[0] = c == 3
                yield
                last = fn(ROW[0:1, r_, :], BK[b][0:1, :], ACT.Copy, t, row_free[r_])
                bbank.give(i, last)
                row_n[r_] += 1
                dst = MOD[32 * c:32 * c + 32, 6 * l + piece, :]
                src = ROW[0:1, r_, :].rearrange("o (p k) -> o p k", k=16)
                t = act.dma(lambda e, dst=dst, src=src: e.dma_start(dst, src), s_row[r_], 16 * row_n[r_], last)
                row_free[r_] = t
                toks.append(t)
            yield
            yield
            col = MOD[:, 6 * l + piece, :]
            b0 = PER_LAYER * l + B_ADA + 16 * piece
            t = tt(col, col, PRM[:, b0:b0 + 16], ALU.add, toks, prm_tok)
            if piece in (SCALE_A, SCALE_M):
                g = PER_LAYER * l + (PRE_MIX if piece == SCALE_A else PRE_MLP)
                t = stt(col, col, 1.0, PRM[:, g:g + 16], ALU.add, ALU.mult, t)
            if piece in (GATE_A, GATE_M):
                g = PER_LAYER * l + (POST_MIX if piece == GATE_A else POST_MLP)
                t = tt(col, col, PRM[:, g:g + 16], ALU.mult, t)
            mod_ready[(l, piece)] = t

        def stage_next():
            n = staged_at[0]
            if n >= len(stream):
                return
            staged_at[0] += 1
            kind, _, key = stream[n]
            s = n % RING
            here = (s_raw[s], 16 * (n // RING + 1))
            if kind == "ada":
                l, piece, k = key
                raw = RAW[s][:, :, :].rearrange("p a b -> p (a b)")
                if k == 0:
                    while not acc_read[0]:
                        pump()
                    t = ts(ACC[:, :], raw, CA[:, 0:1], None, ALU.mult, None, here, ca_tok, acc_tok[0])
                else:
                    t = stt(ACC[:, :], raw, CA[:, k:k + 1], ACC[:, :], ALU.mult, ALU.add, here, dve.last())
                raw_free[s] = [t]
                if k == 15:
                    acc_read[0] = False
                    acc_gen[0] = finish_ada(l, piece, t)
                    tasks["ada"].append(acc_gen[0])
            else:
                i, w, free = wslots.take()
                th = fn(WH[w][:, :, :], RAW[s][:, :, :], ACT.Copy, here, free)
                tl = tt(WL[w][:, :, :], RAW[s][:, :, :], WH[w][:, :, :].bitcast(F32), ALU.subtract, here, th, free)
                raw_free[s] = [th, tl]
                ready.append((i, w, [th, tl]))
            load_next()

        def pump(n=1):
            for r in range(n):
                for kind in tasks:
                    for g in tasks[kind][:WIDTH[kind]]:
                        if r and g in later:
                            continue
                        later.discard(g)
                        try:
                            if next(g):
                                later.add(g)
                        except StopIteration:
                            tasks[kind].remove(g)

        def idle():
            return not any(tasks.values())

        def drain():
            while not idle():
                pump()

        def bank():
            while not bbank.ready():
                pump()
            return bbank.take()

        def want_mod(key):
            while key not in mod_ready:
                if not idle():
                    pump()
                else:
                    stage_next()
            return mod_ready[key]

        def gemm(count, xh, xl, xready, evac, each=2, korder=None):
            order = korder or range(KT)
            pending = None
            for n in range(count):
                while not ready:
                    stage_next()
                i, w, wt = ready.pop(0)
                g, b, free = gbank.take()
                ps = BK[b][:, 0:T]
                for q, k in enumerate(order):
                    wh, wl = WH[w][:, k, :], WL[w][:, k, :]
                    mm(ps, wh, xh(k), q == 0, False, wt[0], free, xready(k))
                    mm(ps, wh, xl(k), False, False)
                    t = mm(ps, wl, xh(k), False, q == KT - 1, wt[1], sig=q == KT - 1)
                wslots.give(i, t)
                while not ready and staged_at[0] < len(stream):
                    stage_next()
                if pending:
                    gbank.give(pending[0], evac(*pending[1:]))
                pending = (g, n, ps, t)
                pump(each)
            gbank.give(pending[0], evac(*pending[1:]))
            return t

        Xf = X[:, :, :]
        cst_tok = sp.dma(lambda e: e.dma_start(CST[:, :], d["cst"]), s_cst, 16)
        prm_tok = sp.dma(lambda e: e.dma_start(PRM[:, :], d["prm"]), s_prm, 16)
        for _ in range(RING):
            load_next()
        x_tok = act.dma(lambda e: e.dma_start(Xf, d["x"]), s_tab, 16)
        ones_tok = dve.put(lambda e: e.memset(ONES[:, :], 1.0))
        pe.need([cst_tok, ones_tok])
        pe.items.append(([cst_tok, ones_tok], lambda e: e.wait_ge(s_cst, 16), None, 0))

        CA, CE = SM[:, 16:32], SM[:, 32:48]
        ccol = PRM[:, C_COL:C_COL + 16]
        t = fn(CE, ccol, ACT.Exp, prm_tok, scale=-1.0)
        t = ts(CE, CE, 1.0, None, ALU.add, None, t)
        t = rec(CE, CE, t)
        ca_tok = tt(CA, CE, ccol, ALU.mult, t, prm_tok)

        SQ = m("sq", (KT, T), 60)

        def stats(*waits):
            i, b, free = bank()
            for k in range(KT):
                t = fn(SQ[:, k, :], X[:, k, :], ACT.Square, *waits)
                t = mm(BK[b][:, 0:T], ONES[:, 0:128], SQ[:, k, :], k == 0, k == KT - 1, t, free, sig=k == KT - 1)
            t = rsqrt(RS[:, :], BK[b][:, 0:T], D, LN[:, :], t)
            bbank.give(i, act.last())
            return t

        def rsqrt(out_, in_, n, tmp, *waits):
            t = fn(tmp, in_, ACT.Ln, *waits, scale=1.0 / n, bias=EPSC[:, :])
            return fn(out_, tmp, ACT.Exp, t, scale=-0.5)

        EPSC = SM[:, 0:1]
        eps_tok = dve.put(lambda e: e.memset(EPSC, EPS))
        act.items.append((act.need([eps_tok]), lambda e: e.wait_ge(dve.sem, eps_tok[1]), None, 0))

        def scaled(gs, *waits):
            return [stt(SQ[:, k, :], X[:, k, :], gs[:, k:k + 1], RS[:, :], ALU.mult, ALU.mult, *waits)
                    for k in range(KT)]

        def to_h(gs, sh, ts_, *waits, early=None):
            toks, hi = [], {}
            for k in range(KT + 2):
                if k < KT:
                    t = early[k] if early else stt(SQ[:, k, :], X[:, k, :], gs[:, k:k + 1], RS[:, :],
                                                   ALU.mult, ALU.mult, ts_, *waits)
                    if sh is None:
                        hi[k] = fn(HH[:, k, :], SQ[:, k, :], ACT.Copy, t, *waits)
                    else:
                        hi[k] = fn(HH[:, k, :], SQ[:, k, :], ACT.Identity, t, *waits, bias=sh[:, k:k + 1])
                if k >= 2:
                    j = k - 2
                    hf = HH[:, j, :].bitcast(F32)
                    if sh is None:
                        t = tt(HL[:, j, :], SQ[:, j, :], hf, ALU.subtract, hi[j])
                    else:
                        t = stt(HL[:, j, :], SQ[:, j, :], sh[:, j:j + 1], hf, ALU.add, ALU.subtract, hi[j])
                    toks.append([hi[j], t])
            return toks

        class Squares:

            def __init__(self, off, name, *waits):
                self.t = [m(f"{name}{i}", (T,), off + i) for i in range(3)]
                self.n, self.tok, self.waits = 0, None, list(waits)

            def add(self, src, *waits):
                s = self.t[0] if self.n == 0 else self.t[1 + self.n % 2]
                prev = self.tok[1] if self.n > 2 else None
                t = fn(s[:, :], src, ACT.Square, *waits, prev, self.waits)
                if self.n:
                    u = tt(self.t[0][:, :], self.t[0][:, :], s[:, :], ALU.add, t, self.tok[0])
                    self.tok = [u, self.tok[0]]
                else:
                    self.tok = [t, None]
                self.n += 1
                return t

        def add_y(Y, gg, gtok, sq, *waits, norm=True):
            i, b, free = bank()
            t = mm(BK[b][:, 0:T], ONES[:, 0:128], sq.t[0][:, :], True, True, sq.tok[0], free, sig=True)
            t0 = rsqrt(RS[:, :], BK[b][:, 0:T], D, LN[:, :], t, *waits)
            bbank.give(i, t0)
            i, b, free = bank()
            st, xs = [], []
            for k in range(KT + 1):
                if k < KT:
                    st.append(stt(SQ[:, k, :], Y[:, k, :], gg[:, k:k + 1], RS[:, :], ALU.mult, ALU.mult,
                                  t0, gtok, *waits))
                if k:
                    j = k - 1
                    t = tt(X[:, j, :], SQ[:, j, :], X[:, j, :], ALU.add, st[j])
                    xs.append(t)
                    if norm:
                        t = fn(SQ[:, j, :], X[:, j, :], ACT.Square, t)
                        t = mm(BK[b][:, 0:T], ONES[:, 0:128], SQ[:, j, :], j == 0, j == KT - 1, t, free,
                               sig=j == KT - 1)
            if norm:
                t = rsqrt(RS[:, :], BK[b][:, 0:T], D, LN[:, :], t, st[-1])
            bbank.give(i, t)
            return xs, t

        def split(hi, lo, src, *waits):
            th = fn(hi, src, ACT.Copy, *waits)
            tl = tt(lo, src, hi.bitcast(F32), ALU.subtract, th, *waits)
            return [th, tl]

        QA = m("qa", (8, T), 0)
        QAL = m("qal", (8, T), 0, F32R)
        KA = m("ka", (2, T), 8)
        VA = m("va", (2, T), 10)
        QM = m("qm", (4, T), 12)
        KM = m("km", (4, T), 16)
        VM = m("vm", (2, 1024), 20)
        OS = m("os", (8, T), 28)
        OSL = m("osl", (8, T), 28, F32R)
        AHI = m("ahi", (8, T), 36, F32R)
        MHI = m("mhi", (8, T), 44, F32R)
        S0 = 52
        Y1 = m("y1", (KT, T), 12)
        CV = [m(f"cv{i}", (3 + T,), S0 + 1.125 * i) for i in range(2)]
        CO = [m(f"co{i}", (T,), S0 + 2.25 + i) for i in range(2)]
        TV = [m(f"tv{i}", (T,), S0 + 4.25 + i) for i in range(2)]
        EV = [m(f"ev{i}", (T,), S0 + 6.25 + i) for i in range(2)]
        GI = m("gi", (T,), S0 + 8.25)
        GF = m("gf", (T,), S0 + 9.25)
        GT = m("gt", (T,), S0 + 10.25)
        GR = m("gr", (2, T), S0 + 11.25)
        AC = m("ac", (2, 4), S0 + 13.25)
        DN, EM = GF, GT
        E0 = m("e0", (384,), S0 + 13.5)
        HN = m("hn", (2, T), S0 + 15)
        HS = m("hs", (2, T), S0 + 17)
        MF = m("mf", (8, T), 44)
        HG = m("hg", (2, T), 20)
        TA = [[m(f"ta{i}{j}", (384,), S0 + 19 + 3 * i + 1.5 * j) for j in range(2)] for i in range(2)]
        ASS = m("ass", (T,), S0 + 25)
        ARS = m("ars", (T,), S0 + 26)

        def transposed(dst, src, got, *waits):
            yield True
            yield True
            (i, b, free), = yield from grab()
            tr(BK[b][:, 0:128], src[:, 0:128], *waits, free)
            t = tr(BK[b][:, 128:256], src[:, 128:256], sig=True)
            yield
            t = cp(dst, BK[b][:, 0:256].rearrange("p (a f) -> p a f", a=2), t)
            bbank.give(i, t)
            got(t)

        def fetch(table, key):
            while key not in table:
                pump()
            return table[key]

        def await_(table, *keys):
            while not all(key in table for key in keys):
                yield

        def sigmoid_of(dst, e, *waits):
            t = fn(e, e, ACT.Ln, *waits, bias=1.0)
            return fn(dst, e, ACT.Exp, t, scale=-1.0)

        def conv_evac(l, n, ps, t, slot, dst, fr):
            cv, co, ev = CV[slot], CO[slot], EV[slot]
            w0 = PER_LAYER * l + CONV_W + 4 * n
            b0 = PER_LAYER * l + CONV_B + n
            t = fn(cv[:, 3:3 + T], ps, ACT.Copy, t, fr)
            free = t
            t = ts(co[:, :], cv[:, 0:T], PRM[:, w0:w0 + 1], PRM[:, b0:b0 + 1], ALU.mult, ALU.add, t)
            for j in range(1, 4):
                t = stt(co[:, :], cv[:, j:j + T], PRM[:, w0 + j:w0 + j + 1], co[:, :], ALU.mult, ALU.add, t)
            t = fn(ev[:, :], co[:, :], ACT.Exp, t, scale=-1.0)
            t = sigmoid_of(ev[:, :], ev[:, :], t)
            t = tt(dst, co[:, :], ev[:, :], ALU.mult, t)
            return free, t

        def mixer(l, xtok, start_tok):
            prm = PER_LAYER * l
            tokv = {}
            zt = None
            for i in range(2):
                zt = dve.put(lambda e, i=i: e.memset(CV[i][:, 0:3], 0.0), start_tok)
            slot_tok = [zt, zt]
            last_tv = [None, None]

            def evac(n, ps, t):
                kind, i = SLABS[n]
                if kind == "ka":
                    r = fn(KA[:, i, :], ps, ACT.Copy, t, start_tok)
                    tokv["ka", i] = r
                elif kind in ("va", "v"):
                    s = i % 2
                    prev = fetch(tokv, last_tv[s]) if last_tv[s] else None
                    r = fn(TV[s][:, :], ps, ACT.Copy, t, prev, start_tok)
                    dst = VA if kind == "va" else VM
                    last_tv[s] = (kind, i)
                    tasks["tr"].append(transposed(dst[:, :, 128 * i:128 * i + 128], TV[s],
                                                  lambda t, key=(kind, i): tokv.update({key: t}), r))
                    if kind == "v" and s:
                        tasks["mix"].append(mlstm(i // 2))
                elif kind == "qa":
                    r = fn(QA[:, i, :], ps, ACT.Copy, t, start_tok)
                    tokv["qa", i] = r
                    tasks["att"].append(attention(i // 4, i % 4))
                    if i == 7:
                        tasks["att"].append(att_norm())
                elif kind == "gate":
                    cp(GI[0:4, :], ps[0:4, :], t, start_tok)
                    r = cp(GF[0:4, :], ps[32:36, :], t, start_tok)
                    tasks["tr"].append(gates(r))
                elif kind in ("q", "k"):
                    s = int(kind == "k")
                    dst = KM[:, i, :] if s else QM[:, i, :]
                    r, slot_tok[s] = conv_evac(l, i + 4 * s, ps, t, s, dst, slot_tok[s])
                    tokv[kind, i] = slot_tok[s]
                else:
                    r = fn(OS[:, i, :], ps, ACT.Exp, t, start_tok, scale=-1.0)
                    tokv["os", i] = sigmoid_of(OS[:, i, :], OS[:, i, :], r)
                    if i % 2:
                        tasks["mix"].append(gated(i // 2))
                return r

            def gates(t):
                gi, gf, gt = GI[0:4, :], GF[0:4, :], GT[0:4, :]
                t = ts(gi, gi, PRM[0:4, prm + GATE_B:prm + GATE_B + 1], None, ALU.add, None, t)
                t = ts(gf, gf, PRM[0:4, prm + GATE_B + 1:prm + GATE_B + 2], None, ALU.add, None, t)
                t = fn(gt, gf, ACT.Abs, t)
                t = fn(gt, gt, ACT.Exp, t, scale=-1.0)
                t = fn(gt, gt, ACT.Ln, t, bias=1.0)
                t = stt(gf, gf, 0.0, gt, ALU.min, ALU.subtract, t)
                t = dve.put(lambda e: e.tensor_tensor_scan(gt, ONES[0:4, :], gf, 0.0, ALU.mult, ALU.add), t)
                t = tt(gi, gi, gt, ALU.subtract, t)
                t = dve.put(lambda e: e.tensor_tensor_scan(gf, ONES[0:4, :], gi, 0.0, ALU.mult, ALU.max), t)
                a_tok = t
                t = ts(GR[0:4, 0, :], gf, -1.0, None, ALU.mult, None, t)
                t = tt(gt, gt, gf, ALU.add, t)
                t = fn(GR[0:4, 1, :], gt, ACT.Exp, t, scale=-1.0)
                tokv["rows"] = t
                yield True
                yield True
                yield True
                (i, b, free), = yield from grab()
                tr(BK[b][:, 0:4], GI[0:4, 0:128], a_tok, free)
                t = tr(BK[b][:, 4:8], GI[0:4, 128:256], sig=True)
                yield
                t = cp(AC[:, :, :], BK[b][:, 0:8].rearrange("p (a h) -> p a h", a=2), t)
                bbank.give(i, t)
                tokv["acol"] = t

            def attention(pair, i):
                tile = 4 * pair + i
                u = tile % 2
                TT = TA[u]
                x0 = 64 + 16 * u
                yield from await_(tokv, ("va", 0), ("va", 1))
                wait = [tokv["qa", tile], tokv["ka", pair], tokv["va", 0], tokv["va", 1]]
                mx, nm, rs, es = (SM[:, x0 + 4 * n:x0 + 4 * n + 4] for n in range(4))
                prev = tokv.get(("att", u))
                held = yield from grab(2)
                st = []
                for par in range(2):
                    a = slice(64 * par, 64 * par + 64)
                    _, b, free = held[par]
                    mm(BK[b][:, 0:256], QA[a, tile, 128:256], KA[a, pair, :], True, True, *wait, free)
                    st.append(mm(BK[b][:, 256:384], QA[a, tile, 0:128], KA[a, pair, 0:128], True, True, sig=True))
                yield
                t = None
                for par in range(2):
                    head = (2 * pair + par) * 4 + i
                    bi, b, _ = held[par]
                    slope = 2.0 ** (-8.0 * (head + 1) / 16) * 8.0
                    t = stt(TT[par][:, :], CST[:, NDIST:NDIST + 384], slope, BK[b][:, 0:384],
                            ALU.mult, ALU.add, st[par], prev, start_tok)
                    bbank.give(bi, t)
                for par in range(2):
                    for j, q in ((0, slice(0, 256)), (1, slice(256, 384))):
                        c = 2 * par + j
                        t = dve.put(lambda e, c=c, q=q, par=par: e.tensor_reduce(
                            mx[:, c:c + 1], TT[par][:, q], AX.X, ALU.max), t)
                for par in range(2):
                    head = (2 * pair + par) * 4 + i
                    sk = PRM[:, prm + SINK + head:prm + SINK + head + 1]
                    t2 = ts(nm[:, 2 * par:2 * par + 2], mx[:, 2 * par:2 * par + 2], 0.125, sk,
                            ALU.mult, ALU.max, t, prev)
                tm = ts(nm, nm, -1.0, None, ALU.mult, None, t2)
                yield
                for par in range(2):
                    head = (2 * pair + par) * 4 + i
                    sk = PRM[:, prm + SINK + head:prm + SINK + head + 1]
                    for blk, s in ((0, slice(0, 256)), (1, slice(256, 384))):
                        c = 2 * par + blk
                        fn(TT[par][:, s], TT[par][:, s], ACT.Exp, tm, scale=0.125,
                           bias=nm[:, c:c + 1], accum_out=rs[:, c:c + 1])
                    te = fn(es[:, 2 * par:2 * par + 2], nm[:, 2 * par:2 * par + 2], ACT.Exp, bias=sk)
                yield
                t = tt(rs, rs, es, ALU.add, te)
                t = rec(rs, rs, t)
                for par in range(2):
                    for blk, s in ((0, slice(0, 256)), (1, slice(256, 384))):
                        c = 2 * par + blk
                        tn = ts(TT[par][:, s], TT[par][:, s], rs[:, c:c + 1], None, ALU.mult, None, t)
                yield True
                held = yield from grab(2)
                st = []
                for par in range(2):
                    _, b, fr = held[par]
                    tr(BK[b][:, 0:128], TT[par][:, 256:384], tn, fr)
                    tr(BK[b][:, 128:256], TT[par][:, 0:128])
                    st.append(tr(BK[b][:, 256:384], TT[par][:, 128:256], sig=True))
                yield
                c1 = fn(TT[0][:, :], BK[held[0][1]][:, 0:384], ACT.Copy, st[0])
                bbank.give(held[0][0], c1)
                c2 = cp(TT[1][:, :], BK[held[1][1]][:, 0:384], st[1])
                bbank.give(held[1][0], c2)
                yield True
                (bo, bout, free), = yield from grab()
                for par in range(2):
                    v = slice((2 * pair + par) * 64, (2 * pair + par) * 64 + 64)
                    a = slice(64 * par, 64 * par + 64)
                    mm(BK[bout][a, 0:256], VA[:, 0, v], TT[par][:, 0:256], True, False, c1, c2, free)
                    t = mm(BK[bout][a, 128:256], VA[:, 1, v], TT[par][:, 256:384], False, True, sig=True)
                yield
                q = fn(QA[:, tile, :], BK[bout][:, 0:256], ACT.Copy, t)
                bbank.give(bo, q)
                if tile == 0:
                    t = fn(ASS[:, :], QA[:, tile, :], ACT.Square, q, start_tok)
                    tokv["ass"] = t
                else:
                    t = fn(TT[0][:, 0:256], QA[:, tile, :], ACT.Square, q)
                    yield
                    t = tokv["ass"] = tt(ASS[:, :], ASS[:, :], TT[0][:, 0:256], ALU.add, t, tokv["ass"])
                tokv["att", u] = t

            def att_norm():
                while ("att", 1) not in tokv or len(tasks["att"]) > 1:
                    yield
                (i, b, free), = yield from grab()
                t = mm(BK[b][:, 0:T], ONES[:, 0:128], ASS[:, :], True, True,
                       tokv["ass"], tokv["att", 0], tokv["att", 1], free, sig=True)
                yield
                t0 = rsqrt(ARS[:, :], BK[b][:, 0:T], 1024, ARS[:, :], t, start_tok)
                bbank.give(i, t0)
                yield
                for k in range(8):
                    c = prm + G_ATT + k
                    t = stt(QA[:, k, :], QA[:, k, :], PRM[:, c:c + 1], ARS[:, :], ALU.mult, ALU.mult, t0)
                    yield
                    tokv["a_hl", k] = split(AHI[:, k, :], QAL[:, k, :], QA[:, k, :], t, start_tok)

            def mlstm(h):
                yield from await_(tokv, "acol", ("v", 2 * h), ("v", 2 * h + 1))
                (i1, b1, f1), (i2, b2, f2) = yield from grab(2)
                rowb = mm(BK[b1][:, :], ident[0:4, h:h + 1].to_broadcast([4, 128]),
                          GR[0:4, :, :].rearrange("p a t -> p (a t)"), True, True, tokv["rows"], f1, sig=True)
                sc = BK[b2]
                mm(sc[:, 0:256], KM[:, h, 0:128], QM[:, h, :], True, True, tokv["q", h], tokv["k", h], f2)
                st = mm(sc[:, 256:384], KM[:, h, 128:256], QM[:, h, 128:256], True, True, sig=True)
                yield
                prev = tokv.get("m_done")
                em = fn(EM[:, :], BK[b1][:, 256:512], ACT.Copy, rowb, prev, tokv["rows"])
                yield
                mk = CST[:, MASKT:MASKT + 128]
                stt(E0[:, 0:128], BK[b1][:, 0:128], AC[:, 0, h:h + 1], mk, ALU.add, ALU.add,
                    em, tokv["acol"], prev)
                t = stt(E0[:, 256:384], BK[b1][:, 128:256], AC[:, 1, h:h + 1], mk, ALU.add, ALU.add)
                yield
                t = fn(E0[:, 128:256], BK[b1][:, 128:256], ACT.Exp, t, bias=AC[:, 0, h:h + 1])
                bbank.give(i1, t)
                fn(E0[:, 0:128], E0[:, 0:128], ACT.Exp)
                t = fn(E0[:, 256:384], E0[:, 256:384], ACT.Exp)
                yield
                t = stt(E0[:, :], sc[:, 0:384], 128.0 ** -0.5, E0[:, :], ALU.mult, ALU.mult, t, st)
                bbank.give(i2, t)
                yield True
                (i3, b3, f3), (i4, b4, f4) = yield from grab(2)
                for j in range(2):
                    v = slice(256 * h + 128 * j, 256 * h + 128 * j + 128)
                    o0 = 256 * j
                    mm(BK[b3][:, o0:o0 + 256], VM[:, 0, v], E0[:, 0:256], True, False,
                       t, f3, tokv["v", 2 * h], tokv["v", 2 * h + 1])
                    nt = mm(BK[b3][:, o0 + 128:o0 + 256], VM[:, 1, v], E0[:, 256:384], False, True, sig=True)
                mm(BK[b4][:, 0:256], ONES[:, 0:128], E0[:, 0:256], True, False, f4)
                t = mm(BK[b4][:, 128:256], ONES[:, 0:128], E0[:, 256:384], False, True, sig=True)
                yield
                t = fn(DN[:, :], BK[b4][:, 0:256], ACT.Abs, t, prev, tokv["rows"])
                bbank.give(i4, t)
                yield
                t = tt(DN[:, :], DN[:, :], EM[:, :], ALU.max, t, em)
                t = rec(DN[:, :], DN[:, :], t)
                hn = tt(HN[:, :, :], BK[b3][:, :].rearrange("p (a t) -> p a t", a=2), bc(DN[:, :], 2),
                        ALU.mult, t, nt, prev)
                bbank.give(i3, hn)
                yield
                t = fn(HS[:, :, :], HN[:, :, :], ACT.Square, hn)
                yield True
                (i4, b4, f4), = yield from grab()
                mm(BK[b4][:, 0:256], ONES[:, 0:128], HS[:, 0, :], True, False, t, f4)
                t = mm(BK[b4][:, 0:256], ONES[:, 0:128], HS[:, 1, :], False, True, sig=True)
                yield
                t = rsqrt(DN[:, :], BK[b4][:, 0:256], 256, DN[:, :], t, hn)
                bbank.give(i4, t)
                yield
                for j in range(2):
                    c = prm + G_HEAD + 2 * h + j
                    t1 = stt(MF[:, 2 * h + j, :], HN[:, j, :], PRM[:, c:c + 1], DN[:, :],
                             ALU.mult, ALU.mult, t, start_tok)
                tokv["m_done"] = tokv["mf", h] = t1

            def gated(h):
                while ("mf", h) not in tokv:
                    yield
                q = slice(2 * h, 2 * h + 2)
                t = tt(HG[:, :, :], MF[:, q, :], OS[:, q, :], ALU.mult, tokv["mf", h], tokv["os", 2 * h],
                       tokv["os", 2 * h + 1], tokv.get("hg"))
                yield
                tokv["m_hl", h] = split(MHI[:, q, :], OSL[:, q, :], HG[:, :, :], t, start_tok)
                tokv["hg"] = tokv["m_hl", h][1]

            return evac, tokv

        HBH = m("hbh", (KT, T), 28, F32R)
        HBL = m("hbl", (KT, T), 44, F32R)
        UR = [m(f"ur{i}", (T,), 60 + i) for i in range(2)]

        def first_layer(l, x_ready):
            t0 = x_ready
            want_mod((l, SCALE_A))
            want_mod((l, SHIFT_A))
            gs, sh, gg = (MOD[:, 6 * l + p_, :] for p_ in (SCALE_A, SHIFT_A, GATE_A))
            xt = to_h(gs, sh, [mod_ready[l, SCALE_A], mod_ready[l, SHIFT_A]], t0)
            start = fence()
            evac, tokv = mixer(l, xt, start)
            gemm(37, lambda k: HH[:, k, :], lambda k: HL[:, k, :], lambda k: xt[k], evac, each=2)
            while tasks["att"] or tasks["mix"]:
                pump()

            def xh(k):
                return MHI[:, k, :] if k < 8 else AHI[:, k - 8, :]

            def xl(k):
                return OSL[:, k, :] if k < 8 else QAL[:, k - 8, :]

            def xr(k):
                return tokv["m_hl", k // 2] if k < 8 else tokv["a_hl", k - 8]

            f = fence()
            yt = []

            sq = Squares(62, f"ya{l}", f)

            def yevac(n, ps, t):
                yt.append(fn(Y1[:, n, :], ps, ACT.Copy, t, f))
                return sq.add(ps, t)

            gemm(16, xh, xl, xr, yevac, korder=list(range(8, 16)) + list(range(8)))
            gt = want_mod((l, GATE_A))
            _, t0 = add_y(Y1, gg, gt, sq, fence())
            want_mod((l, SCALE_M))
            want_mod((l, SHIFT_M))
            gs, sh, gg = (MOD[:, 6 * l + p_, :] for p_ in (SCALE_M, SHIFT_M, GATE_M))
            xt = to_h(gs, sh, [mod_ready[l, SCALE_M], mod_ready[l, SHIFT_M]], t0)
            f = fence()
            ht = {}
            ur = Slots(UR)
            yprev = [None] * KT
            pe_done = [f]
            sq2 = Squares(62, f"yb{l}", f)

            def up_evac(n, ps, t):
                i, u, free = ur.take()
                r = fn(u[:, :], ps, ACT.Relu, t, free, pe_done[0])
                t1 = tt(u[:, :], u[:, :], u[:, :], ALU.mult, r)
                ht[n] = split(HBH[:, n, :], HBL[:, n, :], u[:, :], t1, pe_done[0])
                ur.give(i, *ht[n])
                return r

            def down_evac(n, ps, t):
                if yprev[n] is None:
                    yprev[n] = fn(Y1[:, n, :], ps, ACT.Copy, t, f)
                else:
                    yprev[n] = tt(Y1[:, n, :], ps, Y1[:, n, :], ALU.add, t, yprev[n])
                if j_now[0] == 3:
                    sq2.add(Y1[:, n, :], yprev[n])
                return yprev[n]

            j_now = [0]
            for j in range(4):
                j_now[0] = j
                gemm(16, lambda k: HH[:, k, :], lambda k: HL[:, k, :], lambda k: xt[k], up_evac)
                h_now = dict(ht)
                t = gemm(16, lambda k: HBH[:, k, :], lambda k: HBL[:, k, :], lambda k: h_now[k], down_evac)
                pe_done[0] = t
            gt = want_mod((l, GATE_M))
            return add_y(Y1, gg, gt, sq2, fence())[1]

        xt_ = stats(x_tok)
        for l in range(2):
            xt_ = first_layer(l, xt_)
        drain()

        H = m("Hst", (129, 2, 64), 0)
        AP_ = m("ap", (12, 64), 0)
        CR = m("cr", (2, 64, 16), 4)
        CT = m("ct", (2, 64, 16), 12)
        C2 = m("c2", (64, 16), 20)
        CC = m("cc", (2, 64, 2, 32), 24)
        BT = [m(f"bt{i}", (2, 128), 56 + i) for i in range(2)]
        MASKB = m("maskb", (128,), 58)
        U = m("u", (KT, T), 64.5)
        K0 = m("k0", (KT, 128), 80.5)
        TAB = m("tab", (2, 2, 64), 88.5)
        PR = m("pr", (2, 2, 64), 89.5)
        SS = m("ss", (2, 64), 90.5)
        AT = m("atr", (256,), 91)
        Z = at("z", (KT, T), base)
        BS = [at(f"bs{i}", (2, 128), base + i * kb) for i in range(3)]
        AB = [at(f"ab{i}", (2, 128), base + (3 + i) * kb) for i in range(3)]
        AQ = [at(f"aq{i}", (2, 2, 128), base + (6 + 2 * i) * kb) for i in range(2)]
        SEL = [at(f"sel{i}", (4, 32), base + 10 * kb + 512 * i) for i in range(2)]
        CL = at("cl", (2, 64, 2, 32), A0)
        x_keep = nc.dram_tensor("x_keep", (P, KT, T), F32, kind="Internal").ap()
        c_keep = nc.dram_tensor("c_keep", (P, 2 * 64 * 2 * 32), F32, kind="Internal").ap()
        s_keep, s_cc = sem("s_keep"), sem("s_cc")

        f0 = fence()
        act.dma(lambda e: e.dma_start(AP_[:, 0:3, :], d["s5_ap"]), s_tab, 32, f0)
        act.dma(lambda e: e.dma_start(CR[:, :, :, :], d["s5_c"]), s_tab, 48, f0)
        tab_tok = act.dma(lambda e: e.dma_start(MASKB[:, :], d["s5_mask"]), s_tab, 64, f0)
        xt = to_h(PRM[:, S5_PRE:S5_PRE + 16], None, None, xt_, f0)
        f = fence()
        x_kept = act.dma(lambda e: e.dma_start(x_keep, Xf), s_keep, 16, f)
        uz = {}

        def u_evac(n, ps, t):
            uz[n] = fn(U[:, n, :], ps, ACT.Copy, t, f)
            return uz[n]

        a_re, a_im, ldt, dt_, mag, th, sn, cs, arr, t8, t9, t10 = (AP_[:, i, :] for i in range(12))
        s5 = {}

        def tables():
            t = fn(dt_, ldt, ACT.Exp, tab_tok, f)
            t = tt(mag, a_re, dt_, ALU.mult, t)
            t = fn(mag, mag, ACT.Exp, t)
            mag_t = t
            t = tt(th, a_im, dt_, ALU.mult, dve.last())
            TWO_PI = 2.0 * np.pi
            C1 = float(np.float32(6.28125))
            C2_ = float(np.float32(TWO_PI - 6.28125))
            C3_ = float(TWO_PI - C1 - C2_)
            MAGIC = float(1.5 * 2 ** 23)

            def reduced(dst, src, add, *waits):
                t = ts(t8, src, add, 1.0 / TWO_PI, ALU.add, ALU.mult, *waits)
                t = ts(t8, t8, MAGIC, None, ALU.add, None, t)
                t = ts(t8, t8, -MAGIC, None, ALU.add, None, t)
                t = stt(dst, t8, -C1, src, ALU.mult, ALU.add, t)
                t = stt(dst, t8, -C2_, dst, ALU.mult, ALU.add, t)
                t = stt(dst, t8, -C3_, dst, ALU.mult, ALU.add, t)
                t = ts(dst, dst, add, float(np.float32(np.pi) - np.float32(2e-7)), ALU.add, ALU.min, t)
                return ts(dst, dst, -float(np.float32(np.pi) - np.float32(2e-7)), None, ALU.max, None, t)

            yield
            t = reduced(sn, th, 0.0, t)
            yield
            t = reduced(cs, th, float(np.pi / 2), t)
            yield
            t = fn(sn, sn, ACT.Sin, t)
            t = fn(cs, cs, ACT.Sin, t)
            t = tt(cs, cs, mag, ALU.mult, t, mag_t)
            t = tt(sn, sn, mag, ALU.mult, t)
            s5["a"] = t
            yield
            tt(t8, cs, cs, ALU.mult, t)
            tt(t9, sn, sn, ALU.mult)
            t1 = tt(t10, cs, sn, ALU.mult)
            tt(TAB[:, 0, 0, :], t8, t9, ALU.subtract, t1, f)
            tt(TAB[:, 0, 1, :], t8, t9, ALU.subtract)
            ts(TAB[:, 1, 0, :], t10, 2.0, None, ALU.mult, None)
            s5["tab"] = t = ts(TAB[:, 1, 1, :], t10, -2.0, None, ALU.mult, None)
            yield
            t = ts(arr, cs, -1.0, None, ALU.add, None, t)
            t = tt(t8, a_re, a_re, ALU.mult, t)
            t = tt(t9, a_im, a_im, ALU.mult, t)
            t = tt(t8, t8, t9, ALU.add, t)
            t = rec(t8, t8, t)
            t = tt(t9, arr, a_re, ALU.mult, t)
            t = tt(t10, sn, a_im, ALU.mult, t)
            t = tt(t9, t9, t10, ALU.add, t)
            t = tt(t9, t9, t8, ALU.mult, t)
            t = tt(t10, sn, a_re, ALU.mult, t)
            t = tt(arr, arr, a_im, ALU.mult, t)
            t = tt(t10, t10, arr, ALU.subtract, t)
            t = tt(t10, t10, t8, ALU.mult, t)
            yield

            def over_c(ap):
                return ap.rearrange("p (g c) -> p g c", c=1).to_broadcast([P, 64, 16])

            zt = dve.put(lambda e: e.memset(CC[:, :, :, :, :], 0.0), t)
            yield
            cre, cim = CR[:, 0, :, :], CR[:, 1, :, :]
            t = tt(CT[:, 0, :, :], cre, over_c(t9), ALU.mult, zt)
            t = tt(C2[:, :, :], cim, over_c(t10), ALU.mult, t)
            t = tt(CT[:, 0, :, :], CT[:, 0, :, :], C2[:, :, :], ALU.subtract, t)
            yield
            t = tt(CT[:, 1, :, :], cre, over_c(t10), ALU.mult, t)
            t = tt(C2[:, :, :], cim, over_c(t9), ALU.mult, t)
            t = stt(CT[:, 1, :, :].rearrange("p g c -> p (g c)"), CT[:, 1, :, :].rearrange("p g c -> p (g c)"), -1.0,
                    C2[:, :, :].rearrange("p g c -> p (g c)"), ALU.mult, ALU.subtract, t)
            yield

            def blocks(kind, src, t):
                for gh in range(2):
                    for ri in range(2):
                        t = fn(CC[64 * gh:64 * gh + 64, kind, :, ri, 16 * gh:16 * gh + 16],
                               src[64 * gh:64 * gh + 64, ri, :, :], ACT.Copy, t)
                return t

            s5["cb"] = blocks(0, CT, t)
            t = tt(cre, CT[:, 0, :, :], over_c(cs), ALU.mult, t)
            t = tt(C2[:, :, :], CT[:, 1, :, :], over_c(sn), ALU.mult, t)
            t = tt(cre, cre, C2[:, :, :], ALU.add, t)
            yield
            t = tt(cim, CT[:, 1, :, :], over_c(cs), ALU.mult, t)
            t = tt(C2[:, :, :], CT[:, 0, :, :], over_c(sn), ALU.mult, t)
            t = tt(cim, cim, C2[:, :, :], ALU.subtract, t)
            yield
            t = blocks(1, CR, t)
            s5["cc"] = act.dma(lambda e: e.dma_start(c_keep, CC[:, :, :, :, :].rearrange("p a g r c -> p (a g r c)")),
                               s_cc, 16, t)
            yield True
            (i, b, free), = yield from grab()
            tr(BK[b][0:64, 0:128], cs, s5["a"], free)
            t = tr(BK[b][0:64, 128:256], sn, sig=True)
            yield
            s5["at"] = fn(AT[0:64, :], BK[b][0:64, 0:256], ACT.Copy, t, f)
            bbank.give(i, s5["at"])
            btf, btn = [None, None], [0, 0]
            for q in range(16):
                j = q % 2
                btn[j] += 16
                t = sp.dma(lambda e, q=q, j=j: e.dma_start(BT[j][:, :, :], d["s5_bt"][q]),
                           s_bt[j], btn[j], btf[j], f)
                yield
                (i, b, free), = yield from grab()
                for ri in range(2):
                    t = mm(BK[b][:, 0:128], BT[j][:, ri, :], CC[:, 0, 4 * q:4 * q + 4, ri, :], ri == 0, ri == 1,
                           t, free, s5["cb"], sig=ri == 1)
                btf[j] = t
                yield
                s5["k0"] = tt(K0[:, q, :], BK[b][:, 0:128], MASKB[:, :], ALU.mult, t, f)
                bbank.give(i, s5["k0"])
            s5["end"] = fence()

        tasks["mix"].append(tables())
        gemm(16, lambda k: HH[:, k, :], lambda k: HL[:, k, :], lambda k: xt[k], u_evac, each=4)
        drain()

        bs = Slots([0, 1, 2])
        bn = [0, 0, 0]
        aq_free, sel_free = [None, None], [None, None]
        x_tok = None
        f = [fence(), s5["cc"], x_kept, s5["end"]]
        zt = dve.put(lambda e: e.memset(H[:, 0, :, :], 0.0), f)
        lo = hi = None

        def load_b(q):
            i, b_, free = bs.take()
            bn[b_] += 16
            bt = sp.dma(lambda e: e.dma_start(BS[b_][:, :, :], d["s5_b"][q]), s_b[b_], bn[b_], free, f)
            gi_, bk, fr = bank()
            sel = SEL[q % 2]
            pick = ident[0:64, 4 * q:4 * q + 4].rearrange("k (w c) -> k w c", c=1).to_broadcast([64, 4, 32])
            t = cp(sel[0:64, :, :], pick, f, sel_free[q % 2])
            t = sel_free[q % 2] = mm(BK[bk][:, 0:256], sel[0:64, :, :].rearrange("k w c -> k (w c)"), AT[0:64, :],
                                     True, True, t, s5["at"], fr, sig=True)
            aq = AQ[q % 2]
            a2 = BK[bk][:, 0:256].rearrange("p (a s) -> p a s", a=2)
            tt(aq[:, 0, :, :], a2, bc(BS[b_][:, 0, :], 2), ALU.mult, t, bt, f, aq_free[q % 2])
            t = tt(aq[:, 1, :, :], a2, bc(BS[b_][:, 1, :], 2), ALU.mult)
            bbank.give(gi_, t)
            tt(AB[b_][:, 0, :], aq[:, 0, 0, :], aq[:, 1, 1, :], ALU.subtract, t, free)
            t = tt(AB[b_][:, 1, :], aq[:, 0, 1, :], aq[:, 1, 0, :], ALU.add)
            aq_free[q % 2] = t
            return i, b_, [bt, t]

        nxt = load_b(0)
        for q in range(16):
            i, b_, bt = nxt
            if q < 15:
                nxt = load_b(q + 1)
            for w in range(4):
                rows = slice(32 * w, 32 * w + 32)
                gt = 4 * q + w
                gi_, bk, fr = bank()
                for ri in range(2):
                    o = BK[bk][:, 128 * ri:128 * ri + 128]
                    mm(o, AB[b_][rows, ri, :], U[rows, q, 0::2], True, False, bt, fr, uz[q])
                    last = mm(o, BS[b_][rows, ri, :], U[rows, q, 1::2], False, True, sig=ri == 1)
                x_done = fn(H[:, 1:129, :, gt].rearrange("p t r -> p r t"),
                            BK[bk][:, 0:256].rearrange("p (r t) -> p r t", r=2), ACT.Copy, last, f)
                bbank.give(gi_, x_done)
            bs.give(i, last)

        def scan():
            th = [x_done, x_done]
            for s in range(1, 128):
                for half in range(2):
                    g = slice(32 * half, 32 * half + 32)
                    src = H[:, s, :, g].rearrange("p (a r) g -> p a r g", a=1).to_broadcast([P, 2, 2, 32])
                    th[half] = tt(PR[:, :, :, g], TAB[:, :, :, g], src, ALU.mult, th[half], s5["tab"])
                for half in range(2):
                    g = slice(32 * half, 32 * half + 32)
                    th[half] = tt(SS[:, :, g], PR[:, 0, :, g], PR[:, 1, ::-1, g], ALU.add, th[half])
                for half in range(2):
                    g = slice(32 * half, 32 * half + 32)
                    th[half] = tt(H[:, s + 1, :, g], H[:, s + 1, :, g], SS[:, :, g], ALU.add, th[half])
                yield
            s5["h"] = th

        fz = fence()

        def z_evac(n, ps, t):
            r = fn(Z[:, n, :], ps, ACT.Exp, t, fz, scale=-1.0)
            t1 = sigmoid_of(Z[:, n, :], Z[:, n, :], r)
            uz[16 + n] = tt(Z[:, n, :], ps, Z[:, n, :], ALU.mult, t1)
            return uz[16 + n]

        tasks["mix"].append(scan())
        z_pe = gemm(16, lambda k: HH[:, k, :], lambda k: HL[:, k, :], lambda k: xt[k], z_evac, each=3)
        cl_tok = sp.dma(lambda e: e.dma_start(CL[:, :, :, :, :].rearrange("p a g r c -> p (a g r c)"), c_keep),
                        s_cc, 32, z_pe, s5["cc"])
        drain()
        uy = []
        for q in range(16):
            gi_, bk, fr = bank()
            ps = BK[bk]
            mm(ps[:, 0:128], K0[:, q, :], U[:, q, 0::2], True, False, fr, s5["h"], cl_tok, zt, s5["k0"])
            for w in range(4):
                rows = slice(32 * w, 32 * w + 32)
                gt = 4 * q + w
                for ri in range(2):
                    mm(ps[rows, 0:128], CL[:, 1, gt, ri, :], H[:, 0:128, ri, gt], False, ri == 1)
                for ri in range(2):
                    last = mm(ps[rows, 128:256], CL[:, 0, gt, ri, :], H[:, 1:129, ri, gt], ri == 0, ri == 1,
                              sig=ri == 1)
            u2 = U[:, q, :].rearrange("p (b e) -> p e b", e=2)
            t = stt(u2, u2, PRM[:, S5_D + q:S5_D + q + 1], ps[:, 0:256].rearrange("p (e b) -> p e b", e=2),
                    ALU.mult, ALU.add, last)
            bbank.give(gi_, t)
            uy.append(fn(U[:, q, :], U[:, q, :], ACT.Gelu_apprx_tanh, t))

        ff = fence()
        yt = [split(HH[:, q, :], HL[:, q, :], U[:, q, :], uy[q], ff) for q in range(16)]
        GOH = m("goh", (KT, T), 32, F32R)
        GOL = m("gol", (KT, T), 0, F32R)
        Y2 = m("y2", (KT, T), 16)
        NB = m("nb", (16,), 88.5)
        nb = ts(NB[:, :], PRM[:, S5_BGLU:S5_BGLU + 16], -1.0, None, ALU.mult, None, ff)
        ff = fence()
        go = {}
        ZF = [m(f"zf{i}", (T,), 90 + i) for i in range(2)]
        ze = Slots(ZF)

        def glu_evac(n, ps, t):
            i, e_, free = ze.take()
            r = fn(e_[:, :], ps, ACT.Exp, t, free, ff, nb, scale=-1.0, bias=NB[:, n:n + 1])
            t1 = sigmoid_of(e_[:, :], e_[:, :], r)
            t1 = tt(e_[:, :], e_[:, :], U[:, n, :], ALU.mult, t1)
            t1 = tt(e_[:, :], e_[:, :], Z[:, n, :], ALU.mult, t1)
            go[n] = split(GOH[:, n, :], GOL[:, n, :], e_[:, :], t1, ff)
            ze.give(i, *go[n])
            return r

        gemm(16, lambda k: HH[:, k, :], lambda k: HL[:, k, :], lambda k: yt[k], glu_evac)
        y2t = []
        x_back = sp.dma(lambda e: e.dma_start(Xf, x_keep), s_keep, 32, x_kept, fence())
        sq = Squares(50, "yc", fence())

        def y2_evac(n, ps, t):
            y2t.append(fn(Y2[:, n, :], ps, ACT.Copy, t, ff))
            return sq.add(ps, t)

        gemm(16, lambda k: GOH[:, k, :], lambda k: GOL[:, k, :], lambda k: go[k], y2_evac)
        _, t0 = add_y(Y2, PRM[:, S5_POST:S5_POST + 16], None, sq, fence(), x_back)

        KF = m("kf", (KT, T), 0)
        VF = m("vf", (2, D), 16)
        QF = m("qf", (KT, T), 32)
        ZZ = m("zz", (KT, T), 48)
        FOL = m("fol", (KT, T), 48, F32R)
        FOH = m("foh", (KT, T), 64, F32R)
        FV = [m(f"fv{i}", (T,), 80 + i) for i in range(2)]
        FE = [m(f"fe{i}", (T,), 82 + i) for i in range(2)]
        CG = m("cg", (T,), 84)
        CN = m("cn", (T,), 85)
        TF = [m(f"tf{i}", (384,), 86 + 1.5 * i) for i in range(2)]
        PF = [m(f"pf{i}", (384,), 89 + 1.5 * i) for i in range(2)]
        XF = SM[:, 64:80]
        Y3 = m("y3", (KT, T), 0)

        xt = to_h(PRM[:, KV_G:KV_G + 16], None, None, t0)
        f = fence()
        kv = {}

        def kv_evac(n, ps, t):
            if n == 0:
                r = cp(CG[0:16, :], ps[0:16, :], t, f)
                t1 = ts(CG[0:16, :], CG[0:16, :], PRM[0:16, KV_BF:KV_BF + 1], None, ALU.add, None, r)
                t1 = fn(CN[0:16, :], CG[0:16, :], ACT.Abs, t1)
                t1 = fn(CN[0:16, :], CN[0:16, :], ACT.Exp, t1, scale=-1.0)
                t1 = fn(CN[0:16, :], CN[0:16, :], ACT.Ln, t1, bias=1.0)
                t1 = stt(CG[0:16, :], CG[0:16, :], 0.0, CN[0:16, :], ALU.min, ALU.subtract, t1)
                t1 = dve.put(lambda e: e.tensor_tensor_scan(CN[0:16, :], ONES[0:16, :], CG[0:16, :], 0.0,
                                                            ALU.mult, ALU.add), t1)
                kv["c"] = ts(CN[0:16, :], CN[0:16, :], -(128.0 ** 0.5), None, ALU.mult, None, t1)
                return r
            n -= 1
            if n < 16:
                kv["k", n] = fn(KF[:, n, :], ps, ACT.Copy, t, f)
                return kv["k", n]
            n -= 16
            s = n % 2
            prev = fetch(kv, ("v", n - 2)) if n > 1 else None
            r = fn(FV[s][:, :], ps, ACT.Copy, t, prev, f)
            tasks["tr"].append(transposed(VF[:, :, 128 * n:128 * n + 128], FV[s],
                                          lambda t, n=n: kv.update({("v", n): t}), r))
            return r

        early = scaled(PRM[:, FOX_PRE:FOX_PRE + 16], f)
        kv_pe = gemm(33, lambda k: HH[:, k, :], lambda k: HL[:, k, :], lambda k: xt[k], kv_evac)
        xt = to_h(None, None, None, kv_pe, early=early)
        f = fence()
        fe = Slots(FE)

        def fox(h):
            scale = 128.0 ** -0.5
            yield from await_(kv, ("v", h))
            wait = [kv["k", h], kv["q", h], kv["c"], kv["v", h]]
            s = h % 2
            tf, pf = TF[s], PF[s]
            x4 = XF[:, 4 * s:4 * s + 4]
            (i, b, free), = yield from grab()
            row = ident[0:16, h:h + 1].to_broadcast([16, 128])
            mm(BK[b][:, 0:256], QF[:, h, 128:256], KF[:, h, :], True, False, *wait, free)
            mm(BK[b][:, 0:256], row, CN[0:16, :], False, True)
            mm(BK[b][:, 256:384], QF[:, h, 0:128], KF[:, h, 0:128], True, False)
            t = mm(BK[b][:, 256:384], row, CN[0:16, 0:128], False, True, sig=True)
            yield
            prev = kv.get(("fox", s))
            mk = CST[:, MASKF:MASKF + 384]
            t = tt(tf[:, :], BK[b][:, 0:384], mk, ALU.add, t, prev, f)
            bbank.give(i, t)
            t = dve.put(lambda e: e.tensor_reduce(x4[:, 0:1], tf[:, 0:256], AX.X, ALU.max), t)
            t = dve.put(lambda e: e.tensor_reduce(x4[:, 1:2], tf[:, 256:384], AX.X, ALU.max))
            t = ts(x4[:, 0:2], x4[:, 0:2], -scale, None, ALU.mult, None, t)
            yield
            for c, q in ((0, slice(0, 256)), (1, slice(256, 384))):
                t2 = fn(pf[:, q], tf[:, q], ACT.Exp, t, prev, scale=scale, bias=x4[:, c:c + 1],
                        accum_out=x4[:, 2 + c:3 + c])
            yield
            t = rec(x4[:, 2:4], x4[:, 2:4], t2)
            ts(pf[:, 0:256], pf[:, 0:256], x4[:, 2:3], None, ALU.mult, None, t)
            t = ts(pf[:, 256:384], pf[:, 256:384], x4[:, 3:4], None, ALU.mult, None)
            yield True
            (i, b, free), = yield from grab()
            tr(BK[b][:, 0:128], pf[:, 256:384], t, free)
            tr(BK[b][:, 128:256], pf[:, 0:128])
            t = tr(BK[b][:, 256:384], pf[:, 128:256], sig=True)
            yield
            t = cp(tf[:, :], BK[b][:, 0:384], t)
            bbank.give(i, t)
            yield True
            (i, b, free), = yield from grab()
            v = slice(128 * h, 128 * h + 128)
            mm(BK[b][:, 0:256], VF[:, 0, v], tf[:, 0:256], True, False, t, free)
            t = mm(BK[b][:, 128:256], VF[:, 1, v], tf[:, 256:384], False, True, sig=True)
            yield
            kv["o", h] = kv["fox", s] = cp(QF[:, h, :], BK[b][:, 0:256], t)
            bbank.give(i, kv["o", h])
            yield

        def qz_evac(n, ps, t):
            if n < 16:
                kv["q", n] = fn(QF[:, n, :], ps, ACT.Copy, t, f)
                tasks["att"].append(fox(n))
                return kv["q", n]
            n -= 16
            i, e_, free = fe.take()
            r = fn(e_[:, :], ps, ACT.Exp, t, free, f, scale=-1.0)
            t1 = sigmoid_of(e_[:, :], e_[:, :], r)
            kv["z", n] = tt(ZZ[:, n, :], ps, e_[:, :], ALU.mult, t1)
            fe.give(i, kv["z", n])
            return kv["z", n]

        gemm(32, lambda k: HH[:, k, :], lambda k: HL[:, k, :], lambda k: xt[k], qz_evac, each=2)
        drain()
        ft = []
        for c in range(4):
            q = slice(4 * c, 4 * c + 4)
            t = tt(QF[:, q, :], QF[:, q, :], ZZ[:, q, :], ALU.mult, kv["o", 4 * c + 3], kv["z", 4 * c + 3])
            ft += [split(FOH[:, q, :], FOL[:, q, :], QF[:, q, :], t, f)] * 4
        ff = fence()
        y3t = []

        sq = Squares(32, "yd", ff)

        def y3_evac(n, ps, t):
            y3t.append(fn(Y3[:, n, :], ps, ACT.Copy, t, ff))
            return sq.add(ps, t)

        gemm(16, lambda k: FOH[:, k, :], lambda k: FOL[:, k, :], lambda k: ft[k], y3_evac)
        xs, _ = add_y(Y3, PRM[:, FOX_POST:FOX_POST + 16], None, sq, fence(), norm=False)
        for c in range(4):
            q = slice(4 * c, 4 * c + 4)
            sp.dma(lambda e, q=q: e.dma_start(out[:, q, :], X[:, q, :]), s_out, 16 * (c + 1), xs[4 * c + 3])
        sp.items.append(([(s_out, 64)], lambda e: e.wait_ge(s_out, 64), None, 0))

        with nc.Block() as block:
            @block.sync
            def _(e):
                sp.emit(e)

            @block.scalar
            def _(e):
                act.emit(e)

            @block.vector
            def _(e):
                dve.emit(e)

            @block.tensor
            def _(e):
                pe.emit(e)


def constants():
    cst = np.zeros((P, N_CST), np.float32)
    cst[:, IDENT:IDENT + 128] = np.eye(128, dtype=np.float32)
    r = np.arange(128)[:, None]
    u = np.arange(256)[None, :]
    dist = r + 128 - u
    nd = np.where((dist >= 0) & (dist < 128), -dist, BIG).astype(np.float32)
    cst[:, NDIST:NDIST + 256] = nd
    cst[:, NDIST + 256:NDIST + 384] = nd[:, 128:256]
    s = np.arange(128)[:, None]
    t = np.arange(128)[None, :]
    cst[:, MASKT:MASKT + 128] = np.where(s <= t, 0.0, BIG)
    tri = np.where(t <= s, 0.0, BIG).astype(np.float32)
    cst[:, MASKF + 128:MASKF + 256] = tri
    cst[:, MASKF + 256:MASKF + 384] = tri
    return cst


def head_columns():
    cols = []
    for pair in range(2):
        for i in range(4):
            for par in range(2):
                head = (2 * pair + par) * 4 + i
                cols += list(range(64 * head, 64 * head + 64))
    return np.array(cols)


def slab(w):
    k, n = w.shape
    a = w.reshape(k // D, KT, P, n // 128, 128).transpose(0, 3, 2, 1, 4)
    return np.ascontiguousarray(a).reshape(k // D * (n // 128), P, KT * 128)


def col(v):
    return v.reshape(-1, P).T


def layout(i):
    f = {}
    f["cst"] = constants()
    f["x"] = np.ascontiguousarray(i["x"][0].T.reshape(KT, P, T).transpose(1, 0, 2))
    f["w_ada"] = np.ascontiguousarray(
        i["w_ada"].reshape(2, 16, P, 6, 16, P).transpose(0, 3, 1, 2, 5, 4)).reshape(2, 6, 16, P, D)
    hc = head_columns()
    w_in = i["w_in"]
    gate = np.zeros((2, D, 128), np.float32)
    gate[:, :, 0:4] = w_in[:, :, 3072:3076]
    gate[:, :, 32:36] = w_in[:, :, 3076:3080]
    at = {"ka": 4104, "va": 4360, "q": 0, "k": 512, "v": 1024, "os": 2048}
    f["w_in"] = np.stack([slab(np.concatenate(
        [gate[l] if kind == "gate" else w_in[l][:, 3080 + hc[128 * n:128 * n + 128]] if kind == "qa"
         else w_in[l][:, at[kind] + 128 * n:at[kind] + 128 * n + 128] for kind, n in SLABS], axis=1))
        for l in range(2)])
    f["w_out"] = np.stack([slab(np.concatenate([i["w_out"][l][0:1024], i["w_out"][l][1024 + hc]]))
                           for l in range(2)])
    f["w_up"] = np.stack([slab(i["w_up"][l]) for l in range(2)])
    f["w_down"] = np.stack([slab(i["w_down"][l]) for l in range(2)])
    f["s5_w_in"] = slab(i["s5_w_in_2"][0])
    f["s5_w_glu"] = slab(i["s5_w_glu_2"][0])
    f["s5_w_out"] = slab(i["s5_w_out_2"][0])
    kv = i["kv_w_2"]
    pad = np.zeros((D, 128), np.float32)
    pad[:, 0:16] = kv[:, 4096:4112]
    f["kv_w"] = slab(np.concatenate([pad, kv[:, 0:4096]], axis=1))
    f["fox_w_in"] = slab(i["fox_w_in_2"][0])
    f["fox_w_out"] = slab(i["fox_w_out_2"][0])
    prm = np.zeros((P, N_PRM), np.float32)
    for l in range(2):
        b = PER_LAYER * l
        for off, name in ((PRE_MIX, "g_pre_mix"), (POST_MIX, "g_post_mix"), (PRE_MLP, "g_pre_mlp"),
                          (POST_MLP, "g_post_mlp")):
            prm[:, b + off:b + off + 16] = col(i[name][l])
        prm[:, b + B_ADA:b + B_ADA + 96] = col(i["b_ada"][l])
        prm[:, b + CONV_W:b + CONV_W + 32] = i["conv_w"][l].reshape(4, 8, P).transpose(2, 1, 0).reshape(P, 32)
        prm[:, b + CONV_B:b + CONV_B + 8] = col(i["conv_b"][l])
        prm[:, b + G_HEAD:b + G_HEAD + 8] = col(i["g_mlstm_head"][l].reshape(-1))
        prm[:, b + G_ATT:b + G_ATT + 8] = col(i["g_attn_out"][l][hc])
        prm[:, b + SINK:b + SINK + 16] = i["attn_sinks"][l][None, :]
        prm[0:4, b + GATE_B] = i["b_i"][l]
        prm[0:4, b + GATE_B + 1] = i["b_f"][l]
    for off, v in ((S5_PRE, i["norm_pre_2"][0]), (S5_POST, i["norm_post_2"][0]), (S5_D, i["s5_d_2"][0]),
                   (S5_BGLU, i["s5_b_glu_2"][0]), (KV_G, i["kv_norm_2"]), (FOX_PRE, i["norm_pre_2"][1]),
                   (FOX_POST, i["norm_post_2"][1]), (C_COL, i["c"][0])):
        prm[:, off:off + 16] = col(v)
    prm[0:16, KV_BF] = i["kv_b_f_2"]
    f["prm"] = prm

    def states(a):
        return a.reshape(64, 2, 64).transpose(1, 2, 0).reshape(P, 64)

    f["s5_ap"] = np.ascontiguousarray(np.stack(
        [states(i["s5_a_re_2"][0]), states(i["s5_a_im_2"][0]),
         states(np.broadcast_to(i["s5_log_dt_2"][0][:, None], (128, 64)))], axis=1))
    sc = []
    for name in ("s5_c_re_2", "s5_c_im_2"):
        c = i[name][0].reshape(64, 2, 16, 64).transpose(1, 3, 0, 2)
        sc.append(c.reshape(P, 64, 16))
    f["s5_c"] = np.ascontiguousarray(np.stack(sc, axis=1))
    sb = np.zeros((64, 2, 16, 2, 2, 64), np.float32)
    for ri, name in enumerate(("s5_b_re_2", "s5_b_im_2")):
        b = i[name][0].reshape(64, 2, 64, 16)
        for gh in range(2):
            sb[:, gh, :, ri, gh, :] = b[:, gh].transpose(0, 2, 1)
    f["s5_b"] = sb.reshape(16, P, 2, 128)
    sbt = np.zeros((16, 2, 64, 2, 4, 2, 16), np.float32)
    for ri, name in enumerate(("s5_b_re_2", "s5_b_im_2")):
        b = i[name][0].reshape(16, 4, 2, 64, 16)
        for gh in range(2):
            sbt[:, gh, :, ri, :, gh, :] = b[:, :, gh].transpose(0, 2, 1, 3)
    f["s5_bt"] = sbt.reshape(16, P, 2, 128)
    f["s5_mask"] = np.kron(np.eye(4), np.ones((32, 32)))
    return {k: np.ascontiguousarray(v, dtype=np.float32) for k, v in f.items()}


def kernel(**inputs):
    import concourse.bacc as _bacc
    from concourse.bass_utils import run_bass_kernel_spmd as _run

    arrays = layout({k: np.asarray(v) for k, v in inputs.items()})
    nc = _bacc.Bacc("TRN2", target_bir_lowering=False, num_devices=1, dynamic_dma_scratch_size=1024)
    d = {k: nc.dram_tensor(f"in_{k}", v.shape, F32, kind="ExternalInput").ap() for k, v in arrays.items()}
    out = nc.dram_tensor("out_x", (P, KT, T), F32, kind="ExternalOutput").ap()
    build(nc, d, out)
    r = _run(nc, [{f"in_{k}": v for k, v in arrays.items()}], core_ids=[0])
    got = r.results[0]["out_x"]
    return np.ascontiguousarray(np.asarray(got).transpose(1, 0, 2).reshape(D, T).T)[None]
```

```python
import numpy as np
from contextlib import ExitStack

import concourse.bass as bass
from concourse import mybir

F32 = mybir.dt.float32
F32R = mybir.dt.float32r
ALU = mybir.AluOpType
ACT = mybir.ActivationFunctionType
AX = mybir.AxisListType

P = 128
T = 256
KT = 16
D = 2048
BIG = -1e30
RING = 5
EARLY = 14
GAP = 2
EPS = 1e-6

PRE_MIX, POST_MIX, PRE_MLP, POST_MLP, B_ADA, CONV_W, CONV_B, G_HEAD, G_ATT, SINK, GATE_B = (
    0, 16, 32, 48, 64, 160, 192, 200, 208, 216, 232)
PER_LAYER = 234
S5_PRE, S5_POST, S5_D, S5_BGLU, KV_G, FOX_PRE, FOX_POST, C_COL, KV_BF = (
    2 * PER_LAYER + n for n in (0, 16, 32, 48, 64, 80, 96, 112, 128))
N_PRM = 2 * PER_LAYER + 129

IDENT, NDIST, MASKT, MASKF, N_CST = 0, 128, 512, 640, 1024


SLABS = ([("ka", 0), ("ka", 1), ("va", 0), ("va", 1), ("gate", 0)]
         + [s for h in range(4) for s in (("q", h), ("k", h), ("v", 2 * h), ("v", 2 * h + 1),
                                          ("qa", 2 * h), ("qa", 2 * h + 1))]
         + [("os", v) for v in range(8)])


class Lane:

    def __init__(self, sem):
        self.sem, self.n, self.items, self.seen = sem, 0, [], {}

    def need(self, waits):
        out = []
        for w in waits:
            if w is None:
                continue
            if isinstance(w, list):
                out += self.need(w)
            elif self.seen.get(id(w[0]), 0) < w[1]:
                self.seen[id(w[0])] = w[1]
                out.append(w)
        return out

    def put(self, fn, *waits, sig=True):
        w = self.need(waits)
        if sig:
            self.n += 1
        self.items.append((w, fn, self.sem if sig else None, 1))
        return (self.sem, self.n)

    def dma(self, fn, sem, value, *waits):
        self.items.append((self.need(waits), fn, sem, 16))
        return (sem, value)

    def last(self):
        return (self.sem, self.n) if self.n else None

    def emit(self, eng):
        for waits, fn, sem, by in self.items:
            for s, v in waits:
                eng.wait_ge(s, v)
            ins = fn(eng)
            if sem is not None:
                ins.then_inc(sem, by)


class Slots:

    def __init__(self, items):
        self.items, self.free, self.order = items, [[] for _ in items], list(range(len(items)))

    def ready(self, n=1):
        return len(self.order) >= n

    def take(self):
        i = self.order.pop(0)
        return i, self.items[i], self.free[i]

    def give(self, i, *tokens):
        self.free[i] = list(tokens)
        self.order.append(i)


def build(nc, d, out):
    ctx = ExitStack()
    with ctx:
        base = (nc.sbuf_base + 63) // 64 * 64
        top = nc.sbuf_usable_end
        kb = 1024

        def at(name, shape, off, dt=F32):
            return nc.alloc_sbuf_tensor_at(name, (P, *shape), dt, offset=off)

        def psum(name):
            return ctx.enter_context(nc.psum_tensor(name, [P, 512], F32))

        def sem(name):
            return ctx.enter_context(nc.semaphore(name))

        o = base
        X = at("X", (KT, T), o); o += 16 * kb
        RAW = [at(f"raw{i}", (KT, 128), o + 8 * kb * i) for i in range(RING)]; o += 8 * kb * RING
        WH = [at(f"wh{i}", (KT, 128), o + 8 * kb * i, F32R) for i in range(2)]; o += 16 * kb
        WL = [at(f"wl{i}", (KT, 128), o + 8 * kb * i, F32R) for i in range(2)]; o += 16 * kb
        CST = at("cst", (N_CST,), o); o += 4 * N_CST
        PRM = at("prm", (N_PRM,), o); o += (4 * N_PRM + 63) // 64 * 64
        MOD = at("mod", (12, 16), o); o += 768
        ONES = at("ones", (256,), o); o += 1024
        SM = at("sm", (96,), o); o += 384
        RS = at("rs", (T,), o); o += 1024
        LN = at("ln", (T,), o); o += 1024
        A0 = o
        HH = at("HH", (KT, T), A0, F32R)
        HL = at("HL", (KT, T), A0 + 16 * kb, F32R)
        M = A0 + 32 * kb
        assert M + 92 * kb <= top, (M + 92 * kb, top)

        def m(name, shape, off, dt=F32):
            return at(name, shape, int(M + off * kb), dt)

        BK = [psum(f"bk{i}") for i in range(8)]
        ident = CST[:, IDENT:IDENT + 128]

        pe, act, dve, sp = (Lane(sem(f"s_{n}")) for n in ("pe", "act", "dve", "sp"))
        s_raw = [sem(f"s_raw{i}") for i in range(RING)]
        s_cst, s_prm, s_tab, s_out = (sem(f"s_{n}") for n in ("cst", "prm", "tab", "out"))
        s_row = [sem(f"s_row{i}") for i in range(2)]
        s_b = [sem(f"s_b{i}") for i in range(3)]
        s_bt = [sem(f"s_bt{i}") for i in range(2)]
        gbank = Slots([0, 1, 2])
        bbank = Slots([3, 4, 5, 6, 7])

        def mm(out_, l, r, start, stop, *waits, sig=False):
            return pe.put(lambda e: e.matmul(out_, l, r, start=start, stop=stop, skip_group_check=True),
                          *waits, sig=sig)

        def tr(out_, in_, *waits, sig=False):
            n = in_.shape[0]
            return pe.put(lambda e: e.transpose(out_, in_, ident[0:n, 0:n]), *waits, sig=sig)

        def fn(out_, in_, f, *waits, **kw):
            return act.put(lambda e: e.activation(out_, in_, f, **kw), *waits)

        def tt(out_, a, b, op, *waits):
            return dve.put(lambda e: e.tensor_tensor(out_, a, b, op), *waits)

        def ts(out_, a, s1, s2, op0, op1, *waits):
            if op1 is None:
                return dve.put(lambda e: e.tensor_scalar(out_, a, s1, None, op0), *waits)
            return dve.put(lambda e: e.tensor_scalar(out_, a, s1, s2, op0, op1), *waits)

        def stt(out_, a, s, b, op0, op1, *waits):
            return dve.put(lambda e: e.scalar_tensor_tensor(out_, a, s, b, op0, op1), *waits)

        def cp(out_, in_, *waits):
            return dve.put(lambda e: e.tensor_copy(out_, in_), *waits)

        def rec(out_, in_, *waits):
            return dve.put(lambda e: e.reciprocal(out_, in_), *waits)

        def bc(ap, n):
            return ap.rearrange("p (a t) -> p a t", a=1).to_broadcast([ap.shape[0], n, ap.shape[1]])

        def fence():
            return [t for t in (pe.last(), act.last(), dve.last()) if t]

        stream = []

        def ada(l, piece):
            return [("ada", d["w_ada"][l, piece, k], (l, piece, k)) for k in range(16)]

        def slabs(w, idx):
            return [("w", w[i], None) for i in idx]

        def blend(a, b):
            out_, n = [], 0
            for i, s in enumerate(a):
                out_.append(s)
                while n < len(b) and (n + 1) * len(a) <= (i + 1) * len(b):
                    out_ += [b[n]] if b[n] else []
                    n += 1
            return out_ + [v for v in b[n:] if v]

        def apart(*pieces):
            return [v for p in pieces if p for v in p + [None] * GAP]

        SHIFT_A, SCALE_A, GATE_A, SHIFT_M, SCALE_M, GATE_M = range(6)
        stream += ada(0, SCALE_A) + ada(0, SHIFT_A)
        mlp_order = [n for j in range(4) for n in [("u", 16 * j + i) for i in range(16)]
                     + [("d", 16 * j + i) for i in range(16)]]
        for l in range(2):
            mods = apart(ada(l, GATE_A) * (l == 0), ada(l, SCALE_M), ada(l, SHIFT_M))
            stream += blend(slabs(d["w_in"][l], range(37)), mods[:-EARLY])
            stream += blend(slabs(d["w_out"][l], range(16)), mods[-EARLY:])
            up_down = [("w", d["w_up" if k == "u" else "w_down"][l, i], None) for k, i in mlp_order]
            stream += blend(up_down, apart(ada(l, GATE_M), *((ada(1, p_) for p_ in (SCALE_A, SHIFT_A, GATE_A)) if l == 0 else ())))
        stream += slabs(d["s5_w_in"], range(32))
        stream += slabs(d["s5_w_glu"], range(16))
        stream += slabs(d["s5_w_out"], range(16))
        stream += slabs(d["kv_w"], range(33))
        stream += slabs(d["fox_w_in"], range(32))
        stream += slabs(d["fox_w_out"], range(16))

        raw_free = [[] for _ in range(RING)]
        loaded, staged_at = [0], [0]
        wslots = Slots([0, 1])
        ready = []
        tasks = {"scan": [], "tr": [], "ada": [], "att": [], "mix": []}
        WIDTH = {"scan": 4, "tr": 4, "ada": 1, "att": 2, "mix": 1}
        later = set()

        def load_next():
            n = loaded[0]
            if n >= len(stream):
                return
            loaded[0] += 1
            s = n % RING
            dst = RAW[s][:, :, :].rearrange("p a b -> p (a b)")
            sp.dma(lambda e, dst=dst, src=stream[n][1]: e.dma_start(dst, src), s_raw[s],
                   16 * (n // RING + 1), raw_free[s])

        ACC = m("acc", (D,), 80)
        ROW = m("row", (2, 512), 88)
        acc_tok, acc_read, acc_gen = [None], [True], [None]
        row_n = [0, 0]
        row_free = [None, None]
        mod_ready = {}

        def grab(n=1):
            while not bbank.ready(n):
                yield
            return [bbank.take() for _ in range(n)]

        def finish_ada(l, piece, tok):
            toks = []
            col = MOD[:, 6 * l + piece, :]
            total, direct = col, l == 0 and piece in (SCALE_A, SHIFT_A)
            if direct:
                (i, b, free), = yield from grab()
                for k in range(16):
                    t = mm(BK[b][:, k:k + 1], ACC[:, k::16], ONES[:, 0:1], True, True, tok, free, ones_tok,
                           sig=k == 15)
                acc_tok[0] = t
                acc_read[0] = True
                total, toks = BK[b][:, 0:16], t
            if not direct:
                yield True
            for c in range(4 * direct, 4):
                (i, b, free), = yield from grab()
                r_ = c % 2
                t = mm(BK[b][0:1, :], ONES[:, 0:1], ACC[:, 512 * c:512 * c + 512], True, True,
                       tok, free, ones_tok, sig=True)
                acc_tok[0] = t
                acc_read[0] = c == 3
                yield
                last = fn(ROW[0:1, r_, :], BK[b][0:1, :], ACT.Copy, t, row_free[r_])
                bbank.give(i, last)
                row_n[r_] += 1
                dst = MOD[32 * c:32 * c + 32, 6 * l + piece, :]
                src = ROW[0:1, r_, :].rearrange("o (p k) -> o p k", k=16)
                t = act.dma(lambda e, dst=dst, src=src: e.dma_start(dst, src), s_row[r_], 16 * row_n[r_], last)
                row_free[r_] = t
                toks.append(t)
            if not direct:
                yield
                yield
            b0 = PER_LAYER * l + B_ADA + 16 * piece
            t = tt(col, total, PRM[:, b0:b0 + 16], ALU.add, toks, prm_tok)
            if direct:
                bbank.give(i, t)
            if piece in (SCALE_A, SCALE_M):
                g = PER_LAYER * l + (PRE_MIX if piece == SCALE_A else PRE_MLP)
                t = stt(col, col, 1.0, PRM[:, g:g + 16], ALU.add, ALU.mult, t)
            if piece in (GATE_A, GATE_M):
                g = PER_LAYER * l + (POST_MIX if piece == GATE_A else POST_MLP)
                t = tt(col, col, PRM[:, g:g + 16], ALU.mult, t)
            mod_ready[(l, piece)] = t

        def stage_next():
            n = staged_at[0]
            if n >= len(stream):
                return
            staged_at[0] += 1
            kind, _, key = stream[n]
            s = n % RING
            here = (s_raw[s], 16 * (n // RING + 1))
            if kind == "ada":
                l, piece, k = key
                raw = RAW[s][:, :, :].rearrange("p a b -> p (a b)")
                if k == 0:
                    while not acc_read[0]:
                        pump()
                    t = ts(ACC[:, :], raw, CA[:, 0:1], None, ALU.mult, None, here, ca_tok, acc_tok[0])
                else:
                    t = stt(ACC[:, :], raw, CA[:, k:k + 1], ACC[:, :], ALU.mult, ALU.add, here, dve.last())
                raw_free[s] = [t]
                if k == 15:
                    acc_read[0] = False
                    acc_gen[0] = finish_ada(l, piece, t)
                    tasks["ada"].append(acc_gen[0])
            else:
                i, w, free = wslots.take()
                th = fn(WH[w][:, :, :], RAW[s][:, :, :], ACT.Copy, here, free)
                tl = tt(WL[w][:, :, :], RAW[s][:, :, :], WH[w][:, :, :].bitcast(F32), ALU.subtract, here, th, free)
                raw_free[s] = [th, tl]
                ready.append((i, w, [th, tl]))
            load_next()

        def pump(n=1):
            for r in range(n):
                for kind in tasks:
                    for g in tasks[kind][:WIDTH[kind]]:
                        if r and g in later:
                            continue
                        later.discard(g)
                        try:
                            if next(g):
                                later.add(g)
                        except StopIteration:
                            tasks[kind].remove(g)

        def idle():
            return not any(tasks.values())

        def drain():
            while not idle():
                pump()

        def bank():
            while not bbank.ready():
                pump()
            return bbank.take()

        def want_mod(key):
            while key not in mod_ready:
                if not idle():
                    pump()
                else:
                    stage_next()
            return mod_ready[key]

        def gemm(count, xh, xl, xready, evac, each=1, korder=None):
            order = korder or range(KT)
            pending = None
            for n in range(count):
                while not ready:
                    stage_next()
                i, w, wt = ready.pop(0)
                g, b, free = gbank.take()
                ps = BK[b][:, 0:T]
                for q, k in enumerate(order):
                    mm(ps, WH[w][:, k, :], xh(k), q == 0, False, wt[0], free, xready(k))
                    mm(ps, WH[w][:, k, :], xl(k), False, False)
                for q, k in enumerate(order):
                    t = mm(ps, WL[w][:, k, :], xh(k), False, q == KT - 1, wt[1], sig=q == KT - 1)
                wslots.give(i, t)
                while not ready and staged_at[0] < len(stream):
                    stage_next()
                if pending:
                    gbank.give(pending[0], evac(*pending[1:]))
                pending = (g, n, ps, t)
                pump(each)
            gbank.give(pending[0], evac(*pending[1:]))
            return t

        Xf = X[:, :, :]
        cst_tok = sp.dma(lambda e: e.dma_start(CST[:, :], d["cst"]), s_cst, 16)
        prm_tok = sp.dma(lambda e: e.dma_start(PRM[:, :], d["prm"]), s_prm, 16)
        for _ in range(RING):
            load_next()
        x_tok = act.dma(lambda e: e.dma_start(Xf, d["x"]), s_tab, 16)
        ones_tok = dve.put(lambda e: e.memset(ONES[:, :], 1.0))
        pe.need([cst_tok, ones_tok])
        pe.items.append(([cst_tok, ones_tok], lambda e: e.wait_ge(s_cst, 16), None, 0))

        CA, CE = SM[:, 16:32], SM[:, 32:48]
        ccol = PRM[:, C_COL:C_COL + 16]
        t = fn(CE, ccol, ACT.Exp, prm_tok, scale=-1.0)
        t = ts(CE, CE, 1.0, None, ALU.add, None, t)
        t = rec(CE, CE, t)
        ca_tok = tt(CA, CE, ccol, ALU.mult, t, prm_tok)

        SQ = m("sq", (KT, T), 60)

        def stats(*waits):
            i, b, free = bank()
            for k in range(KT):
                t = fn(SQ[:, k, :], X[:, k, :], ACT.Square, *waits)
                t = mm(BK[b][:, 0:T], ONES[:, 0:128], SQ[:, k, :], k == 0, k == KT - 1, t, free, sig=k == KT - 1)
            t = rsqrt(RS[:, :], BK[b][:, 0:T], D, LN[:, :], t)
            bbank.give(i, act.last())
            return t

        def rsqrt(out_, in_, n, tmp, *waits):
            t = fn(tmp, in_, ACT.Ln, *waits, scale=1.0 / n, bias=EPSC[:, :])
            return fn(out_, tmp, ACT.Exp, t, scale=-0.5)

        EPSC, EPSC4 = SM[:, 0:1], SM[:, 1:2]
        dve.put(lambda e: e.memset(EPSC4, 4.0 * EPS))
        eps_tok = dve.put(lambda e: e.memset(EPSC, EPS))
        act.items.append((act.need([eps_tok]), lambda e: e.wait_ge(dve.sem, eps_tok[1]), None, 0))

        def scaled(gs, toks, *waits):
            for k in range(KT):
                yield
                toks.append(stt(SQ[:, k, :], X[:, k, :], gs[:, k:k + 1], RS[:, :], ALU.mult, ALU.mult, *waits))

        def to_h(gs, sh, ts_, *waits, early=None):
            toks, hi = [], {}
            for k in range(KT + 2):
                if k < KT:
                    t = early[k] if early else stt(SQ[:, k, :], X[:, k, :], gs[:, k:k + 1], RS[:, :],
                                                   ALU.mult, ALU.mult, ts_, *waits)
                    if sh is None:
                        hi[k] = fn(HH[:, k, :], SQ[:, k, :], ACT.Copy, t, *waits)
                    else:
                        hi[k] = fn(HH[:, k, :], SQ[:, k, :], ACT.Identity, t, *waits, bias=sh[:, k:k + 1])
                if k >= 2:
                    j = k - 2
                    hf = HH[:, j, :].bitcast(F32)
                    if sh is None:
                        t = tt(HL[:, j, :], SQ[:, j, :], hf, ALU.subtract, hi[j])
                    else:
                        t = stt(HL[:, j, :], SQ[:, j, :], sh[:, j:j + 1], hf, ALU.add, ALU.subtract, hi[j])
                    toks.append([hi[j], t])
            return toks

        class Squares:

            def __init__(self, off, name, *waits):
                self.t = [m(f"{name}{i}", (T,), off + i) for i in range(3)]
                self.n, self.tok, self.waits = 0, None, list(waits)

            def add(self, src, *waits, scale=1.0):
                s = self.t[0] if self.n == 0 else self.t[1 + self.n % 2]
                prev = self.tok[1] if self.n > 2 else None
                t = fn(s[:, :], src, ACT.Square, *waits, prev, self.waits, scale=scale)
                if self.n:
                    u = tt(self.t[0][:, :], self.t[0][:, :], s[:, :], ALU.add, t, self.tok[0])
                    self.tok = [u, self.tok[0]]
                else:
                    self.tok = [t, None]
                self.n += 1
                return t

        def add_y(Y, gg, gtok, sq, *waits, norm=True):
            i, b, free = bank()
            t = mm(BK[b][:, 0:T], ONES[:, 0:128], sq.t[0][:, :], True, True, sq.tok[0], free, sig=True)
            t0 = rsqrt(RS[:, :], BK[b][:, 0:T], D, LN[:, :], t, *waits)
            bbank.give(i, t0)
            i, b, free = bank()
            st, xs = [], []
            for k in range(KT + 1):
                if k < KT:
                    st.append(stt(SQ[:, k, :], Y[:, k, :], gg[:, k:k + 1], RS[:, :], ALU.mult, ALU.mult,
                                  t0, gtok, *waits))
                if k:
                    j = k - 1
                    t = tt(X[:, j, :], SQ[:, j, :], X[:, j, :], ALU.add, st[j])
                    xs.append(t)
                    if norm:
                        t = fn(SQ[:, j, :], X[:, j, :], ACT.Square, t)
                        t = mm(BK[b][:, 0:T], ONES[:, 0:128], SQ[:, j, :], j == 0, j == KT - 1, t, free,
                               sig=j == KT - 1)
            if norm:
                t = rsqrt(RS[:, :], BK[b][:, 0:T], D, LN[:, :], t, st[-1])
            bbank.give(i, t)
            return xs, t

        def split(hi, lo, src, *waits):
            th = fn(hi, src, ACT.Copy, *waits)
            tl = tt(lo, src, hi.bitcast(F32), ALU.subtract, th, *waits)
            return [th, tl]

        QA = m("qa", (8, T), 0)
        QAL = m("qal", (8, T), 0, F32R)
        KA = m("ka", (2, T), 8)
        VA = m("va", (2, T), 10)
        QM = m("qm", (4, T), 12)
        KM = m("km", (4, T), 16)
        VM = m("vm", (2, 1024), 20)
        OS = m("os", (8, T), 28)
        OSL = m("osl", (8, T), 28, F32R)
        AHI = m("ahi", (8, T), 36, F32R)
        MHI = m("mhi", (8, T), 44, F32R)
        S0 = 52
        Y1 = m("y1", (KT, T), 12)
        CV = [m(f"cv{i}", (3 + T,), S0 + 1.125 * i) for i in range(2)]
        CO = [m(f"co{i}", (T,), S0 + 2.25 + i) for i in range(2)]
        TV = [m(f"tv{i}", (T,), S0 + 4.25 + i) for i in range(2)]
        EV = [m(f"ev{i}", (T,), S0 + 6.25 + i) for i in range(2)]
        GI = m("gi", (T,), S0 + 8.25)
        GF = m("gf", (T,), S0 + 9.25)
        GT = m("gt", (T,), S0 + 10.25)
        GR = m("gr", (2, T), S0 + 11.25)
        AC = m("ac", (2, 4), S0 + 13.25)
        DN, EM = GF, GT
        E0 = m("e0", (384,), S0 + 13.5)
        HN = m("hn", (2, T), S0 + 15)
        HS = m("hs", (2, T), S0 + 17)
        MF = m("mf", (8, T), 44)
        HG = m("hg", (2, T), 20)
        TA = [[m(f"ta{i}{j}", (384,), S0 + 19 + 3 * i + 1.5 * j) for j in range(2)] for i in range(2)]
        ASS = m("ass", (T,), S0 + 25)
        ARS = m("ars", (T,), S0 + 26)

        def transposed(dst, src, got, *waits):
            yield True
            yield True
            (i, b, free), = yield from grab()
            tr(BK[b][:, 0:128], src[:, 0:128], *waits, free)
            t = tr(BK[b][:, 128:256], src[:, 128:256], sig=True)
            yield
            t = cp(dst, BK[b][:, 0:256].rearrange("p (a f) -> p a f", a=2), t)
            bbank.give(i, t)
            got(t)

        def fetch(table, key):
            while key not in table:
                pump()
            return table[key]

        def await_(table, *keys):
            while not all(key in table for key in keys):
                yield


        def conv_evac(l, n, ps, t, slot, dst, fr):
            cv, co, ev = CV[slot], CO[slot], EV[slot]
            w0 = PER_LAYER * l + CONV_W + 4 * n
            b0 = PER_LAYER * l + CONV_B + n
            t = fn(cv[:, 3:3 + T], ps, ACT.Copy, t, fr)
            free = t
            t = ts(co[:, :], cv[:, 0:T], PRM[:, w0:w0 + 1], PRM[:, b0:b0 + 1], ALU.mult, ALU.add, t)
            for j in range(1, 4):
                t = stt(co[:, :], cv[:, j:j + T], PRM[:, w0 + j:w0 + j + 1], co[:, :], ALU.mult, ALU.add, t)
            t = fn(ev[:, :], co[:, :], ACT.Tanh, t, scale=0.5)
            t = stt(dst, ev[:, :], 1.0, co[:, :], ALU.add, ALU.mult, t)
            return free, t

        def mixer(l, xtok, start_tok):
            prm = PER_LAYER * l
            tokv = {}
            zt = None
            for i in range(2):
                zt = dve.put(lambda e, i=i: e.memset(CV[i][:, 0:3], 0.0), start_tok)
            slot_tok = [zt, zt]
            last_tv = [None, None]

            def evac(n, ps, t):
                kind, i = SLABS[n]
                if kind == "ka":
                    r = fn(KA[:, i, :], ps, ACT.Copy, t, start_tok)
                    tokv["ka", i] = r
                elif kind in ("va", "v"):
                    s = i % 2
                    prev = fetch(tokv, last_tv[s]) if last_tv[s] else None
                    r = fn(TV[s][:, :], ps, ACT.Copy, t, prev, start_tok)
                    dst = VA if kind == "va" else VM
                    last_tv[s] = (kind, i)
                    tasks["tr"].append(transposed(dst[:, :, 128 * i:128 * i + 128], TV[s],
                                                  lambda t, key=(kind, i): tokv.update({key: t}), r))
                    if kind == "v" and s:
                        tasks["mix"].append(mlstm(i // 2))
                elif kind == "qa":
                    r = fn(QA[:, i, :], ps, ACT.Copy, t, start_tok)
                    tokv["qa", i] = r
                    tasks["att"].append(attention(i // 4, i % 4))
                    if i == 7:
                        tasks["att"].append(att_norm())
                elif kind == "gate":
                    cp(GI[0:4, :], ps[0:4, :], t, start_tok)
                    r = cp(GF[0:4, :], ps[32:36, :], t, start_tok)
                    tasks["tr"].append(gates(r))
                elif kind in ("q", "k"):
                    s = int(kind == "k")
                    dst = KM[:, i, :] if s else QM[:, i, :]
                    r, slot_tok[s] = conv_evac(l, i + 4 * s, ps, t, s, dst, slot_tok[s])
                    tokv[kind, i] = slot_tok[s]
                else:
                    r = tokv["os", i] = fn(OS[:, i, :], ps, ACT.Tanh, t, start_tok, scale=0.5)
                    if i % 2:
                        tasks["mix"].append(gated(i // 2))
                return r

            def gates(t):
                gi, gf, gt = GI[0:4, :], GF[0:4, :], GT[0:4, :]
                t = ts(gi, gi, PRM[0:4, prm + GATE_B:prm + GATE_B + 1], None, ALU.add, None, t)
                t = ts(gf, gf, PRM[0:4, prm + GATE_B + 1:prm + GATE_B + 2], None, ALU.add, None, t)
                t = fn(gt, gf, ACT.Abs, t)
                t = fn(gt, gt, ACT.Exp, t, scale=-1.0)
                t = fn(gt, gt, ACT.Ln, t, bias=1.0)
                t = stt(gf, gf, 0.0, gt, ALU.min, ALU.subtract, t)
                t = dve.put(lambda e: e.tensor_tensor_scan(gt, ONES[0:4, :], gf, 0.0, ALU.mult, ALU.add), t)
                t = tt(gi, gi, gt, ALU.subtract, t)
                t = dve.put(lambda e: e.tensor_tensor_scan(gf, ONES[0:4, :], gi, 0.0, ALU.mult, ALU.max), t)
                a_tok = t
                t = ts(GR[0:4, 0, :], gf, -1.0, None, ALU.mult, None, t)
                t = tt(gt, gt, gf, ALU.add, t)
                t = fn(GR[0:4, 1, :], gt, ACT.Exp, t, scale=-1.0)
                tokv["rows"] = t
                yield True
                yield True
                yield True
                (i, b, free), = yield from grab()
                tr(BK[b][:, 0:4], GI[0:4, 0:128], a_tok, free)
                t = tr(BK[b][:, 4:8], GI[0:4, 128:256], sig=True)
                yield
                t = cp(AC[:, :, :], BK[b][:, 0:8].rearrange("p (a h) -> p a h", a=2), t)
                bbank.give(i, t)
                tokv["acol"] = t

            def attention(pair, i):
                tile = 4 * pair + i
                u = tile % 2
                TT = TA[u]
                x0 = 64 + 16 * u
                yield from await_(tokv, ("va", 0), ("va", 1))
                wait = [tokv["qa", tile], tokv["ka", pair], tokv["va", 0], tokv["va", 1]]
                mx, nm, rs, es = (SM[:, x0 + 4 * n:x0 + 4 * n + 4] for n in range(4))
                prev = tokv.get(("att", u))
                held = yield from grab(2)
                st = []
                for par in range(2):
                    a = slice(64 * par, 64 * par + 64)
                    _, b, free = held[par]
                    mm(BK[b][:, 0:256], QA[a, tile, 128:256], KA[a, pair, :], True, True, *wait, free)
                    st.append(mm(BK[b][:, 256:384], QA[a, tile, 0:128], KA[a, pair, 0:128], True, True, sig=True))
                yield
                t = None
                for par in range(2):
                    head = (2 * pair + par) * 4 + i
                    bi, b, _ = held[par]
                    slope = 2.0 ** (-8.0 * (head + 1) / 16) * 8.0
                    t = stt(TT[par][:, :], CST[:, NDIST:NDIST + 384], slope, BK[b][:, 0:384],
                            ALU.mult, ALU.add, st[par], prev, start_tok)
                    bbank.give(bi, t)
                for par in range(2):
                    for j, q in ((0, slice(0, 256)), (1, slice(256, 384))):
                        c = 2 * par + j
                        t = dve.put(lambda e, c=c, q=q, par=par: e.tensor_reduce(
                            mx[:, c:c + 1], TT[par][:, q], AX.X, ALU.max), t)
                for par in range(2):
                    head = (2 * pair + par) * 4 + i
                    sk = PRM[:, prm + SINK + head:prm + SINK + head + 1]
                    t2 = ts(nm[:, 2 * par:2 * par + 2], mx[:, 2 * par:2 * par + 2], 0.125, sk,
                            ALU.mult, ALU.max, t, prev)
                tm = ts(nm, nm, -1.0, None, ALU.mult, None, t2)
                yield
                for par in range(2):
                    head = (2 * pair + par) * 4 + i
                    sk = PRM[:, prm + SINK + head:prm + SINK + head + 1]
                    for blk, s in ((0, slice(0, 256)), (1, slice(256, 384))):
                        c = 2 * par + blk
                        fn(TT[par][:, s], TT[par][:, s], ACT.Exp, tm, scale=0.125,
                           bias=nm[:, c:c + 1], accum_out=rs[:, c:c + 1])
                    te = fn(es[:, 2 * par:2 * par + 2], nm[:, 2 * par:2 * par + 2], ACT.Exp, bias=sk)
                yield
                t = tt(rs, rs, es, ALU.add, te)
                t = rec(rs, rs, t)
                for par in range(2):
                    for blk, s in ((0, slice(0, 256)), (1, slice(256, 384))):
                        c = 2 * par + blk
                        tn = ts(TT[par][:, s], TT[par][:, s], rs[:, c:c + 1], None, ALU.mult, None, t)
                yield True
                held = yield from grab(2)
                st = []
                for par in range(2):
                    _, b, fr = held[par]
                    tr(BK[b][:, 0:128], TT[par][:, 256:384], tn, fr)
                    tr(BK[b][:, 128:256], TT[par][:, 0:128])
                    st.append(tr(BK[b][:, 256:384], TT[par][:, 128:256], sig=True))
                yield
                c1 = fn(TT[0][:, :], BK[held[0][1]][:, 0:384], ACT.Copy, st[0])
                bbank.give(held[0][0], c1)
                c2 = cp(TT[1][:, :], BK[held[1][1]][:, 0:384], st[1])
                bbank.give(held[1][0], c2)
                yield True
                (bo, bout, free), = yield from grab()
                for par in range(2):
                    v = slice((2 * pair + par) * 64, (2 * pair + par) * 64 + 64)
                    a = slice(64 * par, 64 * par + 64)
                    mm(BK[bout][a, 0:256], VA[:, 0, v], TT[par][:, 0:256], True, False, c1, c2, free)
                    t = mm(BK[bout][a, 128:256], VA[:, 1, v], TT[par][:, 256:384], False, True, sig=True)
                yield
                q = fn(QA[:, tile, :], BK[bout][:, 0:256], ACT.Copy, t)
                bbank.give(bo, q)
                if tile == 0:
                    t = fn(ASS[:, :], QA[:, tile, :], ACT.Square, q, start_tok)
                    tokv["ass"] = t
                else:
                    t = fn(TT[0][:, 0:256], QA[:, tile, :], ACT.Square, q)
                    yield
                    t = tokv["ass"] = tt(ASS[:, :], ASS[:, :], TT[0][:, 0:256], ALU.add, t, tokv["ass"])
                tokv["att", u] = t

            def att_norm():
                while ("att", 1) not in tokv or len(tasks["att"]) > 1:
                    yield
                (i, b, free), = yield from grab()
                t = mm(BK[b][:, 0:T], ONES[:, 0:128], ASS[:, :], True, True,
                       tokv["ass"], tokv["att", 0], tokv["att", 1], free, sig=True)
                yield
                t0 = rsqrt(ARS[:, :], BK[b][:, 0:T], 1024, ARS[:, :], t, start_tok)
                bbank.give(i, t0)
                yield
                for k in range(8):
                    c = prm + G_ATT + k
                    t = stt(QA[:, k, :], QA[:, k, :], PRM[:, c:c + 1], ARS[:, :], ALU.mult, ALU.mult, t0)
                    yield
                    tokv["a_hl", k] = split(AHI[:, k, :], QAL[:, k, :], QA[:, k, :], t, start_tok)

            def mlstm(h):
                yield from await_(tokv, "acol", ("v", 2 * h), ("v", 2 * h + 1))
                (i1, b1, f1), (i2, b2, f2) = yield from grab(2)
                rowb = mm(BK[b1][:, :], ident[0:4, h:h + 1].to_broadcast([4, 128]),
                          GR[0:4, :, :].rearrange("p a t -> p (a t)"), True, True, tokv["rows"], f1, sig=True)
                sc = BK[b2]
                mm(sc[:, 0:256], KM[:, h, 0:128], QM[:, h, :], True, True, tokv["q", h], tokv["k", h], f2)
                st = mm(sc[:, 256:384], KM[:, h, 128:256], QM[:, h, 128:256], True, True, sig=True)
                yield
                prev = tokv.get("m_done")
                em = fn(EM[:, :], BK[b1][:, 256:512], ACT.Copy, rowb, prev, tokv["rows"])
                yield
                mk = CST[:, MASKT:MASKT + 128]
                stt(E0[:, 0:128], BK[b1][:, 0:128], AC[:, 0, h:h + 1], mk, ALU.add, ALU.add,
                    em, tokv["acol"], prev)
                t = stt(E0[:, 256:384], BK[b1][:, 128:256], AC[:, 1, h:h + 1], mk, ALU.add, ALU.add)
                yield
                t = fn(E0[:, 128:256], BK[b1][:, 128:256], ACT.Exp, t, bias=AC[:, 0, h:h + 1])
                bbank.give(i1, t)
                fn(E0[:, 0:128], E0[:, 0:128], ACT.Exp)
                t = fn(E0[:, 256:384], E0[:, 256:384], ACT.Exp)
                yield
                t = stt(E0[:, :], sc[:, 0:384], 0.25 * 128.0 ** -0.5, E0[:, :], ALU.mult, ALU.mult, t, st)
                bbank.give(i2, t)
                yield True
                (i3, b3, f3), (i4, b4, f4) = yield from grab(2)
                for j in range(2):
                    v = slice(256 * h + 128 * j, 256 * h + 128 * j + 128)
                    o0 = 256 * j
                    mm(BK[b3][:, o0:o0 + 256], VM[:, 0, v], E0[:, 0:256], True, False,
                       t, f3, tokv["v", 2 * h], tokv["v", 2 * h + 1])
                    nt = mm(BK[b3][:, o0 + 128:o0 + 256], VM[:, 1, v], E0[:, 256:384], False, True, sig=True)
                mm(BK[b4][:, 0:256], ONES[:, 0:128], E0[:, 0:256], True, False, f4)
                t = mm(BK[b4][:, 128:256], ONES[:, 0:128], E0[:, 256:384], False, True, sig=True)
                yield
                t = fn(DN[:, :], BK[b4][:, 0:256], ACT.Abs, t, prev, tokv["rows"])
                bbank.give(i4, t)
                yield
                t = tt(DN[:, :], DN[:, :], EM[:, :], ALU.max, t, em)
                t = rec(DN[:, :], DN[:, :], t)
                hn = tt(HN[:, :, :], BK[b3][:, :].rearrange("p (a t) -> p a t", a=2), bc(DN[:, :], 2),
                        ALU.mult, t, nt, prev)
                bbank.give(i3, hn)
                yield
                t = fn(HS[:, :, :], HN[:, :, :], ACT.Square, hn)
                yield True
                (i4, b4, f4), = yield from grab()
                mm(BK[b4][:, 0:256], ONES[:, 0:128], HS[:, 0, :], True, False, t, f4)
                t = mm(BK[b4][:, 0:256], ONES[:, 0:128], HS[:, 1, :], False, True, sig=True)
                yield
                t = fn(DN[:, :], BK[b4][:, 0:256], ACT.Ln, t, hn, scale=4.0 / 256, bias=EPSC4)
                t = fn(DN[:, :], DN[:, :], ACT.Exp, t, scale=-0.5)
                bbank.give(i4, t)
                yield
                for j in range(2):
                    c = prm + G_HEAD + 2 * h + j
                    t1 = stt(MF[:, 2 * h + j, :], HN[:, j, :], PRM[:, c:c + 1], DN[:, :],
                             ALU.mult, ALU.mult, t, start_tok)
                tokv["m_done"] = tokv["mf", h] = t1

            def gated(h):
                while ("mf", h) not in tokv:
                    yield
                q = slice(2 * h, 2 * h + 2)
                t = stt(HG[:, :, :], OS[:, q, :], 1.0, MF[:, q, :], ALU.add, ALU.mult, tokv["mf", h],
                        tokv["os", 2 * h], tokv["os", 2 * h + 1], tokv.get("hg"))
                yield
                tokv["m_hl", h] = split(MHI[:, q, :], OSL[:, q, :], HG[:, :, :], t, start_tok)
                tokv["hg"] = tokv["m_hl", h][1]

            return evac, tokv

        AP_ = m("ap", (12, 64), 0)
        CR = m("cr", (2, 64, 16), 4)
        CT = [m(f"ct{i}", (64, 16), 65 + 4 * i) for i in range(3)]
        a_re, a_im, ldt, dt_, mag, th, sn, cs, arr, t8, t9, t10 = (AP_[:, i, :] for i in range(12))
        cre, cim = CR[:, 0, :, :], CR[:, 1, :, :]
        s5 = {}

        def over_c(ap):
            return ap.rearrange("p (g c) -> p g c", c=1).to_broadcast([P, 64, 16])

        def parameters(f):
            sp.dma(lambda e: e.dma_start(AP_[:, 0:3, :], d["s5_ap"]), s_tab, 32, f)
            tab_tok = sp.dma(lambda e: e.dma_start(CR[:, :, :, :], d["s5_c"]), s_tab, 48, f)
            yield
            t = fn(dt_, ldt, ACT.Exp, tab_tok)
            t = tt(mag, a_re, dt_, ALU.mult, t)
            t = fn(mag, mag, ACT.Exp, t)
            mag_t = t
            t = tt(th, a_im, dt_, ALU.mult, dve.last())
            TWO_PI = 2.0 * np.pi
            C1 = float(np.float32(6.28125))
            C2_ = float(np.float32(TWO_PI - 6.28125))
            C3_ = float(TWO_PI - C1 - C2_)
            MAGIC = float(1.5 * 2 ** 23)

            def reduced(dst, src, add, *waits):
                t = ts(t8, src, add, 1.0 / TWO_PI, ALU.add, ALU.mult, *waits)
                t = ts(t8, t8, MAGIC, None, ALU.add, None, t)
                t = ts(t8, t8, -MAGIC, None, ALU.add, None, t)
                t = stt(dst, t8, -C1, src, ALU.mult, ALU.add, t)
                t = stt(dst, t8, -C2_, dst, ALU.mult, ALU.add, t)
                t = stt(dst, t8, -C3_, dst, ALU.mult, ALU.add, t)
                t = ts(dst, dst, add, float(np.float32(np.pi) - np.float32(2e-7)), ALU.add, ALU.min, t)
                return ts(dst, dst, -float(np.float32(np.pi) - np.float32(2e-7)), None, ALU.max, None, t)

            yield
            t = reduced(sn, th, 0.0, t)
            yield
            t = reduced(cs, th, float(np.pi / 2), t)
            yield
            t = fn(sn, sn, ACT.Sin, t)
            t = fn(cs, cs, ACT.Sin, t)
            t = tt(cs, cs, mag, ALU.mult, t, mag_t)
            t = tt(sn, sn, mag, ALU.mult, t)
            s5["a"] = t
            yield
            t = ts(arr, cs, -1.0, None, ALU.add, None, t)
            t = tt(t8, a_re, a_re, ALU.mult, t)
            t = tt(t9, a_im, a_im, ALU.mult, t)
            t = tt(t8, t8, t9, ALU.add, t)
            t = rec(t8, t8, t)
            t = tt(t9, arr, a_re, ALU.mult, t)
            t = tt(t10, sn, a_im, ALU.mult, t)
            t = tt(t9, t9, t10, ALU.add, t)
            t = tt(t9, t9, t8, ALU.mult, t)
            t = tt(t10, sn, a_re, ALU.mult, t)
            t = tt(arr, arr, a_im, ALU.mult, t)
            t = tt(t10, t10, arr, ALU.subtract, t)
            t = tt(t10, t10, t8, ALU.mult, t)
            yield
            t = tt(CT[0][:, :, :], cre, over_c(t9), ALU.mult, t, tab_tok, f)
            yield
            t = tt(CT[1][:, :, :], cim, over_c(t10), ALU.mult, t)
            yield
            t = tt(CT[2][:, :, :], cre, over_c(t10), ALU.mult, t)
            yield
            t = tt(cre, CT[0][:, :, :], CT[1][:, :, :], ALU.subtract, t)
            yield
            t = tt(cim, cim, over_c(t9), ALU.mult, t)
            yield
            s5["c"] = stt(cim, cim, -1.0, CT[2][:, :, :], ALU.mult, ALU.subtract, t)

        HBH = m("hbh", (KT, T), 28, F32R)
        HBL = m("hbl", (KT, T), 44, F32R)
        UR = [m(f"ur{i}", (T,), 60 + i) for i in range(2)]

        def first_layer(l, x_ready):
            t0 = x_ready
            want_mod((l, SCALE_A))
            want_mod((l, SHIFT_A))
            gs, sh, gg = (MOD[:, 6 * l + p_, :] for p_ in (SCALE_A, SHIFT_A, GATE_A))
            xt = to_h(gs, sh, [mod_ready[l, SCALE_A], mod_ready[l, SHIFT_A]], t0)
            start = fence()
            evac, tokv = mixer(l, xt, start)
            gemm(37, lambda k: HH[:, k, :], lambda k: HL[:, k, :], lambda k: xt[k], evac, each=2)
            while tasks["att"] or tasks["mix"]:
                pump()

            def xh(k):
                return MHI[:, k, :] if k < 8 else AHI[:, k - 8, :]

            def xl(k):
                return OSL[:, k, :] if k < 8 else QAL[:, k - 8, :]

            def xr(k):
                return tokv["m_hl", k // 2] if k < 8 else tokv["a_hl", k - 8]

            f = fence()
            yt = []

            sq = Squares(62, f"ya{l}", f)

            def yevac(n, ps, t):
                yt.append(fn(Y1[:, n, :], ps, ACT.Copy, t, f))
                return sq.add(ps, t)

            gemm(16, xh, xl, xr, yevac, korder=list(range(8, 16)) + list(range(8)))
            gt = want_mod((l, GATE_A))
            _, t0 = add_y(Y1, gg, gt, sq, fence())
            want_mod((l, SCALE_M))
            want_mod((l, SHIFT_M))
            gs, sh, gg = (MOD[:, 6 * l + p_, :] for p_ in (SCALE_M, SHIFT_M, GATE_M))
            xt = to_h(gs, sh, [mod_ready[l, SCALE_M], mod_ready[l, SHIFT_M]], t0)
            f = fence()
            ht = {}
            ur = Slots(UR)
            yprev = [None] * KT
            pe_done = [f]
            sq2 = Squares(62, f"yb{l}", f)
            if l:
                tasks["mix"].append(parameters(f))

            def up_evac(n, ps, t):
                i, u, free = ur.take()
                r = fn(u[:, :], ps, ACT.Relu, t, free, pe_done[0])
                t1 = tt(u[:, :], u[:, :], u[:, :], ALU.mult, r)
                ht[n] = split(HBH[:, n, :], HBL[:, n, :], u[:, :], t1, pe_done[0])
                ur.give(i, *ht[n])
                return r

            def down_evac(n, ps, t):
                if yprev[n] is None:
                    yprev[n] = fn(Y1[:, n, :], ps, ACT.Copy, t, f)
                else:
                    yprev[n] = tt(Y1[:, n, :], ps, Y1[:, n, :], ALU.add, t, yprev[n])
                if j_now[0] == 3:
                    sq2.add(Y1[:, n, :], yprev[n])
                return yprev[n]

            j_now = [0]
            for j in range(4):
                j_now[0] = j
                gemm(16, lambda k: HH[:, k, :], lambda k: HL[:, k, :], lambda k: xt[k], up_evac)
                h_now = dict(ht)
                t = gemm(16, lambda k: HBH[:, k, :], lambda k: HBL[:, k, :], lambda k: h_now[k], down_evac)
                pe_done[0] = t
            gt = want_mod((l, GATE_M))
            return add_y(Y1, gg, gt, sq2, fence())[1]

        xt_ = stats(x_tok)
        while staged_at[0] < 33:
            if acc_read[0] or stream[staged_at[0]][2][2]:
                stage_next()
            if staged_at[0] == 32:
                stage_next()
            pump()
        for l in range(2):
            xt_ = first_layer(l, xt_)
        drain()

        H = m("Hst", (129, 2, 64), 0)
        C1 = m("c1", (2, 64, 16), 12)
        C2 = m("c2", (64, 16), 20)
        CC = m("cc", (2, 64, 2, 32), 24)
        BT = [m(f"bt{i}", (2, 128), 56 + i) for i in range(2)]
        MASKB = m("maskb", (128,), 58)
        U = m("u", (KT, T), 64.5)
        K0 = m("k0", (KT, 128), 80.5)
        TAB = m("tab", (2, 2, 64), 88.5)
        PR = m("pr", (2, 2, 64), 89.5)
        SS = m("ss", (2, 64), 90.5)
        AT = m("atr", (256,), 91)
        Z = at("z", (KT, T), base)
        BS = [at(f"bs{i}", (2, 128), base + i * kb) for i in range(3)]
        AB = [at(f"ab{i}", (2, 128), base + (3 + i) * kb) for i in range(3)]
        AQ = [at(f"aq{i}", (2, 2, 128), base + (6 + 2 * i) * kb) for i in range(2)]
        SEL = [at(f"sel{i}", (4, 32), base + 10 * kb + 512 * i) for i in range(2)]
        CL = at("cl", (2, 64, 2, 32), A0)
        x_keep = nc.dram_tensor("x_keep", (P, KT, T), F32, kind="Internal").ap()
        c_keep = nc.dram_tensor("c_keep", (4, P, 2, 16, 2, 32), F32, kind="Internal").ap()
        s_keep, s_cc = sem("s_keep"), sem("s_cc")
        s_cl = [sem(f"s_cl{i}") for i in range(4)]

        f0 = fence()
        mask_tok = sp.dma(lambda e: e.dma_start(MASKB[:, :], d["s5_mask"]), s_tab, 64, f0)
        xt = to_h(PRM[:, S5_PRE:S5_PRE + 16], None, None, xt_, f0)
        f = fence()
        x_kept = sp.dma(lambda e: e.dma_start(x_keep, Xf), s_keep, 16, f)
        uz = {}

        def u_evac(n, ps, t):
            uz[n] = fn(U[:, n, :], ps, ACT.Copy, t, f)
            return uz[n]

        def tables():
            t = s5["a"]
            tt(t8, cs, cs, ALU.mult, t, s5["c"])
            tt(t9, sn, sn, ALU.mult)
            t1 = tt(t10, cs, sn, ALU.mult)
            tt(TAB[:, 0, 0, :], t8, t9, ALU.subtract, t1, f)
            tt(TAB[:, 0, 1, :], t8, t9, ALU.subtract)
            ts(TAB[:, 1, 0, :], t10, 2.0, None, ALU.mult, None)
            s5["tab"] = ts(TAB[:, 1, 1, :], t10, -2.0, None, ALU.mult, None)

            def blocks(kind, src, t):
                for gh in range(2):
                    yield
                    for ri in range(2):
                        t = fn(CC[64 * gh:64 * gh + 64, kind, :, ri, 16 * gh:16 * gh + 16],
                               src[64 * gh:64 * gh + 64, ri, :, :], ACT.Copy, t)
                return t

            btf, btn = [None, None], [0, 0]

            def load_bt(q):
                j = q % 2
                btn[j] += 16
                return sp.dma(lambda e: e.dma_start(BT[j][:, :, :], d["s5_bt"][q]), s_bt[j], btn[j], btf[j], f)

            bt_tok = [load_bt(0), load_bt(1)]
            zt = [None, None]
            for kind in range(2):
                for c in range(4):
                    yield
                    zt[kind] = dve.put(lambda e, kind=kind, c=c: e.memset(
                        CC[:, kind, 16 * c:16 * c + 16, :, :], 0.0), f)
                if not kind:
                    s5["cb"] = yield from blocks(0, CR, [zt[0], s5["c"]])
            yield
            t = tt(C1[:, 0, :, :], cre, over_c(cs), ALU.mult, f, s5["c"])
            yield
            t = tt(C2[:, :, :], cim, over_c(sn), ALU.mult, t)
            yield
            t = tt(C1[:, 0, :, :], C1[:, 0, :, :], C2[:, :, :], ALU.add, t)
            yield
            t = tt(C1[:, 1, :, :], cim, over_c(cs), ALU.mult, t)
            yield
            t = tt(C2[:, :, :], cre, over_c(sn), ALU.mult, t)
            yield
            t = tt(C1[:, 1, :, :], C1[:, 1, :, :], C2[:, :, :], ALU.subtract, t)
            yield
            t = yield from blocks(1, C1, [t, zt[1]])
            yield True
            (i, b, free), = yield from grab()
            tr(BK[b][0:64, 0:128], cs, s5["a"], free)
            t2 = tr(BK[b][0:64, 128:256], sn, sig=True)
            yield
            s5["at"] = fn(AT[0:64, :], BK[b][0:64, 0:256], ACT.Copy, t2, f)
            bbank.give(i, s5["at"])
            for q in range(16):
                j = q % 2
                if q % 4 == 1:
                    c = q // 4
                    s5["cc"] = act.dma(lambda e, c=c: e.dma_start(c_keep[c], CC[:, :, 16 * c:16 * c + 16, :, :]),
                                       s_cc, 16 * (c + 1), t)
                (i, b, free), = yield from grab()
                for ri in range(2):
                    t1 = mm(BK[b][:, 0:128], BT[j][:, ri, :], CC[:, 0, 4 * q:4 * q + 4, ri, :], ri == 0, ri == 1,
                            bt_tok[j], free, s5["cb"], sig=ri == 1)
                btf[j] = t1
                if q < 14:
                    bt_tok[j] = load_bt(q + 2)
                yield
                s5["k0"] = tt(K0[:, q, :], BK[b][:, 0:128], MASKB[:, :], ALU.mult, t1, mask_tok, f)
                bbank.give(i, s5["k0"])
                yield True
            s5["end"] = fence()

        tasks["mix"].append(tables())
        gemm(16, lambda k: HH[:, k, :], lambda k: HL[:, k, :], lambda k: xt[k], u_evac, each=5)
        drain()

        bs = Slots([0, 1, 2])
        bn = [0, 0, 0]
        aq_free, sel_free = [None, None], [None, None]
        x_tok = None
        f = [fence(), s5["cc"], x_kept, s5["end"]]
        zt = dve.put(lambda e: e.memset(H[:, 0, :, :], 0.0), f)
        lo = hi = None

        def load_b(q):
            i, b_, free = bs.take()
            bn[b_] += 16
            bt = sp.dma(lambda e: e.dma_start(BS[b_][:, :, :], d["s5_b"][q]), s_b[b_], bn[b_], free, f)
            gi_, bk, fr = bank()
            sel = SEL[q % 2]
            pick = ident[0:64, 4 * q:4 * q + 4].rearrange("k (w c) -> k w c", c=1).to_broadcast([64, 4, 32])
            t = cp(sel[0:64, :, :], pick, f, sel_free[q % 2])
            t = sel_free[q % 2] = mm(BK[bk][:, 0:256], sel[0:64, :, :].rearrange("k w c -> k (w c)"), AT[0:64, :],
                                     True, True, t, s5["at"], fr, sig=True)
            aq = AQ[q % 2]
            a2 = BK[bk][:, 0:256].rearrange("p (a s) -> p a s", a=2)
            tt(aq[:, 0, :, :], a2, bc(BS[b_][:, 0, :], 2), ALU.mult, t, bt, f, aq_free[q % 2])
            t = tt(aq[:, 1, :, :], a2, bc(BS[b_][:, 1, :], 2), ALU.mult)
            bbank.give(gi_, t)
            tt(AB[b_][:, 0, :], aq[:, 0, 0, :], aq[:, 1, 1, :], ALU.subtract, t, free)
            t = tt(AB[b_][:, 1, :], aq[:, 0, 1, :], aq[:, 1, 0, :], ALU.add)
            aq_free[q % 2] = t
            return i, b_, [bt, t]

        PARTS = ((0, 16), (16, 40), (40, 64))

        def scan(g0, g1, t):
            g = slice(g0, g1)
            n = g1 - g0
            for s in range(1, 128):
                src = H[:, s, :, g].rearrange("p (a r) g -> p a r g", a=1).to_broadcast([P, 2, 2, n])
                t = tt(PR[:, :, :, g], TAB[:, :, :, g], src, ALU.mult, t, s5["tab"])
                yield
                t = tt(SS[:, :, g], PR[:, 0, :, g], PR[:, 1, ::-1, g], ALU.add, t)
                yield
                t = tt(H[:, s + 1, :, g], H[:, s + 1, :, g], SS[:, :, g], ALU.add, t)
                yield
            s5["h", g0] = t

        nxt = load_b(0)
        for q in range(16):
            i, b_, bt = nxt
            if q < 15:
                nxt = load_b(q + 1)
            for w in range(4):
                rows = slice(32 * w, 32 * w + 32)
                gt = 4 * q + w
                gi_, bk, fr = bank()
                for ri in range(2):
                    o = BK[bk][:, 128 * ri:128 * ri + 128]
                    mm(o, AB[b_][rows, ri, :], U[rows, q, 0::2], True, False, bt, fr, uz[q])
                    last = mm(o, BS[b_][rows, ri, :], U[rows, q, 1::2], False, True, sig=ri == 1)
                x_done = fn(H[:, 1:129, :, gt].rearrange("p t r -> p r t"),
                            BK[bk][:, 0:256].rearrange("p (r t) -> p r t", r=2), ACT.Copy, last, f)
                bbank.give(gi_, x_done)
                pump(6)
            bs.give(i, last)
            for g0, g1 in PARTS:
                if g1 == 4 * q + 4:
                    tasks["scan"].append(scan(g0, g1, x_done))

        fz = fence()

        def z_evac(n, ps, t):
            r = fn(Z[:, n, :], ps, ACT.Tanh, t, fz, scale=0.5)
            uz[16 + n] = stt(Z[:, n, :], Z[:, n, :], 1.0, ps, ALU.add, ALU.mult, r)
            return uz[16 + n]

        z_pe = gemm(16, lambda k: HH[:, k, :], lambda k: HL[:, k, :], lambda k: xt[k], z_evac, each=9)
        cl_tok = [sp.dma(lambda e, c=c: e.dma_start(CL[:, :, 16 * c:16 * c + 16, :, :], c_keep[c]),
                         s_cl[c], 16, z_pe, s5["cc"]) for c in range(4)]
        uy = []

        def y_out(q, gi_, ps, last):
            u2 = U[:, q, :].rearrange("p (b e) -> p e b", e=2)
            t = stt(u2, u2, PRM[:, S5_D + q:S5_D + q + 1], ps[:, 0:256].rearrange("p (e b) -> p e b", e=2),
                    ALU.mult, ALU.add, last)
            bbank.give(gi_, t)
            uy.append(fn(U[:, q, :], U[:, q, :], ACT.Gelu_apprx_tanh, t))

        got = None
        for q in range(16):
            part = [g0 for g0, g1 in PARTS if g0 <= 4 * q < g1][0]
            h_tok = fetch(s5, ("h", part))
            gi_, bk, fr = bank()
            ps = BK[bk]
            mm(ps[:, 0:128], K0[:, q, :], U[:, q, 0::2], True, False, fr, h_tok, cl_tok[q // 4], zt, s5["k0"])
            for w in range(4):
                rows = slice(32 * w, 32 * w + 32)
                gt = 4 * q + w
                for ri in range(2):
                    mm(ps[rows, 0:128], CL[:, 1, gt, ri, :], H[:, 0:128, ri, gt], False, ri == 1)
                for ri in range(2):
                    last = mm(ps[rows, 128:256], CL[:, 0, gt, ri, :], H[:, 1:129, ri, gt], ri == 0, ri == 1,
                              sig=ri == 1)
            pump(24)
            if got:
                y_out(*got)
            got = (q, gi_, ps, last)
        y_out(*got)

        ff = fence()
        yt = [split(HH[:, q, :], HL[:, q, :], U[:, q, :], uy[q], ff) for q in range(16)]
        GOH = m("goh", (KT, T), 32, F32R)
        GOL = m("gol", (KT, T), 0, F32R)
        Y2 = m("y2", (KT, T), 16)
        NB = m("nb", (16,), 88.5)
        nb = ts(NB[:, :], PRM[:, S5_BGLU:S5_BGLU + 16], 0.5, None, ALU.mult, None, ff)
        ff = fence()
        go = {}
        ZF = [m(f"zf{i}", (T,), 90 + i) for i in range(2)]
        ze = Slots(ZF)

        def glu_evac(n, ps, t):
            i, e_, free = ze.take()
            r = fn(e_[:, :], ps, ACT.Tanh, t, free, ff, nb, scale=0.5, bias=NB[:, n:n + 1])
            t1 = stt(e_[:, :], e_[:, :], 1.0, U[:, n, :], ALU.add, ALU.mult, r)
            t1 = tt(e_[:, :], e_[:, :], Z[:, n, :], ALU.mult, t1)
            go[n] = split(GOH[:, n, :], GOL[:, n, :], e_[:, :], t1, ff)
            ze.give(i, *go[n])
            return r

        gemm(16, lambda k: HH[:, k, :], lambda k: HL[:, k, :], lambda k: yt[k], glu_evac)
        y2t = []
        x_back = sp.dma(lambda e: e.dma_start(Xf, x_keep), s_keep, 32, x_kept, fence())
        sq = Squares(50, "yc", fence())

        def y2_evac(n, ps, t):
            y2t.append(fn(Y2[:, n, :], ps, ACT.Copy, t, ff, scale=0.25))
            return sq.add(ps, t, scale=0.25)

        gemm(16, lambda k: GOH[:, k, :], lambda k: GOL[:, k, :], lambda k: go[k], y2_evac)
        _, t0 = add_y(Y2, PRM[:, S5_POST:S5_POST + 16], None, sq, fence(), x_back)

        KF = m("kf", (KT, T), 0)
        VF = m("vf", (2, D), 16)
        QF = m("qf", (KT, T), 32)
        ZZ = m("zz", (KT, T), 48)
        FOL = m("fol", (KT, T), 48, F32R)
        FOH = m("foh", (KT, T), 64, F32R)
        FV = [m(f"fv{i}", (T,), 80 + i) for i in range(2)]
        FE = [m(f"fe{i}", (T,), 82 + i) for i in range(2)]
        CG = m("cg", (T,), 84)
        CN = m("cn", (T,), 85)
        TF = [m(f"tf{i}", (384,), 86 + 1.5 * i) for i in range(2)]
        PF = [m(f"pf{i}", (384,), 89 + 1.5 * i) for i in range(2)]
        XF = SM[:, 64:80]
        Y3 = m("y3", (KT, T), 0)

        xt = to_h(PRM[:, KV_G:KV_G + 16], None, None, t0)
        f = fence()
        kv = {}

        def kv_evac(n, ps, t):
            if n == 0:
                r = cp(CG[0:16, :], ps[0:16, :], t, f)
                t1 = ts(CG[0:16, :], CG[0:16, :], PRM[0:16, KV_BF:KV_BF + 1], None, ALU.add, None, r)
                t1 = fn(CN[0:16, :], CG[0:16, :], ACT.Abs, t1)
                t1 = fn(CN[0:16, :], CN[0:16, :], ACT.Exp, t1, scale=-1.0)
                t1 = fn(CN[0:16, :], CN[0:16, :], ACT.Ln, t1, bias=1.0)
                t1 = stt(CG[0:16, :], CG[0:16, :], 0.0, CN[0:16, :], ALU.min, ALU.subtract, t1)
                t1 = dve.put(lambda e: e.tensor_tensor_scan(CN[0:16, :], ONES[0:16, :], CG[0:16, :], 0.0,
                                                            ALU.mult, ALU.add), t1)
                kv["c"] = ts(CN[0:16, :], CN[0:16, :], -(128.0 ** 0.5), None, ALU.mult, None, t1)
                return r
            n -= 1
            if n < 16:
                kv["k", n] = fn(KF[:, n, :], ps, ACT.Copy, t, f)
                return kv["k", n]
            n -= 16
            s = n % 2
            prev = fetch(kv, ("v", n - 2)) if n > 1 else None
            r = fn(FV[s][:, :], ps, ACT.Copy, t, prev, f)
            tasks["tr"].append(transposed(VF[:, :, 128 * n:128 * n + 128], FV[s],
                                          lambda t, n=n: kv.update({("v", n): t}), r))
            return r

        early = []
        tasks["mix"].append(scaled(PRM[:, FOX_PRE:FOX_PRE + 16], early, f))
        kv_pe = gemm(33, lambda k: HH[:, k, :], lambda k: HL[:, k, :], lambda k: xt[k], kv_evac)
        xt = to_h(None, None, None, kv_pe, early=early)
        f = fence()
        fe = Slots(FE)

        def fox(h):
            scale = 128.0 ** -0.5
            yield from await_(kv, ("v", h))
            wait = [kv["k", h], kv["q", h], kv["c"], kv["v", h]]
            s = h % 2
            tf, pf = TF[s], PF[s]
            x4 = XF[:, 4 * s:4 * s + 4]
            (i, b, free), = yield from grab()
            row = ident[0:16, h:h + 1].to_broadcast([16, 128])
            mm(BK[b][:, 0:256], QF[:, h, 128:256], KF[:, h, :], True, False, *wait, free)
            mm(BK[b][:, 0:256], row, CN[0:16, :], False, True)
            mm(BK[b][:, 256:384], QF[:, h, 0:128], KF[:, h, 0:128], True, False)
            t = mm(BK[b][:, 256:384], row, CN[0:16, 0:128], False, True, sig=True)
            yield
            prev = kv.get(("fox", s))
            mk = CST[:, MASKF:MASKF + 384]
            t = tt(tf[:, :], BK[b][:, 0:384], mk, ALU.add, t, prev, f)
            bbank.give(i, t)
            t = dve.put(lambda e: e.tensor_reduce(x4[:, 0:1], tf[:, 0:256], AX.X, ALU.max), t)
            t = dve.put(lambda e: e.tensor_reduce(x4[:, 1:2], tf[:, 256:384], AX.X, ALU.max))
            t = ts(x4[:, 0:2], x4[:, 0:2], -scale, None, ALU.mult, None, t)
            yield
            for c, q in ((0, slice(0, 256)), (1, slice(256, 384))):
                t2 = fn(pf[:, q], tf[:, q], ACT.Exp, t, prev, scale=scale, bias=x4[:, c:c + 1],
                        accum_out=x4[:, 2 + c:3 + c])
            yield
            t = rec(x4[:, 2:4], x4[:, 2:4], t2)
            ts(pf[:, 0:256], pf[:, 0:256], x4[:, 2:3], None, ALU.mult, None, t)
            t = ts(pf[:, 256:384], pf[:, 256:384], x4[:, 3:4], None, ALU.mult, None)
            yield True
            (i, b, free), = yield from grab()
            tr(BK[b][:, 0:128], pf[:, 256:384], t, free)
            tr(BK[b][:, 128:256], pf[:, 0:128])
            t = tr(BK[b][:, 256:384], pf[:, 128:256], sig=True)
            yield
            t = cp(tf[:, :], BK[b][:, 0:384], t)
            bbank.give(i, t)
            yield True
            (i, b, free), = yield from grab()
            v = slice(128 * h, 128 * h + 128)
            mm(BK[b][:, 0:256], VF[:, 0, v], tf[:, 0:256], True, False, t, free)
            t = mm(BK[b][:, 128:256], VF[:, 1, v], tf[:, 256:384], False, True, sig=True)
            yield
            kv["o", h] = kv["fox", s] = cp(QF[:, h, :], BK[b][:, 0:256], t)
            bbank.give(i, kv["o", h])
            yield

        ft = {}

        def qz_evac(n, ps, t):
            if n < 16:
                kv["q", n] = fn(QF[:, n, :], ps, ACT.Copy, t, f)
                tasks["att"].append(fox(n))
                return kv["q", n]
            n -= 16
            i, e_, free = fe.take()
            r = fn(e_[:, :], ps, ACT.Tanh, t, free, f, scale=0.5)
            kv["z", n] = stt(ZZ[:, n, :], e_[:, :], 1.0, ps, ALU.add, ALU.mult, r)
            fe.give(i, kv["z", n])
            tasks["mix"].append(gate_out(n))
            return kv["z", n]

        def gate_out(n):
            yield from await_(kv, ("o", n))
            t = tt(QF[:, n, :], QF[:, n, :], ZZ[:, n, :], ALU.mult, kv["o", n], kv["z", n])
            yield
            ft[n] = split(FOH[:, n, :], FOL[:, n, :], QF[:, n, :], t, f)

        gemm(32, lambda k: HH[:, k, :], lambda k: HL[:, k, :], lambda k: xt[k], qz_evac, each=3)
        drain()
        ff = fence()
        y3t = []

        sq = Squares(32, "yd", ff)

        def y3_evac(n, ps, t):
            y3t.append(fn(Y3[:, n, :], ps, ACT.Copy, t, ff, scale=0.5))
            return sq.add(ps, t, scale=0.5)

        gemm(16, lambda k: FOH[:, k, :], lambda k: FOL[:, k, :], lambda k: ft[k], y3_evac)
        xs, _ = add_y(Y3, PRM[:, FOX_POST:FOX_POST + 16], None, sq, fence(), norm=False)
        for c in range(4):
            q = slice(4 * c, 4 * c + 4)
            sp.dma(lambda e, q=q: e.dma_start(out[:, q, :], X[:, q, :]), s_out, 16 * (c + 1), xs[4 * c + 3])
        sp.items.append(([(s_out, 64)], lambda e: e.wait_ge(s_out, 64), None, 0))

        with nc.Block() as block:
            @block.sync
            def _(e):
                sp.emit(e)

            @block.scalar
            def _(e):
                act.emit(e)

            @block.vector
            def _(e):
                dve.emit(e)

            @block.tensor
            def _(e):
                pe.emit(e)


def constants():
    cst = np.zeros((P, N_CST), np.float32)
    cst[:, IDENT:IDENT + 128] = np.eye(128, dtype=np.float32)
    r = np.arange(128)[:, None]
    u = np.arange(256)[None, :]
    dist = r + 128 - u
    nd = np.where((dist >= 0) & (dist < 128), -dist, BIG).astype(np.float32)
    cst[:, NDIST:NDIST + 256] = nd
    cst[:, NDIST + 256:NDIST + 384] = nd[:, 128:256]
    s = np.arange(128)[:, None]
    t = np.arange(128)[None, :]
    cst[:, MASKT:MASKT + 128] = np.where(s <= t, 0.0, BIG)
    tri = np.where(t <= s, 0.0, BIG).astype(np.float32)
    cst[:, MASKF + 128:MASKF + 256] = tri
    cst[:, MASKF + 256:MASKF + 384] = tri
    return cst


def head_columns():
    cols = []
    for pair in range(2):
        for i in range(4):
            for par in range(2):
                head = (2 * pair + par) * 4 + i
                cols += list(range(64 * head, 64 * head + 64))
    return np.array(cols)


def slab(w):
    k, n = w.shape
    a = w.reshape(k // D, KT, P, n // 128, 128).transpose(0, 3, 2, 1, 4)
    return np.ascontiguousarray(a).reshape(k // D * (n // 128), P, KT * 128)


def col(v):
    return v.reshape(-1, P).T


def layout(i):
    f = {}
    f["cst"] = constants()
    f["x"] = np.ascontiguousarray(i["x"][0].T.reshape(KT, P, T).transpose(1, 0, 2))
    f["w_ada"] = np.ascontiguousarray(
        i["w_ada"].reshape(2, 16, P, 6, 16, P).transpose(0, 3, 1, 2, 5, 4)).reshape(2, 6, 16, P, D)
    hc = head_columns()
    w_in = i["w_in"]
    gate = np.zeros((2, D, 128), np.float32)
    gate[:, :, 0:4] = w_in[:, :, 3072:3076]
    gate[:, :, 32:36] = w_in[:, :, 3076:3080]
    at = {"ka": 4104, "va": 4360, "q": 0, "k": 512, "v": 1024, "os": 2048}
    f["w_in"] = np.stack([slab(np.concatenate(
        [gate[l] if kind == "gate" else w_in[l][:, 3080 + hc[128 * n:128 * n + 128]] if kind == "qa"
         else w_in[l][:, at[kind] + 128 * n:at[kind] + 128 * n + 128] for kind, n in SLABS], axis=1))
        for l in range(2)])
    f["w_out"] = np.stack([slab(np.concatenate([i["w_out"][l][0:1024], i["w_out"][l][1024 + hc]]))
                           for l in range(2)])
    f["w_up"] = np.stack([slab(i["w_up"][l]) for l in range(2)])
    f["w_down"] = np.stack([slab(i["w_down"][l]) for l in range(2)])
    f["s5_w_in"] = slab(i["s5_w_in_2"][0])
    f["s5_w_glu"] = slab(i["s5_w_glu_2"][0])
    f["s5_w_out"] = slab(i["s5_w_out_2"][0])
    kv = i["kv_w_2"]
    pad = np.zeros((D, 128), np.float32)
    pad[:, 0:16] = kv[:, 4096:4112]
    f["kv_w"] = slab(np.concatenate([pad, kv[:, 0:4096]], axis=1))
    f["fox_w_in"] = slab(i["fox_w_in_2"][0])
    f["fox_w_out"] = slab(i["fox_w_out_2"][0])
    prm = np.zeros((P, N_PRM), np.float32)
    for l in range(2):
        b = PER_LAYER * l
        for off, name in ((PRE_MIX, "g_pre_mix"), (POST_MIX, "g_post_mix"), (PRE_MLP, "g_pre_mlp"),
                          (POST_MLP, "g_post_mlp")):
            prm[:, b + off:b + off + 16] = col(i[name][l])
        prm[:, b + B_ADA:b + B_ADA + 96] = col(i["b_ada"][l])
        prm[:, b + CONV_W:b + CONV_W + 32] = i["conv_w"][l].reshape(4, 8, P).transpose(2, 1, 0).reshape(P, 32)
        prm[:, b + CONV_B:b + CONV_B + 8] = col(i["conv_b"][l])
        prm[:, b + G_HEAD:b + G_HEAD + 8] = col(i["g_mlstm_head"][l].reshape(-1))
        prm[:, b + G_ATT:b + G_ATT + 8] = col(i["g_attn_out"][l][hc])
        prm[:, b + SINK:b + SINK + 16] = i["attn_sinks"][l][None, :]
        prm[0:4, b + GATE_B] = i["b_i"][l]
        prm[0:4, b + GATE_B + 1] = i["b_f"][l]
    for off, v in ((S5_PRE, i["norm_pre_2"][0]), (S5_POST, i["norm_post_2"][0]), (S5_D, i["s5_d_2"][0]),
                   (S5_BGLU, i["s5_b_glu_2"][0]), (KV_G, i["kv_norm_2"]), (FOX_PRE, i["norm_pre_2"][1]),
                   (FOX_POST, i["norm_post_2"][1]), (C_COL, i["c"][0])):
        prm[:, off:off + 16] = col(v)
    prm[0:16, KV_BF] = i["kv_b_f_2"]
    f["prm"] = prm

    def states(a):
        return a.reshape(64, 2, 64).transpose(1, 2, 0).reshape(P, 64)

    f["s5_ap"] = np.ascontiguousarray(np.stack(
        [states(i["s5_a_re_2"][0]), states(i["s5_a_im_2"][0]),
         states(np.broadcast_to(i["s5_log_dt_2"][0][:, None], (128, 64)))], axis=1))
    sc = []
    for name in ("s5_c_re_2", "s5_c_im_2"):
        c = i[name][0].reshape(64, 2, 16, 64).transpose(1, 3, 0, 2)
        sc.append(c.reshape(P, 64, 16))
    f["s5_c"] = np.ascontiguousarray(np.stack(sc, axis=1))
    sb = np.zeros((64, 2, 16, 2, 2, 64), np.float32)
    for ri, name in enumerate(("s5_b_re_2", "s5_b_im_2")):
        b = i[name][0].reshape(64, 2, 64, 16)
        for gh in range(2):
            sb[:, gh, :, ri, gh, :] = b[:, gh].transpose(0, 2, 1)
    f["s5_b"] = sb.reshape(16, P, 2, 128)
    sbt = np.zeros((16, 2, 64, 2, 4, 2, 16), np.float32)
    for ri, name in enumerate(("s5_b_re_2", "s5_b_im_2")):
        b = i[name][0].reshape(16, 4, 2, 64, 16)
        for gh in range(2):
            sbt[:, gh, :, ri, :, gh, :] = b[:, :, gh].transpose(0, 2, 1, 3)
    f["s5_bt"] = sbt.reshape(16, P, 2, 128)
    f["s5_mask"] = np.kron(np.eye(4), np.ones((32, 32)))
    return {k: np.ascontiguousarray(v, dtype=np.float32) for k, v in f.items()}


def kernel(**inputs):
    import concourse.bacc as _bacc
    from concourse.bass_utils import run_bass_kernel_spmd as _run

    arrays = layout({k: np.asarray(v) for k, v in inputs.items()})
    nc = _bacc.Bacc("TRN2", target_bir_lowering=False, num_devices=1, dynamic_dma_scratch_size=1024)
    d = {k: nc.dram_tensor(f"in_{k}", v.shape, F32, kind="ExternalInput").ap() for k, v in arrays.items()}
    out = nc.dram_tensor("out_x", (P, KT, T), F32, kind="ExternalOutput").ap()
    build(nc, d, out)
    r = _run(nc, [{f"in_{k}": v for k, v in arrays.items()}], core_ids=[0])
    got = r.results[0]["out_x"]
    return np.ascontiguousarray(np.asarray(got).transpose(1, 0, 2).reshape(D, T).T)[None]
```
